# Optimizing a Trainium2 kernel written in Bass

```python
import math
import jax, jax.numpy as jnp
from jax import lax
import numpy as np

D_MODEL = 1024
BATCH = 1
SEQ = 128
DEPTH = 2
DEC_BATCH = 1
DEC_SEQ = 512
PAST_LEN = 128

GRID_W = 64
EPS = 1e-6
ML_HEADS = 4
ML_DIM = 64
ML_WIDTH = ML_HEADS * ML_DIM
ML_CHUNK = 128
CM_GROUPS = 4
CM_DIM = 64
CM_WIDTH = CM_GROUPS * CM_DIM
CM_CHUNK = 128
MLA_HEADS = 8
MLA_NOPE = 64
MLA_ROPE = 32
MLA_V = 64
MLA_Q_RANK = 256
MLA_KV_RANK = 256
MLA_WIDTH = MLA_HEADS * MLA_V
MLA_QBLOCK = 128
ROPE_AXIS = MLA_ROPE // 2
ROPE_THETA = 10000.0
MIX_WIDTH = ML_WIDTH + CM_WIDTH + MLA_WIDTH
IN_SPLITS = (ML_WIDTH, ML_WIDTH, ML_WIDTH, ML_WIDTH, ML_HEADS, ML_HEADS, ML_HEADS, ML_HEADS, CM_WIDTH, CM_WIDTH, MLA_Q_RANK, MLA_KV_RANK, MLA_ROPE)
IN_COLS = 4 * ML_WIDTH + 4 * ML_HEADS + 2 * CM_WIDTH + MLA_Q_RANK + MLA_KV_RANK + MLA_ROPE
PEER_HEADS = 8
PEER_NKEYS = 128
PEER_EXPERTS = PEER_NKEYS * PEER_NKEYS
PEER_DKEY = 256
PEER_TOPK = 16
PEER_TOKBLOCK = 128

kernel_name = 'hybrid_mlstm_sgu_mla_peer_diffusion_step'

def rmsnorm(x, g):
    xf = x.astype(jnp.float32)
    y = xf * lax.rsqrt(jnp.mean(xf * xf, axis=-1, keepdims=True) + EPS)
    return (y * g.astype(jnp.float32)).astype(x.dtype)

def split_cols(proj):
    out = []
    off = 0
    for w in IN_SPLITS:
        out.append(proj[..., off:off + w])
        off += w
    return out

def mlstm_chunkwise(q, k, v, i_pre, f_pre, C0, n0, m0):
    B, T, H, Dh = q.shape
    L = ML_CHUNK
    nc = T // L
    f32 = jnp.float32

    def to_chunks(a):
        return a.astype(f32).reshape(B, nc, L, H, Dh).transpose(1, 0, 3, 2, 4)

    def gates_to_chunks(a):
        return a.astype(f32).reshape(B, nc, L, H).transpose(1, 0, 3, 2)

    qc = to_chunks(q)
    kc = to_chunks(k) * (Dh ** -0.5)
    vc = to_chunks(v)
    ic = gates_to_chunks(i_pre)
    lfc = jax.nn.log_sigmoid(gates_to_chunks(f_pre))
    causal = jnp.tril(jnp.ones((L, L), dtype=bool))

    def step(carry, xs):
        C, n, m = carry
        qb, kb, vb, ib, lfb = xs
        b = jnp.cumsum(lfb, axis=-1)
        d = jnp.where(causal, b[..., :, None] - b[..., None, :] + ib[..., None, :], -jnp.inf)
        m_inter = b + m[..., None]
        m_t = jnp.maximum(m_inter, d.max(-1))
        w_intra = jnp.exp(d - m_t[..., None])
        w_inter = jnp.exp(m_inter - m_t)
        sw = jnp.einsum('bhtd,bhsd->bhts', qb, kb) * w_intra
        num = jnp.einsum('bhts,bhse->bhte', sw, vb) + w_inter[..., None] * jnp.einsum('bhtd,bhde->bhte', qb, C)
        den = sw.sum(-1) + w_inter * jnp.einsum('bhtd,bhd->bht', qb, n)
        h = num / jnp.maximum(jnp.abs(den), jnp.exp(-m_t))[..., None]
        b_end = b[..., -1]
        log_w = b_end[..., None] - b + ib
        m_new = jnp.maximum(b_end + m, log_w.max(-1))
        w_k = jnp.exp(log_w - m_new[..., None])
        decay = jnp.exp(b_end + m - m_new)
        C_new = decay[..., None, None] * C + jnp.einsum('bhs,bhsd,bhse->bhde', w_k, kb, vb)
        n_new = decay[..., None] * n + jnp.einsum('bhs,bhsd->bhd', w_k, kb)
        return (C_new, n_new, m_new), h

    (C, n, m), h = lax.scan(step, (C0.astype(f32), n0.astype(f32), m0.astype(f32)), (qc, kc, vc, ic, lfc))
    h = h.transpose(1, 0, 3, 2, 4).reshape(B, T, H, Dh)
    return h.astype(q.dtype), C, n, m

def chunk_spatial_gating(u, v, norm_g, ws, bs):
    B, T, _ = v.shape
    nc = T // CM_CHUNK
    vn = rmsnorm(v, norm_g).reshape(B, nc, CM_CHUNK, CM_GROUPS, CM_DIM)
    mixed = jnp.einsum('gts,bnsgd->bntgd', ws, vn) + bs.T[None, None, :, :, None]
    return u * mixed.reshape(B, T, CM_WIDTH)

def axial_angles(rows):
    row = jnp.repeat(jnp.arange(rows, dtype=jnp.float32), GRID_W)
    col = jnp.tile(jnp.arange(GRID_W, dtype=jnp.float32), rows)
    freqs = ROPE_THETA ** (-jnp.arange(0, ROPE_AXIS, 2, dtype=jnp.float32) / ROPE_AXIS)
    return row[:, None] * freqs, col[:, None] * freqs

def rotate(x, ang):
    ang = ang.reshape((ang.shape[0],) + (1,) * (x.ndim - 3) + (ang.shape[-1],))
    cos = jnp.cos(ang).astype(x.dtype)
    sin = jnp.sin(ang).astype(x.dtype)
    x1, x2 = jnp.split(x, 2, axis=-1)
    return jnp.concatenate([x1 * cos - x2 * sin, x2 * cos + x1 * sin], axis=-1)

def axial_rope(x, angles):
    ang_r, ang_c = angles
    return jnp.concatenate([rotate(x[..., :ROPE_AXIS], ang_r), rotate(x[..., ROPE_AXIS:], ang_c)], axis=-1)

def mla_kv(ckv_n, w_ukv):
    B, S, _ = ckv_n.shape
    kv = (ckv_n @ w_ukv).reshape(B, S, MLA_HEADS, MLA_NOPE + MLA_V)
    return kv[..., :MLA_NOPE], kv[..., MLA_NOPE:]

def mla_attention(q_nope, q_rope, k_nope, k_rope, v):
    B, Tq, H, _ = q_nope.shape
    nb = Tq // MLA_QBLOCK
    scale = (MLA_NOPE + MLA_ROPE) ** -0.5

    def blocks(a):
        return a.reshape((B, nb, MLA_QBLOCK) + a.shape[2:]).swapaxes(0, 1)

    def one(args):
        qn, qr = args
        s = jnp.einsum('bqhd,bkhd->bhqk', qn, k_nope) + jnp.einsum('bqhd,bkd->bhqk', qr, k_rope)
        p = jax.nn.softmax(s.astype(jnp.float32) * scale, axis=-1).astype(v.dtype)
        return jnp.einsum('bhqk,bkhd->bqhd', p, v)

    out = lax.map(one, (blocks(q_nope), blocks(q_rope)))
    return out.swapaxes(0, 1).reshape(B, Tq, H * MLA_V)

def peer_layer(h, w_q, subkeys, u_tab, v_tab):
    B, T, D = h.shape
    xb = h.reshape(-1, PEER_TOKBLOCK, D)
    half = PEER_DKEY // 2

    def one(xt):
        q = (xt @ w_q).reshape(PEER_TOKBLOCK, PEER_HEADS, 2, half)
        s1 = jnp.einsum('thd,kd->thk', q[:, :, 0], subkeys[0])
        s2 = jnp.einsum('thd,kd->thk', q[:, :, 1], subkeys[1])
        v1, i1 = lax.top_k(s1, PEER_TOPK)
        v2, i2 = lax.top_k(s2, PEER_TOPK)
        cand = (v1[..., :, None] + v2[..., None, :]).reshape(PEER_TOKBLOCK, PEER_HEADS, PEER_TOPK * PEER_TOPK)
        cidx = (i1[..., :, None] * PEER_NKEYS + i2[..., None, :]).reshape(PEER_TOKBLOCK, PEER_HEADS, PEER_TOPK * PEER_TOPK)
        sc, pos = lax.top_k(cand, PEER_TOPK)
        eidx = jnp.take_along_axis(cidx, pos, axis=-1)
        g = jax.nn.softmax(sc.astype(jnp.float32), axis=-1).astype(xt.dtype)
        act = jax.nn.gelu(jnp.einsum('thkd,td->thk', jnp.take(u_tab, eidx, axis=0), xt))
        return jnp.einsum('thk,thkd->td', g * act, jnp.take(v_tab, eidx, axis=0))

    return lax.map(one, xb).reshape(B, T, D)

def trunk_layer(x, cvec, p, ml_state, ctx_cache, angles):
    B, T, _ = x.shape
    mod = (jax.nn.silu(cvec) @ p['ada_w'] + p['ada_b'])[:, None, :]
    sh1, sc1, g1, sh2, sc2, g2 = jnp.split(mod, 6, axis=-1)
    h = rmsnorm(x, p['norm1_g']) * (1 + sc1) + sh1
    (mq, mk, mv, mo, i_f, f_f, i_b, f_b, cu, cv, cq, ckv, kr) = split_cols(h @ p['w_in'])

    def hd(a):
        return a.reshape(B, T, ML_HEADS, ML_DIM)

    def rev(a):
        return jnp.flip(a, axis=1)

    gb = p['mlstm_gate_b']
    C0, n0, m0 = ml_state
    qh, kh, vh = hd(mq), hd(mk), hd(mv)
    hf, Cf, nf, mf = mlstm_chunkwise(qh, kh, vh, i_f + gb[0:4], f_f + gb[4:8], C0[:, 0], n0[:, 0], m0[:, 0])
    hb, Cb, nb_, mb = mlstm_chunkwise(rev(qh), rev(kh), rev(vh), rev(i_b + gb[8:12]), rev(f_b + gb[12:16]), C0[:, 1], n0[:, 1], m0[:, 1])
    ml_out = jax.nn.sigmoid(mo) * (hf + rev(hb)).reshape(B, T, ML_WIDTH)
    new_ml = (jnp.stack([Cf, Cb], axis=1), jnp.stack([nf, nb_], axis=1), jnp.stack([mf, mb], axis=1))

    cm_out = chunk_spatial_gating(cu, cv, p['cm_norm_g'], p['cm_ws'], p['cm_b'])

    q = (rmsnorm(cq, p['mla_q_norm_g']) @ p['mla_w_uq']).reshape(B, T, MLA_HEADS, MLA_NOPE + MLA_ROPE)
    q_nope, q_rope = q[..., :MLA_NOPE], q[..., MLA_NOPE:]
    ckv_n = rmsnorm(ckv, p['mla_kv_norm_g'])
    k_nope, vals = mla_kv(ckv_n, p['mla_w_ukv'])
    k_rope = kr
    if angles is not None:
        q_rope = axial_rope(q_rope, angles)
        k_rope = axial_rope(kr, angles)
    if ctx_cache is not None:
        ctx_ckv, ctx_kr = ctx_cache
        ck_nope, c_vals = mla_kv(ctx_ckv, p['mla_w_ukv'])
        k_nope = jnp.concatenate([ck_nope, k_nope], axis=1)
        vals = jnp.concatenate([c_vals, vals], axis=1)
        k_rope = jnp.concatenate([ctx_kr, k_rope], axis=1)
    att = mla_attention(q_nope, q_rope, k_nope, k_rope, vals)

    mix = jnp.concatenate([ml_out, cm_out, att], axis=-1) @ p['w_out']
    x = x + g1 * mix
    h2 = rmsnorm(x, p['norm2_g']) * (1 + sc2) + sh2
    x = x + g2 * peer_layer(h2, p['peer_w_q'], p['peer_subkeys'], p['peer_u'], p['peer_v'])
    return x, (ckv_n, kr), new_ml

def setup_inputs(seed: int = 0) -> dict:
    key = jax.random.key(seed)
    ks = jax.random.split(key, 40)
    f32 = jnp.float32

    def nrm(k, shape, s):
        return jax.random.normal(k, shape, f32) * s

    def gain(k, shape):
        return 1.0 + 0.05 * jax.random.normal(k, shape, f32)

    gk = jax.random.split(ks[30], 4)
    mlstm_gate_b = jnp.concatenate([
        nrm(gk[0], (DEPTH, ML_HEADS), 0.1), 3.0 + nrm(gk[1], (DEPTH, ML_HEADS), 0.1),
        nrm(gk[2], (DEPTH, ML_HEADS), 0.1), 3.0 + nrm(gk[3], (DEPTH, ML_HEADS), 0.1)], axis=-1)
    return {
        'x_prompt': nrm(ks[0], (BATCH, SEQ, D_MODEL), 1.0),
        'x_sample': nrm(ks[1], (DEC_BATCH, DEC_SEQ, D_MODEL), 1.0),
        'c': nrm(ks[2], (DEC_BATCH, D_MODEL), 1.0),
        'cache_mla_ckv': nrm(ks[3], (DEC_BATCH, DEPTH, PAST_LEN, MLA_KV_RANK), 1.0),
        'cache_mla_krope': nrm(ks[4], (DEC_BATCH, DEPTH, PAST_LEN, MLA_ROPE), 1.0),
        'state_mlstm_C': nrm(ks[5], (DEC_BATCH, DEPTH, 2, ML_HEADS, ML_DIM, ML_DIM), 0.1),
        'state_mlstm_n': nrm(ks[6], (DEC_BATCH, DEPTH, 2, ML_HEADS, ML_DIM), 0.1),
        'state_mlstm_m': nrm(ks[7], (DEC_BATCH, DEPTH, 2, ML_HEADS), 0.5),
        'c_ctx': nrm(ks[8], (D_MODEL,), 1.0),
        'norm1_g': gain(ks[9], (DEPTH, D_MODEL)),
        'ada_w': nrm(ks[10], (DEPTH, D_MODEL, 6 * D_MODEL), 0.5 * D_MODEL ** -0.5),
        'ada_b': nrm(ks[11], (DEPTH, 6 * D_MODEL), 0.02),
        'w_in': nrm(ks[12], (DEPTH, D_MODEL, IN_COLS), D_MODEL ** -0.5),
        'mlstm_gate_b': mlstm_gate_b,
        'cm_norm_g': gain(ks[13], (DEPTH, CM_WIDTH)),
        'cm_ws': nrm(ks[14], (DEPTH, CM_GROUPS, CM_CHUNK, CM_CHUNK), CM_CHUNK ** -0.5),
        'cm_b': nrm(ks[15], (DEPTH, CM_GROUPS, CM_CHUNK), 0.02),
        'mla_q_norm_g': gain(ks[16], (DEPTH, MLA_Q_RANK)),
        'mla_w_uq': nrm(ks[17], (DEPTH, MLA_Q_RANK, MLA_HEADS * (MLA_NOPE + MLA_ROPE)), MLA_Q_RANK ** -0.5),
        'mla_kv_norm_g': gain(ks[18], (DEPTH, MLA_KV_RANK)),
        'mla_w_ukv': nrm(ks[19], (DEPTH, MLA_KV_RANK, MLA_HEADS * (MLA_NOPE + MLA_V)), MLA_KV_RANK ** -0.5),
        'w_out': nrm(ks[20], (DEPTH, MIX_WIDTH, D_MODEL), MIX_WIDTH ** -0.5),
        'norm2_g': gain(ks[21], (DEPTH, D_MODEL)),
        'peer_w_q': nrm(ks[22], (DEPTH, D_MODEL, PEER_HEADS * PEER_DKEY), D_MODEL ** -0.5),
        'peer_subkeys': nrm(ks[23], (DEPTH, 2, PEER_NKEYS, PEER_DKEY // 2), (PEER_DKEY // 2) ** -0.5),
        'peer_u': nrm(ks[24], (DEPTH, PEER_EXPERTS, D_MODEL), D_MODEL ** -0.5),
        'peer_v': nrm(ks[25], (DEPTH, PEER_EXPERTS, D_MODEL), PEER_HEADS ** -0.5),
        'final_g': gain(ks[26], (D_MODEL,)),
    }

def reference(x_prompt, x_sample, c, cache_mla_ckv, cache_mla_krope, state_mlstm_C, state_mlstm_n, state_mlstm_m,
              c_ctx, norm1_g, ada_w, ada_b, w_in, mlstm_gate_b, cm_norm_g, cm_ws, cm_b, mla_q_norm_g, mla_w_uq,
              mla_kv_norm_g, mla_w_ukv, w_out, norm2_g, peer_w_q, peer_subkeys, peer_u, peer_v, final_g):
    def layer_params(l):
        return {'norm1_g': norm1_g[l], 'ada_w': ada_w[l], 'ada_b': ada_b[l], 'w_in': w_in[l],
                'mlstm_gate_b': mlstm_gate_b[l], 'cm_norm_g': cm_norm_g[l], 'cm_ws': cm_ws[l], 'cm_b': cm_b[l],
                'mla_q_norm_g': mla_q_norm_g[l], 'mla_w_uq': mla_w_uq[l], 'mla_kv_norm_g': mla_kv_norm_g[l],
                'mla_w_ukv': mla_w_ukv[l], 'w_out': w_out[l], 'norm2_g': norm2_g[l], 'peer_w_q': peer_w_q[l],
                'peer_subkeys': peer_subkeys[l], 'peer_u': peer_u[l], 'peer_v': peer_v[l]}

    b0 = x_prompt.shape[0]
    zero_state = (jnp.zeros((b0, 2, ML_HEADS, ML_DIM, ML_DIM), jnp.float32),
                  jnp.zeros((b0, 2, ML_HEADS, ML_DIM), jnp.float32),
                  jnp.zeros((b0, 2, ML_HEADS), jnp.float32))
    xc = x_prompt
    ckvs, krs, Cs, ns, ms = [], [], [], [], []
    for l in range(DEPTH):
        xc, (ckv_l, kr_l), (C_l, n_l, m_l) = trunk_layer(xc, c_ctx[None, :], layer_params(l), zero_state, None, None)
        ckvs.append(ckv_l)
        krs.append(kr_l)
        Cs.append(C_l)
        ns.append(n_l)
        ms.append(m_l)
    y_prompt = rmsnorm(xc, final_g)

    rows = x_sample.shape[1] // GRID_W
    angles = axial_angles(rows)
    xs = x_sample
    for l in range(DEPTH):
        state_l = (state_mlstm_C[:, l], state_mlstm_n[:, l], state_mlstm_m[:, l])
        xs, _, _ = trunk_layer(xs, c, layer_params(l), state_l, (cache_mla_ckv[:, l], cache_mla_krope[:, l]), angles)
    y_sample = rmsnorm(xs, final_g)

    return (y_prompt, y_sample, jnp.stack(ckvs, axis=1), jnp.stack(krs, axis=1), jnp.stack(Cs, axis=1),
            jnp.stack(ns, axis=1), jnp.stack(ms, axis=1))


_drawn_inputs = setup_inputs


def setup_inputs(seed=0):
    import zlib

    import numpy as np

    out = dict(_drawn_inputs(seed))
    spreads = {}
    factors = {'cache_mla_ckv': 2.971,
     'cache_mla_krope': 5.37,
     'state_mlstm_C': 4.49,
     'state_mlstm_n': 3.262,
     'state_mlstm_m': 6.268,
     'cm_norm_g': 2.676,
     'cm_b': 5.486,
     'mla_q_norm_g': 8.0}
    for name, (base, spread) in spreads.items():
        noise = np.random.default_rng([zlib.crc32(name.encode()), seed]).standard_normal(out[name].shape)
        drawn = base * np.exp(spread * noise) if base else spread * noise
        out[name] = __import__('jax').numpy.asarray(drawn.astype(out[name].dtype))
    for name, factor in factors.items():
        out[name] = (out[name] * factor).astype(out[name].dtype)
    return out
```

```python
import math
from contextlib import ExitStack

import numpy as np

import concourse.bass as bass
from concourse import mybir

F32 = mybir.dt.float32
BF16 = mybir.dt.bfloat16
U32 = mybir.dt.uint32
ALU = mybir.AluOpType
ACT = mybir.ActivationFunctionType
AX = mybir.AxisListType

P = 128
D = 1024
KD = D // P
DEPTH = 2

NT = 5
T = NT * P
NS = 4
EPS = 1e-6
H = 4
HD = 64
AH = 8
ROPE = 32
QK = HD + ROPE
KT = NT + 1
SCALE = float(QK) ** -0.5
RH = 8
TOP = 16
SLOTS = RH * TOP
NKEYS = 128
MASKED = -1e30
ROWS = 36
GB = 32
NB = T // GB
NG = 4
GROUPS = NKEYS // NG
HALF = T // 2
MK, MV, MO, CU, CV, CQ, CKV = range(7)
SMALL = 2 * ROWS + 2 * ROPE
R_A, R_WK, R_WIN, R_EM = range(4)


def col(ap, n):
    return ap.unsqueeze(len(ap.shape)).to_broadcast(list(ap.shape) + [n])


class Kernel:
    def __init__(self, nc, a, o):
        self.nc, self.a, self.o = nc, a, o
        self.sems = []

    def sem(self, name):
        s = self.nc.alloc_semaphore(name)
        self.sems.append(s)
        return s


def chain_of(eng, sem):
    count = [0]

    def link(ins):
        count[0] += 1
        ins.then_inc(sem, 1)
        eng.wait_ge(sem, count[0])

    return link


def build_program(nc, a, o, upto=99):
    K = Kernel(nc, a, o)
    ctx = ExitStack()
    dbg = o.get("dbg")

    def sb(name, shape, dt=F32, stack=ctx):
        return stack.enter_context(nc.sbuf_tensor(name, shape, dt))

    x = sb("x", [P, NT, D])
    hT = sb("hT", [P, KD, T])
    gate_bc = sb("gate_bc", [P, 2, 2, D])
    modT = sb("modT", [P, 4, KD, 2])
    ident = sb("ident", [P, P])
    ones_row = sb("ones_row", [1, P])
    sel2 = sb("sel2", [2, 2, P])
    cT = sb("cT", [P, KD, 2])
    rstd = sb("rstd", [P, 16])
    ss = sb("ss", [P, 16])
    eps_col = sb("eps_col", [P, 1])
    one_col = sb("one_col", [P, 1])
    xn = sb("xn", [P, 2, D])
    ps = ctx.enter_context(nc.psum_tensor("ps", [P, 8, 512], F32))

    gates_dram = nc.dram_tensor("gates_dram", [NB, P, NKEYS * GB], F32, kind="Internal").ap()

    def normalise(act, dve, pe, which, start):
        psum_ready, hT_taken_act, hT_taken_dve = start["tp"], start["ta"], start["td"]
        sh, sc = 2 * which, 2 * which + 1
        if act is not None:
            for t in range(NT):
                act.activation(xn[:, 1, :], x[:, t, :], ACT.Square,
                               accum_out=ss[:, t:t + 1]).then_inc(start["sq"], 1)
                act.wait_ge(start["sq"], t + 1)
            act.activation(rstd[:, 0:NT], ss[:, 0:NT], ACT.Sqrt, bias=eps_col[:, 0:1], scale=1.0 / D).then_inc(start["rt"], 1)
            if "mod" in start:
                act.wait_ge(start["mod"], 4)
            for t in range(NT):
                c = 0 if t == 0 else 1
                act.wait_ge(psum_ready, t + 1)
                for k in range(4):
                    ins = act.activation(hT[:, k, t * P:(t + 1) * P], ps[:, 4 + 2 * (t % 2), k * P:(k + 1) * P],
                                         ACT.Identity, bias=modT[:, sh, k, c:c + 1], scale=modT[:, sc, k, c:c + 1])
                ins.then_inc(hT_taken_act, 1)
        if dve is not None:
            link = start["link"]
            dve.wait_ge(start["rt"], 1)
            link(dve.reciprocal(rstd[:, 0:NT], rstd[:, 0:NT]))

            def scaled(t):
                if t >= 2:
                    dve.wait_ge(psum_ready, t - 1)
                dve.tensor_scalar(xn[:, t % 2, :], x[:, t, :], rstd[:, t:t + 1], None,
                                  ALU.mult).then_inc(start["xn"], 1)

            scaled(0)
            for t in range(NT):
                c = 0 if t == 0 else 1
                if t + 1 < NT:
                    scaled(t + 1)
                dve.wait_ge(psum_ready, t + 1)
                for k in range(4):
                    ins = dve.tensor_scalar(hT[:, 4 + k, t * P:(t + 1) * P],
                                            ps[:, 5 + 2 * (t % 2), k * P:(k + 1) * P],
                                            modT[:, sc, 4 + k, c:c + 1], modT[:, sh, 4 + k, c:c + 1],
                                            ALU.mult, ALU.add)
                ins.then_inc(hT_taken_dve, 1)
        if pe is not None:
            for t in range(NT):
                pe.wait_ge(start["xn"], t + 1)
                if t >= 2:
                    pe.wait_ge(hT_taken_act, t - 1)
                    pe.wait_ge(hT_taken_dve, t - 1)
                for k in range(KD):
                    ins = pe.transpose(ps[:, 4 + 2 * (t % 2) + k // 4, (k % 4) * P:(k % 4 + 1) * P],
                                       xn[:, t % 2, k * P:(k + 1) * P], ident[:, :])
                ins.then_inc(psum_ready, 1)

    load = K.nc.alloc_semaphore("first_loads")
    pre = K.nc.alloc_semaphore("first_constants")
    silu = K.nc.alloc_semaphore("silu_ready")
    with nc.Block() as block:
        @block.sync
        def _(sp):
            sp.dma_start(x[:, :, :], a["x"].rearrange("(t p) d -> p t d", p=P)).then_inc(load, 16)
            sp.dma_start(ident[:, :], a["ident"]).then_inc(load, 16)
            sp.dma_start(sel2[:, :, :], a["sel2"]).then_inc(load, 16)
            sp.dma_start(cT[:, :, :], a["cT"]).then_inc(load, 16)
            sp.wait_ge(load, 64)

        @block.vector
        def _(dve):
            dve.memset(ones_row[:, :], 1.0).then_inc(pre, 1)
            dve.memset(eps_col[:, :], EPS).then_inc(pre, 1)
            dve.memset(one_col[:, :], 1.0).then_inc(pre, 1)
            dve.wait_ge(pre, 3)

        @block.scalar
        def _(act):
            act.wait_ge(load, 64)
            act.activation(cT[:, :, :], cT[:, :, :], ACT.Silu).then_inc(silu, 1)
            act.wait_ge(silu, 1)

    mix_in = ctx.enter_context(ExitStack())

    def layer(l):
        project(l)
        if upto >= 2:
            mixers(l)
        if upto >= 4:
            retrieve(l)
        if upto >= 5:
            gate_matrices(l)
        if upto >= 6:
            experts(l)

    s1 = ExitStack()
    mixed = sb("mixed", [P, NT, D], stack=s1)
    cqT = sb("cqT", [P, 2, T], stack=s1)
    ckvT = sb("ckvT", [P, 2, KT * P], stack=s1)
    krT = sb("krT", [QK, KT * P], stack=s1)
    cos_sin = sb("cos_sin", [QK, 2, NS * P], stack=s1)
    s2 = ExitStack()
    proj = sb("proj", [P, NT, 7, 256], stack=s2)
    small = sb("small", [P, NT, SMALL], stack=s2)
    mqT = sb("mqT", [P, 2, T], stack=s2)
    s3 = ExitStack()
    wring = sb("wring", [P, 3, KD, 512], stack=s3)
    wsmall = sb("wsmall", [P, KD, SMALL], stack=s3)
    ada_rows = sb("ada_rows", [1, 2, 512], stack=s3)
    mod_row = sb("mod_row", [2, 2, 512], stack=s3)
    normT = sb("normT", [P, 2, KD], stack=s3)
    s3.close()
    s4 = ExitStack()
    mkT = sb("mkT", [P, 2, T], stack=s4)
    v1 = sb("v1", [P, NT, H, HD + 1], stack=s4)
    bwd = xn[:, :, :].rearrange("p a b -> p (a b)")[:, 0:NT * 256].rearrange("p (t e) -> p t e", t=NT)
    rowq = sb("rowq", [ROWS, 4, T], stack=s4)
    r_i, r_e, r_f = rowq[:, R_A, :], rowq[:, R_WK, :], rowq[:, R_WIN, :]
    r_b = sb("r_b", [ROWS, T], stack=s4)
    r_u = sb("r_u", [ROWS, T], stack=s4)
    r_prev = sb("r_prev", [ROWS, NT], stack=s4)
    r_end = sb("r_end", [ROWS, NT], stack=s4)
    r_dec = sb("r_dec", [ROWS, NT], stack=s4)
    r_m = sb("r_m", [ROWS, 1], stack=s4)
    gate_b = sb("gate_b", [ROWS, 2], stack=s4)
    m0 = sb("m0", [ROWS, 1], stack=s4)
    sel8 = sb("sel8", [ROWS, 8, P], stack=s4)
    maskb = sb("maskb", [P, 2, P], stack=s4)
    cols = sb("cols", [P, 4 * NT, ROWS], stack=s4)
    dec = sb("dec", [P, 8, NT], stack=s4)
    cn = sb("cn", [P, 2, 6, 2, HD + 1], stack=s4)
    wT = sb("wT", [P, 2, 512], stack=s4)
    swT = sb("swT", [P, 2, 512], stack=s4)
    kw = sb("kw", [P, 2, 256], stack=s4)
    nd = sb("nd", [P, H, HD + 1], stack=s4)
    dd = sb("dd", [P, 2, H], stack=s4)
    wsT = sb("wsT", [P, H, P], stack=s4)
    cmb = sb("cmb", [P, H], stack=s4)
    normg = sb("normg", [P, 3, 256], stack=s4)
    s4.close()
    s2.close()
    s5 = ExitStack()
    qT = sb("qT", [QK, AH, T], stack=s5)
    kT = sb("kT", [QK, AH, KT * P], stack=s5)
    val = sb("val", [P, KT, 512], stack=s5)
    prob = sb("prob", [P, 2, T], stack=s5)
    probT = sb("probT", [P, 2, T], stack=s5)
    wuq = sb("wuq", [P, 2, AH * QK], stack=s5)
    wqs = sb("wqs", [P, 2, AH * ROPE], stack=s5)
    wuk = sb("wuk", [P, 2, 512], stack=s5)
    wuv = sb("wuv", [P, 2, 512], stack=s5)
    rot = sb("rot", [QK, 2, 512], stack=s5)
    amax = sb("amax", [P, 2, 4], stack=s5)
    wout = sb("wout", [P, KD, 512], stack=s5)
    s5.close()
    s1.close()

    w_slot = [K.sem(f"w_slot{i}") for i in range(3)]
    w_free = K.sem("w_free")
    a_load = K.sem("a_load")
    ada_slot = [K.sem(f"ada_slot{i}") for i in range(2)]
    mod_psum = K.sem("mod_psum")
    mod_copied = K.sem("mod_copied")
    mod_spread = K.sem("mod_spread")
    mod_taken = K.sem("mod_taken")
    mod_final = K.sem("mod_final")
    n1 = dict(tp=K.sem("n1_psum"), ta=K.sem("n1_act"), td=K.sem("n1_dve"), sq=K.sem("n1_sq"), rt=K.sem("n1_root"),
              xn=K.sem("n1_xn"), mod=mod_final)
    proj_psum = K.sem("proj_psum")
    proj_taken = K.sem("proj_taken")
    a_chain = K.sem("a_chain")

    def project(l):
        with nc.Block() as block:
            @block.sync
            def _(sp):
                sp.dma_start(normT[:, :, :], a["normT"][l]).then_inc(a_load, 16)
                sp.dma_start(wsmall[:, :, :], a["w_small"][l]).then_inc(a_load, 16)
                for j in range(16):
                    if 3 <= j < 15:
                        sp.wait_ge(w_free, j - 2)
                    if j == 15:
                        sp.wait_ge(proj_psum, NT)
                    src = a["ada_w"][l, j] if j < 12 else a["w_in"][l, j - 12]
                    sp.dma_start(wring[:, j % 3, :, :], src).then_inc(w_slot[j % 3], 16)
                    if j < 12:
                        if j >= 2:
                            sp.wait_ge(mod_psum, j - 1)
                        sp.dma_start(ada_rows[:, j % 2, :], a["ada_b"][l, j:j + 1, :]).then_inc(ada_slot[j % 2], 16)

            @block.tensor
            def _(pe):
                def mod(j):
                    pe.wait_ge(w_slot[j % 3], 16 * (j // 3 + 1))
                    pe.wait_ge(ada_slot[j % 2], 16 * (j // 2 + 1))
                    if j >= 2:
                        pe.wait_ge(mod_copied, j - 1)
                    for k in range(KD):
                        ins = pe.matmul(ps[0:2, j % 2, :], cT[:, k, :], wring[:, j % 3, k, :], start=(k == 0), stop=False)
                    ins.then_inc(w_free, 1)
                    pe.matmul(ps[0:2, j % 2, :], ones_row[:, 0:2], ada_rows[:, j % 2, :], start=False,
                              stop=True).then_inc(mod_psum, 1)

                def spread(j):
                    pe.wait_ge(mod_copied, j + 1)
                    if j >= 1:
                        pe.wait_ge(mod_taken, j)
                    if (j // 2) % 3 == 2:
                        for v in range(2):
                            ins = pe.matmul(ps[:, 3 + v, :], sel2[:, v, :], mod_row[:, j % 2, :], start=True, stop=True)
                    else:
                        for i in range(4):
                            ins = pe.transpose(ps[:, 2, 2 * i:2 * i + 2], mod_row[:, j % 2, i * P:(i + 1) * P], ident[0:2, 0:2])
                    ins.then_inc(mod_spread, 1)

                mod(0)
                for j in range(12):
                    if j + 1 < 12:
                        mod(j + 1)
                    spread(j)
                pe.wait_ge(mod_taken, 12)
                normalise(None, None, pe, 0, n1)
                pe.wait_ge(n1["ta"], NT)
                pe.wait_ge(n1["td"], NT)
                n = 0

                def bank_free():
                    if n >= 4:
                        pe.wait_ge(proj_taken, n - 3)

                for c in range(4):
                    pe.wait_ge(w_slot[(12 + c) % 3], 16 * ((12 + c) // 3 + 1))
                    for t in range(NT):
                        bank_free()
                        wide = 512 if c < 3 else 256
                        for k in range(KD):
                            ins = pe.matmul(ps[:, n % 4, 0:wide], hT[:, k, t * P:(t + 1) * P],
                                            wring[:, (12 + c) % 3, k, 0:wide], start=(k == 0), stop=(k == KD - 1))
                        ins.then_inc(proj_psum, 1)
                        n += 1
                for b in range(2):
                    for lo, wide in ((0, 512), (512, 128)):
                        bank_free()
                        for k in range(KD):
                            ins = pe.matmul(ps[:, n % 4, 0:wide], wring[:, 15 % 3, k, 256 + b * P:256 + (b + 1) * P],
                                            hT[:, k, lo:lo + wide], start=(k == 0), stop=(k == KD - 1))
                        ins.then_inc(proj_psum, 1)
                        n += 1
                pe.wait_ge(a_load, 32)
                for t in range(NT):
                    bank_free()
                    for k in range(KD):
                        ins = pe.matmul(ps[:, n % 4, 0:SMALL], hT[:, k, t * P:(t + 1) * P], wsmall[:, k, :],
                                        start=(k == 0), stop=(k == KD - 1))
                    ins.then_inc(proj_psum, 1)
                    n += 1

            @block.scalar
            def _(act):
                for j in range(12):
                    act.wait_ge(mod_psum, j + 1)
                    if j >= 2:
                        act.wait_ge(mod_spread, j - 1)
                    act.activation(mod_row[:, j % 2, :], ps[0:2, j % 2, :], ACT.Copy).then_inc(mod_copied, 1)
                normalise(act, None, None, 0, n1)
                n = 0
                for c in range(4):
                    for t in range(NT):
                        act.wait_ge(proj_psum, n + 1)
                        wide = 2 if c < 3 else 1
                        act.activation(proj[:, t, 2 * c:2 * c + wide, :],
                                       ps[:, n % 4, 0:wide * 256].rearrange("p (a b) -> p a b", a=wide),
                                       ACT.Copy).then_inc(proj_taken, 1)
                        n += 1
                for b in range(2):
                    for lo, wide in ((0, 512), (512, 128)):
                        act.wait_ge(proj_psum, n + 1)
                        act.activation(mqT[:, b, lo:lo + wide], ps[:, n % 4, 0:wide], ACT.Copy).then_inc(proj_taken, 1)
                        n += 1
                for t in range(NT):
                    act.wait_ge(proj_psum, n + 1)
                    act.activation(small[:, t, :], ps[:, n % 4, 0:SMALL], ACT.Copy).then_inc(proj_taken, 1)
                    n += 1
                act.wait_ge(proj_taken, n)

            @block.vector
            def _(dve):
                link = chain_of(dve, a_chain)
                for j in range(12):
                    dve.wait_ge(mod_spread, j + 1)
                    kind, half = j // 2, j % 2
                    if kind % 3 == 2:
                        for v in range(2):
                            ins = dve.tensor_copy(gate_bc[:, kind // 3, v, half * 512:(half + 1) * 512], ps[:, 3 + v, :])
                    else:
                        which = kind if kind < 2 else kind - 1
                        ins = dve.tensor_copy(modT[:, which, half * 4:(half + 1) * 4, :],
                                              ps[:, 2, 0:8].rearrange("p (a b) -> p a b", b=2))
                    ins.then_inc(mod_taken, 1)
                dve.wait_ge(mod_taken, 12)
                dve.wait_ge(a_load, 32)
                for w in range(2):
                    for v in range(2):
                        dve.scalar_tensor_tensor(modT[:, 2 * w + 1, :, v], modT[:, 2 * w + 1, :, v], 1.0,
                                                 normT[:, w, :], ALU.add, ALU.mult).then_inc(mod_final, 1)
                dve.wait_ge(mod_final, 4)
                normalise(None, dve, None, 0, dict(n1, link=link))

    b_load = K.sem("b_load")
    b_out = K.sem("b_out")
    b_chain = K.sem("b_chain")
    sig_done = K.sem("sig_done")
    sq15 = K.sem("sq15")
    root15 = K.sem("root15")
    normed = K.sem("normed")
    kq_psum = K.sem("kq_psum")
    kq_taken = K.sem("kq_taken")
    row_psum = K.sem("row_psum")
    row_taken = K.sem("row_taken")
    lat_psum = K.sem("lat_psum")
    lat_taken = K.sem("lat_taken")
    sgu_psum = K.sem("sgu_psum")
    sgu_taken = K.sem("sgu_taken")
    nf_ready = K.sem("nf_ready")
    log_ready = K.sem("log_ready")
    rows_in = K.sem("rows_in")
    rows_exp = K.sem("rows_exp")
    cols_psum = K.sem("cols_psum")
    cols_taken = K.sem("cols_taken")
    w_psum = K.sem("w_psum")
    w_exp = K.sem("w_exp")
    st_psum = K.sem("st_psum")
    sw_ready = K.sem("sw_ready")
    kw_ready = K.sem("kw_ready")
    nd_psum = K.sem("nd_psum")
    nd_taken = K.sem("nd_taken")
    c_psum = K.sem("c_psum")
    c_ready = K.sem("c_ready")
    v1_ready = K.sem("v1_ready")
    done_b = K.sem("done_b")

    def mixers(l):
        with nc.Block() as block:
            @block.sync
            def _(sp):
                loads = [(gate_b[:, :], a["gate_b"][l]), (m0[:, :], a["m0"][l]), (sel8[:, :, :], a["sel8"]),
                         (maskb[:, :, :], a["maskb"]), (wsT[:, :, :], a["wsT"][l]), (cmb[:, :], a["cmb"][l]),
                         (normg[:, :, :], a["normg"][l].partition_broadcast(P)), (cn[:, :, 1, :, :], a["cn0"][l]),
                         (ckvT[:, :, P:2 * P], a["cacheT"][l]), (krT[HD:QK, P:2 * P], a["kr_cacheT"][l]),
                         (cos_sin[HD:QK, :, :], a["cos_sin"])]
                for dst, src in loads:
                    sp.dma_start(dst, src).then_inc(b_load, 16)
                sp.wait_ge(b_load, 16 * 11)
                sp.wait_ge(normed, NT)
                sp.dma_start(o["ckv"][l], proj[:, 0, CKV, :]).then_inc(b_out, 16)
                sp.dma_start(o["kr"][l], small[:, 0, 2 * ROWS:2 * ROWS + ROPE]).then_inc(b_out, 16)
                sp.wait_ge(c_ready, 2 * 1)
                sp.dma_start(o["cn"][l], cn[:, :, 5, :, :]).then_inc(b_out, 16)
                sp.dma_start(o["m"][l], r_m[:, :]).then_inc(b_out, 16)
                sp.wait_ge(b_out, 64)

            @block.tensor
            def _(pe):
                pe.wait_ge(b_load, 16 * 11)
                for t in range(NT):
                    b = 2 * (t % 2)
                    if t >= 2:
                        pe.wait_ge(kq_taken, t - 1)
                        pe.wait_ge(row_taken, t - 1)
                    pe.transpose(ps[:, b, 0:P], proj[:, t, MK, 0:P], ident[:, :])
                    pe.transpose(ps[:, b, P:2 * P], proj[:, t, MK, P:2 * P], ident[:, :]).then_inc(kq_psum, 1)
                    pe.transpose(ps[0:ROWS, b + 1, 0:P], small[:, t, 0:ROWS], ident[:, :])
                    pe.transpose(ps[0:ROWS, b + 1, P:2 * P], small[:, t, ROWS:2 * ROWS], ident[:, :])
                    pe.transpose(ps[0:QK, b + 1, 2 * P:3 * P], small[:, t, 8:8 + QK], ident[:, :])
                    pe.transpose(ps[0:QK, b + 1, 3 * P:4 * P], small[:, t, 8 + ROPE:8 + ROPE + QK],
                                 ident[:, :]).then_inc(row_psum, 1)
                for t in range(NT):
                    pe.wait_ge(normed, t + 1)
                    if t >= 2:
                        pe.wait_ge(lat_taken, t - 1)
                    for i, (c, h) in enumerate(((CQ, 0), (CQ, 1), (CKV, 0), (CKV, 1))):
                        ins = pe.transpose(ps[:, 4 + t % 2, i * P:(i + 1) * P], proj[:, t, c, h * P:(h + 1) * P], ident[:, :])
                    ins.then_inc(lat_psum, 1)
                for t in range(NT):
                    if t >= 2:
                        pe.wait_ge(sgu_taken, t - 1)
                    for g in range(H):
                        ins = pe.matmul(ps[:, 6 + t % 2, g * HD:(g + 1) * HD], wsT[:, g, :],
                                        proj[:, t, CV, g * HD:(g + 1) * HD], start=True, stop=True)
                    ins.then_inc(sgu_psum, 1)
                pe.wait_ge(kq_taken, NT)
                pe.wait_ge(row_taken, NT)
                pe.wait_ge(rows_exp, 2)
                for q in range(4):
                    for t in range(NT):
                        at = ((q % 2) * NT + t) * ROWS
                        pe.transpose(ps[:, q // 2, at:at + ROWS], rowq[:, q, t * P:(t + 1) * P], ident[0:ROWS, 0:ROWS])
                for r in range(8):
                    ins = pe.matmul(ps[:, 2, r * NT:(r + 1) * NT], sel8[:, r, :], r_dec[:, :], start=True, stop=True)
                ins.then_inc(cols_psum, 1)
                pe.wait_ge(cols_taken, 1)
                pe.wait_ge(v1_ready, 2)
                pe.wait_ge(lat_taken, NT)
                pe.wait_ge(sgu_taken, NT)

                def tile(n):
                    s, d = n // 2, n % 2
                    return s if d == 0 else (NT - s) % NT

                def weights_and_scores(n):
                    t, d = tile(n), n % 2
                    span = slice(t * P, (t + 1) * P)
                    if n >= 2:
                        pe.wait_ge(w_exp, n - 1)
                    for m in range(H):
                        h = (m % 2) * 2 + m // 2
                        at_m = ps[:, d, m * P:(m + 1) * P]
                        pe.matmul(at_m, ident[:, :], maskb[:, d, :], start=True, stop=False)
                        ins = pe.matmul(at_m, sel8[:, d * H + h, :], r_u[:, span], start=False, stop=True)
                    ins.then_inc(w_psum, 1)
                    if n >= 1:
                        pe.wait_ge(sw_ready, n)
                    for m in range(H):
                        hp, hh = m // 2, m % 2
                        part = slice(hp * HD, (hp + 1) * HD)
                        ins = pe.matmul(ps[:, 2 + hp, hh * P:(hh + 1) * P], mkT[part, hh, span], mqT[part, hh, span],
                                        start=True, stop=True)
                    ins.then_inc(st_psum, 1)

                weights_and_scores(0)
                for n in range(2 * NT):
                    s, d, t = n // 2, n % 2, tile(n)
                    span = slice(t * P, (t + 1) * P)
                    if n + 1 < 2 * NT:
                        weights_and_scores(n + 1)
                    pe.wait_ge(sw_ready, n + 1)
                    if n >= 1:
                        pe.wait_ge(nd_taken, n)
                    if s >= 2:
                        pe.wait_ge(c_ready, n - 1)
                    for m in range(H):
                        hp, hh = m // 2, m % 2
                        h = hh * 2 + hp
                        part = slice(hp * HD, (hp + 1) * HD)
                        pe.matmul(ps[:, 4, h * (HD + 1):(h + 1) * (HD + 1)], swT[:, d, m * P:(m + 1) * P],
                                  v1[:, t, h, :], start=True, stop=True)
                    for m in range(H):
                        hp, hh = m // 2, m % 2
                        part = slice(hp * HD, (hp + 1) * HD)
                        ins = pe.matmul(ps[:, 5 + hp, hh * (HD + 1):(hh + 1) * (HD + 1)], mqT[part, hh, span],
                                        cn[part, d, s, hh, :], start=True, stop=True)
                    ins.then_inc(nd_psum, 1)
                    if s < NT - 1:
                        pe.wait_ge(kw_ready, n + 1)
                        if n >= 1:
                            pe.wait_ge(c_ready, n)
                        for m in range(H):
                            hp, hh = m // 2, m % 2
                            h = hh * 2 + hp
                            ins = pe.matmul(ps[hp * HD:(hp + 1) * HD, 7, hh * (HD + 1):(hh + 1) * (HD + 1)],
                                            kw[:, d, h * HD:(h + 1) * HD], v1[:, t, h, :], start=True, stop=True)
                        ins.then_inc(c_psum, 1)

            @block.scalar
            def _(act):
                act.activation(proj[:, :, MO, :], proj[:, :, MO, :], ACT.Sigmoid).then_inc(sig_done, 1)
                for t in range(NT):
                    ins = act.activation(v1[:, t, :, 0:HD], proj[:, t, MV, :].rearrange("p (h e) -> p h e", h=H), ACT.Copy)
                ins.then_inc(v1_ready, 1)
                for t in range(NT):
                    for i, c in enumerate((CV, CQ, CKV)):
                        act.activation(nd[:, :, 0:HD], proj[:, t, c, :].rearrange("p (h e) -> p h e", h=H), ACT.Square,
                                       accum_out=ss[:, 3 * t + i:3 * t + i + 1]).then_inc(sq15, 1)
                        act.wait_ge(sq15, 3 * t + i + 1)
                act.activation(rstd[:, 0:15], ss[:, 0:15], ACT.Sqrt, bias=eps_col[:, 0:1], scale=1.0 / 256).then_inc(root15, 1)
                for t in range(NT):
                    act.wait_ge(kq_psum, t + 1)
                    act.activation(mkT[:, :, t * P:(t + 1) * P], ps[:, 2 * (t % 2), 0:2 * P].rearrange("p (a b) -> p a b", a=2),
                                   ACT.Copy).then_inc(kq_taken, 1)
                act.wait_ge(nf_ready, 1)
                act.activation(r_e[:, :], r_e[:, :], ACT.Exp).then_inc(log_ready, 1)
                act.wait_ge(log_ready, 1)
                act.activation(r_e[:, :], r_e[:, :], ACT.Ln, bias=1.0).then_inc(log_ready, 1)
                act.wait_ge(b_load, 16 * 11)
                for t in range(NT):
                    act.wait_ge(lat_psum, t + 1)
                    kt = 0 if t == 0 else t + 1
                    act.activation(cqT[:, :, t * P:(t + 1) * P], ps[:, 4 + t % 2, 0:2 * P].rearrange("p (a b) -> p a b", a=2), ACT.Copy)
                    act.activation(ckvT[:, :, kt * P:(kt + 1) * P],
                                   ps[:, 4 + t % 2, 2 * P:4 * P].rearrange("p (a b) -> p a b", a=2),
                                   ACT.Copy).then_inc(lat_taken, 1)
                act.wait_ge(rows_in, 1)
                act.activation(rowq[:, 1:4, :], rowq[:, 1:4, :], ACT.Exp).then_inc(rows_exp, 1)
                act.activation(r_dec[:, :], r_dec[:, :], ACT.Exp).then_inc(rows_exp, 1)
                act.wait_ge(cols_taken, 1)
                for n in range(2 * NT):
                    s, d = n // 2, n % 2
                    t = s if d == 0 else (NT - s) % NT
                    act.wait_ge(w_psum, n + 1)
                    if n >= 2:
                        act.wait_ge(sw_ready, n - 1)
                    for m in range(H):
                        h = (m % 2) * 2 + m // 2
                        ins = act.activation(wT[:, d, m * P:(m + 1) * P], ps[:, d, m * P:(m + 1) * P], ACT.Exp,
                                             bias=cols[:, R_A * NT + t, 32 * d + h:32 * d + h + 1])
                    ins.then_inc(w_exp, 1)

            @block.vector
            def _(dve):
                link = chain_of(dve, b_chain)
                dve.memset(v1[:, :, :, HD:HD + 1], 1.0).then_inc(v1_ready, 1)
                dve.memset(cn[:, :, 0, :, :], 0.0)
                dve.memset(r_b[:, :], 0.0)
                dve.memset(r_u[:, :], 0.0)
                dve.memset(r_prev[:, :], 0.0)
                dve.memset(r_end[:, :], 0.0)
                link(dve.memset(r_m[:, :], 0.0))
                dve.wait_ge(b_load, 16 * 11)
                for t in range(NT):
                    b = 2 * (t % 2) + 1
                    span = slice(t * P, (t + 1) * P)
                    dve.wait_ge(row_psum, t + 1)
                    dve.tensor_scalar(r_i[:, span], ps[0:ROWS, b, 0:P], gate_b[:, 0:1], None, ALU.add)
                    link(dve.tensor_scalar(r_f[:, span], ps[0:ROWS, b, P:2 * P], gate_b[:, 1:2], None, ALU.add))
                    if t == 0:
                        link(dve.tensor_copy(krT[HD:QK, 0:P], ps[HD:QK, b, 2 * P:3 * P]))
                    else:
                        pos = slice((t - 1) * P, t * P)
                        key = slice((t + 1) * P, (t + 2) * P)
                        link(dve.tensor_tensor(krT[HD:QK, key], ps[HD:QK, b, 2 * P:3 * P], cos_sin[HD:QK, 0, pos], ALU.mult))
                        link(dve.tensor_tensor(xn[HD:QK, 1, 0:P], ps[HD:QK, b, 3 * P:4 * P], cos_sin[HD:QK, 1, pos], ALU.mult))
                        link(dve.tensor_tensor(krT[HD:QK, key], krT[HD:QK, key], xn[HD:QK, 1, 0:P], ALU.add))
                    dve.sem_inc(row_taken, 1)
                dve.scalar_tensor_tensor(r_e[:, :], r_f[:, :], -1.0, r_f[:, :], ALU.mult, ALU.min).then_inc(nf_ready, 1)
                dve.wait_ge(root15, 1)
                link(dve.reciprocal(rstd[:, 0:15], rstd[:, 0:15]))
                for t in range(NT):
                    for i, c in enumerate((CV, CQ, CKV)):
                        ins = dve.scalar_tensor_tensor(proj[:, t, c, :], proj[:, t, c, :], rstd[:, 3 * t + i:3 * t + i + 1],
                                                       normg[:, i, :], ALU.mult, ALU.mult)
                    ins.then_inc(normed, 1)
                dve.wait_ge(log_ready, 2)
                link(dve.scalar_tensor_tensor(r_f[:, :], r_f[:, :], 0.0, r_e[:, :], ALU.min, ALU.subtract))
                fwd, bwd_rows = slice(0, H), slice(32, 32 + H)
                for lo, hi in ((0, P), (P, T)):
                    dve.tensor_tensor_scan(r_b[fwd, lo:hi], one_col[fwd, :].to_broadcast([H, hi - lo]), r_f[fwd, lo:hi], 0.0, ALU.mult, ALU.add)
                    rv = slice(hi - 1, lo - 1 if lo else None, -1)
                    link(dve.tensor_tensor_scan(r_b[bwd_rows, rv], one_col[bwd_rows, :].to_broadcast([H, hi - lo]), r_f[bwd_rows, rv], 0.0,
                                                ALU.mult, ALU.add))
                link(dve.tensor_tensor(rowq[:, R_A, :], r_i[:, :], r_b[:, :], ALU.subtract))
                for lo, hi in ((0, P), (P, T)):
                    rv = slice(hi - 1, lo - 1 if lo else None, -1)
                    dve.tensor_tensor_scan(r_u[fwd, lo:hi], rowq[fwd, R_A, lo:hi], rowq[fwd, R_A, lo:hi],
                                           m0[fwd, 0:1] if lo else 0.0, ALU.max, ALU.max)
                    link(dve.tensor_tensor_scan(r_u[bwd_rows, rv], rowq[bwd_rows, R_A, rv], rowq[bwd_rows, R_A, rv],
                                                m0[bwd_rows, 0:1] if lo else 0.0, ALU.max, ALU.max))
                dve.tensor_copy(r_prev[fwd, 1:2], m0[fwd, :])
                dve.tensor_copy(r_prev[fwd, 2:NT], r_u[fwd, 2 * P - 1:T - P:P])
                dve.tensor_copy(r_end[fwd, :], r_u[fwd, P - 1:T:P])
                dve.tensor_copy(r_prev[bwd_rows, NT - 1:NT], m0[bwd_rows, :])
                dve.tensor_copy(r_prev[bwd_rows, 1:NT - 1], r_u[bwd_rows, 2 * P:T:P])
                dve.tensor_copy(r_end[bwd_rows, :], r_u[bwd_rows, 0:T:P])
                dve.tensor_tensor(r_m[fwd, :], r_b[fwd, P - 1:P], r_u[fwd, P - 1:P], ALU.add)
                link(dve.tensor_tensor(r_m[bwd_rows, :], r_b[bwd_rows, 0:1], r_u[bwd_rows, 0:1], ALU.add))

                def tiles(ap):
                    return ap.rearrange("p (t s) -> p t s", t=NT)

                dve.tensor_tensor(tiles(rowq[:, R_WK, :]), tiles(rowq[:, R_A, :]), col(r_end[:, :], P), ALU.subtract)
                dve.tensor_tensor(tiles(rowq[:, R_WIN, :]), col(r_prev[:, :], P), tiles(r_u[:, :]), ALU.subtract)
                dve.scalar_tensor_tensor(rowq[:, R_EM, :], r_b[:, :], -1.0, r_u[:, :], ALU.mult, ALU.subtract)
                link(dve.tensor_tensor(r_dec[:, :], r_prev[:, :], r_end[:, :], ALU.subtract))
                link(dve.tensor_scalar(r_u[:, :], r_u[:, :], -1.0, None, ALU.mult))
                dve.sem_inc(rows_in, 1)
                for t in range(NT):
                    dve.wait_ge(sgu_psum, t + 1)
                    for g in range(H):
                        span = slice(g * HD, (g + 1) * HD)
                        ins = dve.scalar_tensor_tensor(mixed[:, t, 256 + g * HD:256 + (g + 1) * HD], ps[:, 6 + t % 2, span],
                                                       cmb[:, g:g + 1], proj[:, t, CU, span], ALU.add, ALU.mult)
                    ins.then_inc(sgu_taken, 1)
                dve.wait_ge(cols_psum, 1)
                link(dve.tensor_copy(cols[:, 0:2 * NT, :], ps[:, 0, 0:2 * NT * ROWS].rearrange("p (a b) -> p a b", b=ROWS)))
                link(dve.tensor_copy(cols[:, 2 * NT:, :], ps[:, 1, 0:2 * NT * ROWS].rearrange("p (a b) -> p a b", b=ROWS)))
                link(dve.tensor_copy(dec[:, :, :], ps[:, 2, 0:8 * NT].rearrange("p (a b) -> p a b", b=NT)))
                dve.sem_inc(cols_taken, 1)
                for n in range(2 * NT):
                    s, d = n // 2, n % 2
                    t = s if d == 0 else (NT - s) % NT
                    dve.wait_ge(w_exp, n + 1)
                    dve.wait_ge(st_psum, n + 1)
                    if n >= 2:
                        dve.wait_ge(nd_psum, n - 1)
                    pair = lambda ap: ap.rearrange("p (a b) -> p a b", a=2)
                    dve.scalar_tensor_tensor(pair(swT[:, d, :]), ps[:, 2:4, 0:2 * P], HD ** -0.5, pair(wT[:, d, :]),
                                             ALU.mult, ALU.mult).then_inc(sw_ready, 1)
                    heads = lambda ap: ap.rearrange("p (h e) -> p h e", h=H)
                    if s < NT - 1:
                        if n >= 2:
                            dve.wait_ge(c_psum, n - 1)
                        dve.scalar_tensor_tensor(heads(kw[:, d, :]), heads(proj[:, t, MK, :]), HD ** -0.5,
                                                 col(cols[:, R_WK * NT + t, 32 * d:32 * d + H], HD), ALU.mult,
                                                 ALU.mult).then_inc(kw_ready, 1)
                    dve.wait_ge(nd_psum, n + 1)
                    win = cols[:, R_WIN * NT + t, 32 * d:32 * d + H].rearrange("p (b a) -> p a b", a=2)
                    link(dve.tensor_tensor(nd[:, :, :].rearrange("p (b a) e -> p a b e", a=2),
                                           ps[:, 5:7, 0:2 * (HD + 1)].rearrange("p a (b e) -> p a b e", b=2),
                                           col(win, HD + 1), ALU.mult))
                    link(dve.tensor_tensor(nd[:, :, :], ps[:, 4, 0:H * (HD + 1)].rearrange("p (h e) -> p h e", h=H),
                                           nd[:, :, :], ALU.add))
                    dve.sem_inc(nd_taken, 1)
                    link(dve.scalar_tensor_tensor(dd[:, 0, :], nd[:, :, HD], -1.0, nd[:, :, HD], ALU.mult, ALU.max))
                    link(dve.tensor_tensor(dd[:, 1, :], dd[:, 0, :], cols[:, R_EM * NT + t, 32 * d:32 * d + H], ALU.max))
                    link(dve.reciprocal(dd[:, 0, :], dd[:, 1, :]))
                    out = mixed[:, t, 0:256] if d == 0 else bwd[:, t, :]
                    link(dve.tensor_tensor(heads(out), nd[:, :, 0:HD], col(dd[:, 0, :], HD), ALU.mult))
                    if s < NT - 1:
                        dve.wait_ge(c_psum, n + 1)
                        to = 5 if s == 0 else s + 1
                        for m in range(H):
                            hp, hh = m // 2, m % 2
                            h = hh * 2 + hp
                            part = slice(hp * HD, (hp + 1) * HD)
                            ins = dve.scalar_tensor_tensor(cn[part, d, to, hh, :], cn[part, d, s, hh, :],
                                                           dec[part, d * H + h, t:t + 1],
                                                           ps[part, 7, hh * (HD + 1):(hh + 1) * (HD + 1)], ALU.mult, ALU.add)
                        ins.then_inc(c_ready, 1)
                link(dve.tensor_tensor(mixed[:, :, 0:256], mixed[:, :, 0:256], bwd[:, :, :], ALU.add))
                dve.wait_ge(sig_done, 1)
                link(dve.tensor_tensor(mixed[:, :, 0:256], mixed[:, :, 0:256], proj[:, :, MO, :], ALU.mult))

        if upto >= 3:
            attention(l)

    c_load = K.sem("c_load")
    wout_slot = K.sem("wout_slot")
    q_psum = K.sem("q_psum")
    q_act = K.sem("q_act")
    q_dve = K.sem("q_dve")
    k_psum = K.sem("k_psum")
    k_act = K.sem("k_act")
    kr_ready = K.sem("kr_ready")
    v_psum = K.sem("v_psum")
    v_dve = K.sem("v_dve")
    s_psum = K.sem("s_psum")
    max_ready = K.sem("max_ready")
    p_ready = K.sem("p_ready")
    pt_psum = K.sem("pt_psum")
    pt_taken = K.sem("pt_taken")
    o_psum = K.sem("o_psum")
    o_taken = K.sem("o_taken")
    mt_psum = K.sem("mt_psum")
    mt_taken = K.sem("mt_taken")
    y_psum = K.sem("y_psum")
    y_taken = K.sem("y_taken")
    c_chain = K.sem("c_chain")

    def attention(l):
        units = [(h, t) for h in range(AH) for t in range(NT)]

        def keys(t):
            return (0, P, [0]) if t == 0 else (P, KT * P, list(range(1, KT)))

        with nc.Block() as block:
            @block.sync
            def _(sp):
                sp.dma_start(wuq[:, :, :], a["wuq"][l]).then_inc(c_load, 16)
                sp.dma_start(wqs[:, :, :], a["wqs"][l]).then_inc(c_load, 16)
                sp.dma_start(wuk[:, :, :], a["wuk"][l]).then_inc(c_load, 16)
                sp.dma_start(wuv[:, :, :], a["wuv"][l]).then_inc(c_load, 16)
                sp.dma_start(wout[:, :, :], a["w_out"][l, 0]).then_inc(wout_slot, 16)
                sp.wait_ge(y_psum, NT)
                sp.dma_start(wout[:, :, :], a["w_out"][l, 1]).then_inc(wout_slot, 16)

            @block.tensor
            def _(pe):
                pe.wait_ge(c_load, 64)
                for h in range(AH):
                    b = 3 * (h % 2)
                    if h >= 2:
                        pe.wait_ge(q_act, h - 1)
                        pe.wait_ge(q_dve, h - 1)
                    for k in range(2):
                        pe.matmul(ps[0:QK, b, :], wuq[:, k, h * QK:(h + 1) * QK], cqT[:, k, P:T], start=(k == 0), stop=(k == 1))
                    for k in range(2):
                        pe.matmul(ps[0:QK, b + 1, 0:P], wuq[:, k, h * QK:(h + 1) * QK], cqT[:, k, 0:P], start=(k == 0), stop=(k == 1))
                    for k in range(2):
                        ins = pe.matmul(ps[HD:QK, b + 2, :], wqs[:, k, h * ROPE:(h + 1) * ROPE], cqT[:, k, P:T],
                                        start=(k == 0), stop=(k == 1))
                    ins.then_inc(q_psum, 1)
                pe.wait_ge(q_act, AH)
                pe.wait_ge(q_dve, AH)
                for h in range(AH):
                    b = 2 * (h % 2)
                    if h >= 2:
                        pe.wait_ge(k_act, h - 1)
                    for k in range(2):
                        pe.matmul(ps[0:HD, b, :], wuk[:, k, h * HD:(h + 1) * HD], ckvT[:, k, 0:512], start=(k == 0), stop=(k == 1))
                    for k in range(2):
                        ins = pe.matmul(ps[0:HD, b + 1, 0:256], wuk[:, k, h * HD:(h + 1) * HD], ckvT[:, k, 512:768],
                                        start=(k == 0), stop=(k == 1))
                    ins.then_inc(k_psum, 1)
                for t in range(KT):
                    if t >= 2:
                        pe.wait_ge(v_dve, t - 1)
                    for k in range(2):
                        ins = pe.matmul(ps[:, 4 + t % 2, :], ckvT[:, k, t * P:(t + 1) * P], wuv[:, k, :], start=(k == 0), stop=(k == 1))
                    ins.then_inc(v_psum, 1)
                pe.wait_ge(k_act, AH)
                pe.wait_ge(v_dve, KT)
                pe.wait_ge(kr_ready, 1)

                def scores(n):
                    h, t = units[n]
                    lo, hi, _ = keys(t)
                    b = 2 * (n % 2)
                    if n >= 2:
                        pe.wait_ge(p_ready, n - 1)
                    q = qT[:, h, t * P:(t + 1) * P]
                    mid = min(hi, lo + 512)
                    ins = pe.matmul(ps[:, b, 0:mid - lo], q, kT[:, h, lo:mid], start=True, stop=True)
                    if hi > mid:
                        ins = pe.matmul(ps[:, b + 1, 0:hi - mid], q, kT[:, h, mid:hi], start=True, stop=True)
                    ins.then_inc(s_psum, 1)

                def turn(n):
                    h, t = units[n]
                    pe.wait_ge(p_ready, n + 1)
                    if n >= 1:
                        pe.wait_ge(pt_taken, n)
                    for i in range(len(keys(t)[2])):
                        ins = pe.transpose(ps[:, 4 + i // 4, (i % 4) * P:(i % 4 + 1) * P], prob[:, n % 2, i * P:(i + 1) * P], ident[:, :])
                    ins.then_inc(pt_psum, 1)

                def attend(n):
                    h, t = units[n]
                    pe.wait_ge(pt_taken, n + 1)
                    if n >= 2:
                        pe.wait_ge(o_taken, n - 1)
                    tiles = keys(t)[2]
                    for i, kt in enumerate(tiles):
                        ins = pe.matmul(ps[:, 6 + n % 2, 0:HD], probT[:, n % 2, i * P:(i + 1) * P], val[:, kt, h * HD:(h + 1) * HD],
                                        start=(i == 0), stop=(i == len(tiles) - 1))
                    ins.then_inc(o_psum, 1)

                scores(0)
                for n in range(len(units)):
                    if n + 1 < len(units):
                        scores(n + 1)
                    turn(n)
                    if n >= 1:
                        attend(n - 1)
                attend(len(units) - 1)
                pe.wait_ge(o_taken, len(units))
                for t in range(NT):
                    if t >= 2:
                        pe.wait_ge(mt_taken, t - 1)
                    for k in range(KD):
                        ins = pe.transpose(ps[:, 2 * (t % 2) + k // 4, (k % 4) * P:(k % 4 + 1) * P], mixed[:, t, k * P:(k + 1) * P], ident[:, :])
                    ins.then_inc(mt_psum, 1)
                pe.wait_ge(mt_taken, NT)
                for half in range(2):
                    pe.wait_ge(wout_slot, 16 * (half + 1))
                    for t in range(NT):
                        n = half * NT + t
                        if n >= 2:
                            pe.wait_ge(y_taken, n - 1)
                        for k in range(KD):
                            ins = pe.matmul(ps[:, 4 + n % 2, :], hT[:, k, t * P:(t + 1) * P], wout[:, k, :],
                                            start=(k == 0), stop=(k == KD - 1))
                        ins.then_inc(y_psum, 1)

            @block.scalar
            def _(act):
                for h in range(AH):
                    b = 3 * (h % 2)
                    act.wait_ge(q_psum, h + 1)
                    act.activation(qT[0:HD, h, P:T], ps[0:HD, b, :], ACT.Copy)
                    act.activation(qT[:, h, 0:P], ps[0:QK, b + 1, 0:P], ACT.Copy).then_inc(q_act, 1)
                for h in range(AH):
                    b = 2 * (h % 2)
                    act.wait_ge(k_psum, h + 1)
                    act.activation(kT[0:HD, h, 0:512], ps[0:HD, b, :], ACT.Copy)
                    act.activation(kT[0:HD, h, 512:768], ps[0:HD, b + 1, 0:256], ACT.Copy).then_inc(k_act, 1)
                for n, (h, t) in enumerate(units):
                    lo, hi, _ = keys(t)
                    act.wait_ge(max_ready, n + 1)
                    if n >= 2:
                        act.wait_ge(pt_psum, n - 1)
                        act.wait_ge(o_taken, n - 1)
                    act.activation(prob[:, n % 2, 0:hi - lo],
                                   ps[:, 2 * (n % 2):2 * (n % 2) + 2, :].rearrange("p a b -> p (a b)")[:, 0:hi - lo], ACT.Exp,
                                   bias=amax[:, n % 2, 1:2], scale=SCALE, accum_out=amax[:, n % 2, 2:3]).then_inc(p_ready, 1)
                for t in range(NT):
                    act.wait_ge(mt_psum, t + 1)
                    b = 2 * (t % 2)
                    act.activation(hT[:, :, t * P:(t + 1) * P], ps[:, b:b + 2, :].rearrange("p a (c d) -> p (a c) d", d=P),
                                   ACT.Copy).then_inc(mt_taken, 1)

            @block.vector
            def _(dve):
                link = chain_of(dve, c_chain)
                for h in range(AH):
                    b = 3 * (h % 2)
                    dve.wait_ge(q_psum, h + 1)
                    link(dve.tensor_tensor(rot[HD:QK, 0, :], ps[HD:QK, b, :], cos_sin[HD:QK, 0, :], ALU.mult))
                    link(dve.tensor_tensor(rot[HD:QK, 1, :], ps[HD:QK, b + 2, :], cos_sin[HD:QK, 1, :], ALU.mult))
                    dve.tensor_tensor(qT[HD:QK, h, P:T], rot[HD:QK, 0, :], rot[HD:QK, 1, :], ALU.add).then_inc(q_dve, 1)
                    dve.wait_ge(q_dve, h + 1)
                dve.tensor_copy(kT[HD:QK, :, :], krT[HD:QK, :].unsqueeze(1).to_broadcast([ROPE, AH, KT * P])).then_inc(kr_ready, 1)
                for t in range(KT):
                    dve.wait_ge(v_psum, t + 1)
                    dve.tensor_copy(val[:, t, :], ps[:, 4 + t % 2, :]).then_inc(v_dve, 1)

                def maxima(n):
                    h, t = units[n]
                    lo, hi, _ = keys(t)
                    dve.wait_ge(s_psum, n + 1)
                    if n >= 2:
                        dve.wait_ge(p_ready, n - 1)
                    link(dve.tensor_reduce(amax[:, n % 2, 0:1],
                                           ps[:, 2 * (n % 2):2 * (n % 2) + 2, :].rearrange("p a b -> p (a b)")[:, 0:hi - lo], AX.X, ALU.max))
                    dve.tensor_scalar(amax[:, n % 2, 1:2], amax[:, n % 2, 0:1], -SCALE, None, ALU.mult).then_inc(max_ready, 1)

                def turned(n):
                    dve.wait_ge(pt_psum, n + 1)
                    if n >= 2:
                        dve.wait_ge(o_psum, n - 1)
                    tiles = len(keys(units[n][1])[2])
                    dve.tensor_copy(probT[:, n % 2, 0:tiles * P],
                                    ps[:, 4:6, :].rearrange("p a b -> p (a b)")[:, 0:tiles * P]).then_inc(pt_taken, 1)

                def finish(n):
                    h, t = units[n]
                    dve.wait_ge(p_ready, n + 1)
                    link(dve.reciprocal(amax[:, n % 2, 3:4], amax[:, n % 2, 2:3]))
                    dve.wait_ge(o_psum, n + 1)
                    dve.tensor_scalar(mixed[:, t, 512 + h * HD:512 + (h + 1) * HD], ps[:, 6 + n % 2, 0:HD],
                                      amax[:, n % 2, 3:4], None, ALU.mult).then_inc(o_taken, 1)
                    dve.wait_ge(o_taken, n + 1)

                maxima(0)
                for n in range(len(units)):
                    if n >= 1:
                        finish(n - 1)
                    if n + 1 < len(units):
                        maxima(n + 1)
                    turned(n)
                finish(len(units) - 1)
                for half in range(2):
                    for t in range(NT):
                        n, v = half * NT + t, (0 if t == 0 else 1)
                        span = slice(half * 512, (half + 1) * 512)
                        dve.wait_ge(y_psum, n + 1)
                        link(dve.tensor_tensor(xn[:, n % 2, 0:512], ps[:, 4 + n % 2, :], gate_bc[:, 0, v, span], ALU.mult))
                        dve.sem_inc(y_taken, 1)
                        dve.tensor_tensor(x[:, t, span], x[:, t, span], xn[:, n % 2, 0:512], ALU.add)

    s6 = ExitStack()
    slots = sb("slots", [P, 3, T], stack=s6)
    s7 = ExitStack()
    wq = sb("wq", [P, 2, KD, 512], stack=s7)
    skT = sb("skT", [P, 2, NKEYS], stack=s7)
    pqT = sb("pqT", [P, 2, T], stack=s7)
    topv = sb("topv", [P, NT, RH, 2, TOP], stack=s7)
    topi = sb("topi", [P, NT, RH, 2, TOP], U32, stack=s7)
    topf = sb("topf", [P, NT, RH, 2, TOP], BF16, stack=s7)
    rest = sb("rest", [P, 2, 256], stack=s7)
    cand = sb("cand", [P, 2, 256], stack=s7)
    best = sb("best", [P, NT, RH, TOP], stack=s7)
    pos = sb("pos", [P, NT, SLOTS], U32, stack=s7)
    pos12 = sb("pos12", [P, 2, NT, SLOTS], U32, stack=s7)
    posf = sb("posf", [P, 2, NT, SLOTS], BF16, stack=s7)
    gsum = sb("gsum", [P, 2, NT, RH], stack=s7)
    iota16 = sb("iota16", [P, TOP], BF16, stack=s7)
    hot = sb("hot", [P, SLOTS, TOP], BF16, stack=s7)
    keysel = sb("keysel", [P, NT, 2, SLOTS], stack=s7)
    s7.close()
    s8 = ExitStack()
    iota = sb("iota", [P, NKEYS], stack=s8)
    stage = sb("stage", [P, 3, 2 * GB], stack=s8)
    hot1 = sb("hot1", [P, 2, 4, NKEYS], stack=s8)
    hot2 = sb("hot2", [P, 2, 4, NKEYS], stack=s8)
    gmat = sb("gmat", [P, 2, NKEYS, GB], stack=s8)
    s8.close()
    s6.close()
    s9 = ExitStack()
    y = sb("y", [P, NT, D], stack=s9)
    ut = sb("ut", [P, NG, KD, P], stack=s9)
    vt = sb("vt", [P, 2, NG, D], stack=s9)
    gt = sb("gt", [P, 2, NB, NG, GB], stack=s9)
    at = sb("at", [P, 2, NG, T], stack=s9)
    s9.close()

    d_load = K.sem("d_load")
    wq_slot = [K.sem(f"wq_slot{i}") for i in range(2)]
    n2 = dict(tp=K.sem("n2_psum"), ta=K.sem("n2_act"), td=K.sem("n2_dve"), sq=K.sem("n2_sq"), rt=K.sem("n2_root"),
              xn=K.sem("n2_xn"))
    pq_psum = K.sem("pq_psum")
    pq_taken = K.sem("pq_taken")
    sc_psum = K.sem("sc_psum")
    sc_taken = K.sem("sc_taken")
    d_chain = K.sem("d_chain")
    gate_in = K.sem("gate_in")
    gate_exp = K.sem("gate_exp")
    slot_in = K.sem("slot_in")
    slot_psum = K.sem("slot_psum")
    slot_taken = K.sem("slot_taken")

    def retrieve(l):
        with nc.Block() as block:
            @block.sync
            def _(sp):
                sp.dma_start(skT[:, :, :], a["skT"][l]).then_inc(d_load, 16)
                sp.dma_start(iota16[:, :], a["iota16"]).then_inc(d_load, 16)
                for c in range(4):
                    if c >= 2:
                        sp.wait_ge(pq_psum, 8 * (c - 1))
                    sp.dma_start(wq[:, c % 2, :, :], a["wq"][l, c]).then_inc(wq_slot[c % 2], 16)

            @block.tensor
            def _(pe):
                normalise(None, None, pe, 1, n2)
                pe.wait_ge(n2["ta"], NT)
                pe.wait_ge(n2["td"], NT)
                pe.wait_ge(d_load, 32)

                def query(j):
                    c = j // 4
                    pe.wait_ge(wq_slot[c % 2], 16 * (c // 2 + 1))
                    for half in range(2):
                        n = 2 * j + half
                        if n >= 2:
                            pe.wait_ge(pq_taken, n - 1)
                        for k in range(KD):
                            ins = pe.matmul(ps[:, half, 0:HALF], wq[:, c % 2, k, (j % 4) * P:(j % 4 + 1) * P],
                                            hT[:, k, half * HALF:(half + 1) * HALF], start=(k == 0), stop=(k == KD - 1))
                        ins.then_inc(pq_psum, 1)

                query(0)
                for j in range(2 * RH):
                    if j + 1 < 2 * RH:
                        query(j + 1)
                    pe.wait_ge(pq_taken, 2 * (j + 1))
                    if j >= 2:
                        pe.wait_ge(sc_taken, j - 1)
                    for t in range(NT):
                        b = 2 + 2 * (j % 2) + t // 4
                        ins = pe.matmul(ps[:, b, (t % 4) * P:(t % 4 + 1) * P], pqT[:, j % 2, t * P:(t + 1) * P],
                                        skT[:, j % 2, :], start=True, stop=True)
                    ins.then_inc(sc_psum, 1)
                for t in range(NT):
                    pe.wait_ge(slot_in, t + 1)
                    if t >= 2:
                        pe.wait_ge(slot_taken, t - 1)
                    b = 6 + t % 2
                    pe.transpose(ps[:, b, 0:P], keysel[:, t, 0, :], ident[:, :])
                    pe.transpose(ps[:, b, P:2 * P], keysel[:, t, 1, :], ident[:, :])
                    pe.transpose(ps[:, b, 2 * P:3 * P], best[:, t, :, :].rearrange("p h s -> p (h s)"), ident[:, :]).then_inc(slot_psum, 1)

            @block.scalar
            def _(act):
                normalise(act, None, None, 1, n2)
                for n in range(4 * RH):
                    j, half = n // 2, n % 2
                    act.wait_ge(pq_psum, n + 1)
                    if j >= 2:
                        act.wait_ge(sc_psum, j - 1)
                    act.activation(pqT[:, j % 2, half * HALF:(half + 1) * HALF], ps[:, half, 0:HALF], ACT.Copy).then_inc(pq_taken, 1)
                act.wait_ge(gate_in, 1)
                act.activation(best[:, :, :, :], best[:, :, :, :], ACT.Exp).then_inc(gate_exp, 1)
                for t in range(NT):
                    act.wait_ge(slot_psum, t + 1)
                    act.activation(slots[:, :, t * P:(t + 1) * P], ps[:, 6 + t % 2, 0:3 * P].rearrange("p (a b) -> p a b", a=3),
                                   ACT.Copy).then_inc(slot_taken, 1)

            @block.vector
            def _(dve):
                link = chain_of(dve, d_chain)
                normalise(None, dve, None, 1, dict(n2, link=link))

                def top16(values, v, i, left):
                    link(dve.max(v[:, 0:8], values))
                    dve.max_index(i[:, 0:8], v[:, 0:8], values)
                    link(dve.match_replace(left, v[:, 0:8], values, -3.0e38))
                    link(dve.max(v[:, 8:16], left))
                    return dve.max_index(i[:, 8:16], v[:, 8:16], left)

                for j in range(2 * RH):
                    h, half = j // 2, j % 2
                    dve.wait_ge(sc_psum, j + 1)
                    for t in range(NT):
                        b = 2 + 2 * (j % 2) + t // 4
                        ins = top16(ps[:, b, (t % 4) * P:(t % 4 + 1) * P], topv[:, t, h, half, :], topi[:, t, h, half, :],
                                    rest[:, t % 2, 0:P])
                    ins.then_inc(sc_taken, 1)
                dve.wait_ge(sc_taken, 2 * RH)
                link(dve.tensor_copy(topf[:, :, :, :, :].rearrange("p t h a s -> p (t h a s)"),
                                     topi[:, :, :, :, :].rearrange("p t h a s -> p (t h a s)")))
                n = 0
                for t in range(NT):
                    for h in range(RH):
                        c = n % 2
                        link(dve.tensor_tensor(cand[:, c, :].rearrange("p (i j) -> p i j", i=TOP), col(topv[:, t, h, 0, :], TOP),
                                               topv[:, t, h, 1, :].unsqueeze(1).to_broadcast([P, TOP, TOP]), ALU.add))
                        ins = top16(cand[:, c, :], best[:, t, h, :], pos[:, t, h * TOP:(h + 1) * TOP], rest[:, c, :])
                        n += 1
                link(ins)
                link(dve.tensor_copy(gsum[:, 0, :, :].rearrange("p t h -> p (t h)"),
                                     best[:, :, :, 0:1].rearrange("p t h s -> p (t h s)")))
                link(dve.tensor_tensor(best[:, :, :, :].rearrange("p t h s -> p (t h) s"),
                                       best[:, :, :, :].rearrange("p t h s -> p (t h) s"),
                                       col(gsum[:, 0, :, :].rearrange("p t h -> p (t h)"), TOP), ALU.subtract))
                dve.sem_inc(gate_in, 1)
                link(dve.tensor_scalar(pos12[:, 0, :, :], pos[:, :, :], 4, None, ALU.logical_shift_right))
                link(dve.tensor_scalar(pos12[:, 1, :, :], pos[:, :, :], TOP - 1, None, ALU.bitwise_and))
                link(dve.tensor_copy(posf[:, :, :, :], pos12[:, :, :, :]))
                dve.wait_ge(gate_exp, 1)
                link(dve.tensor_reduce(gsum[:, 0, :, :].rearrange("p t h -> p (t h)"), best[:, :, :, :].rearrange("p t h s -> p (t h) s"), AX.X, ALU.add))
                link(dve.reciprocal(gsum[:, 1, :, :], gsum[:, 0, :, :]))
                link(dve.tensor_tensor(best[:, :, :, :].rearrange("p t h s -> p (t h) s"),
                                       best[:, :, :, :].rearrange("p t h s -> p (t h) s"),
                                       col(gsum[:, 1, :, :].rearrange("p t h -> p (t h)"), TOP), ALU.mult))
                for t in range(NT):
                    for half in range(2):
                        link(dve.tensor_tensor(hot[:, :, :], col(posf[:, half, t, :], TOP),
                                               iota16[:, :].unsqueeze(1).to_broadcast([P, SLOTS, TOP]), ALU.is_equal))
                        link(dve.tensor_tensor(hot[:, :, :].rearrange("p (h s) j -> p h s j", h=RH),
                                               hot[:, :, :].rearrange("p (h s) j -> p h s j", h=RH),
                                               topf[:, t, :, half, :].unsqueeze(2).to_broadcast([P, RH, TOP, TOP]), ALU.mult))
                        link(dve.tensor_reduce(keysel[:, t, half, :], hot[:, :, :], AX.X, ALU.add))
                    dve.sem_inc(slot_in, 1)

    e_load = K.sem("e_load")
    staged = K.sem("staged")
    hots_ready = K.sem("hots_ready")
    hots_used = K.sem("hots_used")
    gm_taken = K.sem("gm_taken")
    gm_stored = [K.sem(f"gm_stored{i}") for i in range(2)]

    def gate_matrices(l):
        quads = GB // 4
        turns = NB // 2
        with nc.Block() as block:
            @block.sync
            def _(sp):
                sp.dma_start(iota[:, :], a["iota"]).then_inc(e_load, 16)
                with sp.Fori(0, turns) as i:
                    for b in range(2):
                        sp.wait_ge(gm_taken, i * (2 * quads) + (b + 1) * quads + 8)
                        sp.dma_start(gates_dram[i * 2 + b], gmat[:, b, :, :].rearrange("p a b -> p (a b)")).then_inc(gm_stored[b], 16)
                for b in range(2):
                    sp.wait_ge(gm_stored[b], 16 * turns + 16)

            @block.vector
            def _(dve):
                dve.wait_ge(e_load, 16)
                dve.sem_inc(staged, 1)
                with dve.Fori(0, turns) as i:
                    dve.tensor_copy(stage[:, :, :], slots[:, :, bass.ds(i * (2 * GB), 2 * GB)]).then_inc(staged, 1)
                    dve.wait_ge(staged, i + 2)
                    for q in range(2 * quads):
                        s = q % 2
                        dve.wait_ge(hots_used, i * (2 * quads) + q + 1)
                        for r in range(4):
                            n = q * 4 + r
                            dve.tensor_scalar(hot2[:, s, r, :], iota[:, :], stage[:, 1, n:n + 1], None, ALU.is_equal)
                            ins = dve.tensor_scalar(hot1[:, s, r, :], iota[:, :], stage[:, 0, n:n + 1], stage[:, 2, n:n + 1],
                                                    ALU.is_equal, ALU.mult)
                        ins.then_inc(hots_ready, 1)
                    dve.wait_ge(hots_ready, i * (2 * quads) + 2 * quads)

            @block.tensor
            def _(pe):
                pe.sem_inc(hots_used, 2)
                with pe.Fori(0, turns) as i:
                    for q in range(2 * quads):
                        s = q % 2
                        pe.wait_ge(hots_ready, i * (2 * quads) + q + 1)
                        pe.wait_ge(gm_taken, i * (2 * quads) + q + 1)
                        for r in range(4):
                            ins = pe.matmul(ps[:, q % 8, r * P:(r + 1) * P], hot2[:, s, r, :], hot1[:, s, r, :], start=True, stop=True)
                        ins.then_inc(hots_used, 1)

            @block.scalar
            def _(act):
                act.sem_inc(gm_taken, 8)
                act.sem_inc(gm_stored[0], 16)
                act.sem_inc(gm_stored[1], 16)
                with act.Fori(0, turns) as i:
                    for b in range(2):
                        act.wait_ge(gm_stored[b], i * 16 + 16)
                        for q in range(quads):
                            n = b * quads + q
                            act.wait_ge(hots_used, i * (2 * quads) + n + 3)
                            act.activation(gmat[:, b, :, q * 4:(q + 1) * 4], ps[:, n % 8, :].rearrange("p (t k) -> p k t", t=4),
                                           ACT.Copy).then_inc(gm_taken, 1)

    u_in = [K.sem(f"u_in{i}") for i in range(NG)]
    v_in = [K.sem(f"v_in{i}") for i in range(2)]
    g_in = [K.sem(f"g_in{i}") for i in range(2)]
    u_used = K.sem("u_used")
    h_act = K.sem("h_act")
    a_ready = K.sem("a_ready")
    o2_psum = K.sem("o2_psum")
    y_added = K.sem("y_added")
    f_chain = K.sem("f_chain")

    def experts(l):
        with nc.Block() as block:
            @block.sync
            def _(sp):
                gd = gates_dram.rearrange("b p (k t) -> p b k t", t=GB)
                with sp.Fori(0, GROUPS // 2) as i:
                    for p in range(2):
                        g = i * 2 + p
                        for j in range(NG):
                            sp.wait_ge(u_used, g * NG + j + 1)
                            sp.dma_start(ut[:, j, :, :], a["u"][l, g * NG + j]).then_inc(u_in[j], 16)
                        sp.wait_ge(a_ready, g * NG + NG)
                        sp.dma_start(gt[:, p, :, :, :].rearrange("p b k t -> p b (k t)"),
                                     gates_dram[:, :, bass.ds(g * (NG * GB), NG * GB)].rearrange("b p n -> p b n")).then_inc(g_in[p], 16)
                        sp.wait_ge(o2_psum, g * (2 * NT) + 2 * NT)
                        sp.dma_start(vt[:, p, :, :], a["v"][l, bass.ds(g * NG, NG)].rearrange("k p d -> p k d")).then_inc(v_in[p], 16)

            @block.tensor
            def _(pe):
                pe.sem_inc(u_used, NG)
                pe.sem_inc(o2_psum, 4 * NT)

                def hidden(g, p):
                    for j in range(NG):
                        pe.wait_ge(u_in[j], g * 16 + 16)
                        if not (isinstance(g, int) and g == 0 and j < 2):
                            pe.wait_ge(a_ready, g * NG + j - 1 + 2 * NG)
                        for half in range(2):
                            for k in range(KD):
                                ins = pe.matmul(ps[:, 2 * (j % 2) + half, 0:HALF], ut[:, j, k, :],
                                                hT[:, k, half * HALF:(half + 1) * HALF], start=(k == 0), stop=(k == KD - 1))
                        ins.then_inc(u_used, 1)

                def outputs(i, g, p):
                    pe.wait_ge(v_in[p], i * 16 + 16)
                    pe.wait_ge(a_ready, g * NG + NG + 2 * NG)
                    for c in range(2 * NT):
                        t, half = c // 2, c % 2
                        pe.wait_ge(y_added, g * (2 * NT) + c + 1)
                        for j in range(NG):
                            ins = pe.matmul(ps[:, 4 + (2 * p + c) % 4, :], at[:, p, j, t * P:(t + 1) * P],
                                            vt[:, p, j, half * 512:(half + 1) * 512], start=(j == 0), stop=(j == NG - 1))
                        ins.then_inc(o2_psum, 1)

                hidden(0, 0)
                with pe.Fori(0, GROUPS // 2 - 1) as i:
                    hidden(i * 2 + 1, 1)
                    outputs(i, i * 2, 0)
                    hidden(i * 2 + 2, 0)
                    outputs(i, i * 2 + 1, 1)
                hidden(GROUPS - 1, 1)
                outputs(GROUPS // 2 - 1, GROUPS - 2, 0)
                outputs(GROUPS // 2 - 1, GROUPS - 1, 1)

            @block.scalar
            def _(act):
                with act.Fori(0, GROUPS) as g:
                    for j in range(NG):
                        act.wait_ge(u_used, g * NG + j + 1 + NG)
                        act.activation(ps[:, 2 * (j % 2):2 * (j % 2) + 2, 0:HALF], ps[:, 2 * (j % 2):2 * (j % 2) + 2, 0:HALF],
                                       ACT.Gelu_apprx_tanh).then_inc(h_act, 1)

            @block.vector
            def _(dve):
                link = chain_of(dve, f_chain)
                link(dve.memset(y[:, :, :], 0.0))
                dve.sem_inc(y_added, 4)
                dve.sem_inc(a_ready, 2 * NG)

                def gated(i, g, p):
                    dve.wait_ge(g_in[p], i * 16 + 16)
                    dve.wait_ge(o2_psum, g * (2 * NT) + 2 * NT)
                    for j in range(NG):
                        dve.wait_ge(h_act, g * NG + j + 1)
                        for half in range(2):
                            ins = dve.tensor_tensor(
                                at[:, p, j, half * HALF:(half + 1) * HALF].rearrange("p (b t) -> p b t", t=GB),
                                ps[:, 2 * (j % 2) + half, 0:HALF].rearrange("p (b t) -> p b t", t=GB),
                                gt[:, p, half * (NB // 2):(half + 1) * (NB // 2), j, :], ALU.mult)
                        ins.then_inc(a_ready, 1)

                def added(g, p):
                    for c in range(2 * NT):
                        t, half = c // 2, c % 2
                        dve.wait_ge(o2_psum, g * (2 * NT) + c + 1 + 4 * NT)
                        span = slice(half * 512, (half + 1) * 512)
                        dve.tensor_tensor(y[:, t, span], ps[:, 4 + (2 * p + c) % 4, :], y[:, t, span], ALU.add).then_inc(y_added, 1)

                def settled(g):
                    dve.wait_ge(y_added, g * (2 * NT) + 2 * NT + 4)

                gated(0, 0, 0)
                with dve.Fori(0, GROUPS // 2 - 1) as i:
                    gated(i, i * 2 + 1, 1)
                    added(i * 2, 0)
                    gated(i + 1, i * 2 + 2, 0)
                    settled(i * 2)
                    added(i * 2 + 1, 1)
                    settled(i * 2 + 1)
                gated(GROUPS // 2 - 1, GROUPS - 1, 1)
                added(GROUPS - 2, 0)
                settled(GROUPS - 2)
                added(GROUPS - 1, 1)
                settled(GROUPS - 1)
                for t in range(NT):
                    v = 0 if t == 0 else 1
                    ins = dve.tensor_tensor(y[:, t, :], y[:, t, :], gate_bc[:, 1, v, :], ALU.mult)
                link(ins)
                for t in range(NT):
                    dve.tensor_tensor(x[:, t, :], x[:, t, :], y[:, t, :], ALU.add)

    with nc.Fori(0, DEPTH) as l:
        layer(l)
        for s in K.sems:
            nc.gpsimd.sem_clear(s)
        nc.all_engine_barrier()

    fg = sb("fg", [P, D])
    f_load = K.nc.alloc_semaphore("f_load")
    f_sq = K.nc.alloc_semaphore("f_sq")
    f_norm = K.nc.alloc_semaphore("f_norm")
    f_out = K.nc.alloc_semaphore("f_out")
    with nc.Block() as block:
        @block.sync
        def _(sp):
            sp.dma_start(fg[:, :], a["final_g"].partition_broadcast(P)).then_inc(f_load, 16)
            for t in range(NT):
                sp.wait_ge(f_norm, t + 2)
                sp.dma_start(o["y"][t * P:(t + 1) * P, :], x[:, t, :]).then_inc(f_out, 16)
            sp.wait_ge(f_out, 16 * NT)

        @block.scalar
        def _(act):
            for t in range(NT):
                act.activation(xn[:, 0, :], x[:, t, :], ACT.Square, accum_out=ss[:, t:t + 1]).then_inc(f_sq, 1)
                act.wait_ge(f_sq, t + 1)
            act.activation(rstd[:, 0:NT], ss[:, 0:NT], ACT.Sqrt, bias=eps_col[:, 0:1], scale=1.0 / D).then_inc(f_sq, 1)

        @block.vector
        def _(dve):
            dve.wait_ge(f_sq, NT + 1)
            dve.wait_ge(f_load, 16)
            dve.reciprocal(rstd[:, 0:NT], rstd[:, 0:NT]).then_inc(f_norm, 1)
            dve.wait_ge(f_norm, 1)
            for t in range(NT):
                dve.scalar_tensor_tensor(x[:, t, :], x[:, t, :], rstd[:, t:t + 1], fg[:, :], ALU.mult,
                                         ALU.mult).then_inc(f_norm, 1)


ROPE_SWAP = np.r_[8:16, 0:8, 24:32, 16:24]


def constants():
    f = np.float32
    eye = np.eye(P, dtype=f)
    s, t = np.arange(P)[:, None], np.arange(P)[None, :]
    maskb = np.stack([np.where(s <= t, 0.0, MASKED), np.where(s >= t, 0.0, MASKED)], axis=1).astype(f)
    sel2 = np.zeros((2, 2, P), f)
    sel2[0, 0], sel2[1, 1] = 1.0, 1.0
    sel8 = np.zeros((ROWS, 8, P), f)
    for d in range(2):
        for h in range(H):
            sel8[32 * d + h, d * H + h] = 1.0
    grid_w, axis = 64, ROPE // 2
    freqs = (f(10000.0) ** (-np.arange(0, axis, 2, dtype=f) / f(axis))).astype(f)
    position = np.arange(NS * P)
    row, column = (position // grid_w).astype(f), (position % grid_w).astype(f)
    ang = np.concatenate([row[None] * freqs[:, None]] * 2 + [column[None] * freqs[:, None]] * 2).astype(f)
    sign = np.where(np.arange(ROPE) % axis < axis // 2, -1.0, 1.0).astype(f)[:, None]
    cos_sin = np.stack([np.cos(ang), np.sin(ang) * sign], axis=1).astype(f)
    bf16 = mybir.dt.np(BF16)
    return {
        "ident": eye, "maskb": maskb, "sel2": sel2, "sel8": sel8, "cos_sin": cos_sin,
        "iota": np.tile(np.arange(NKEYS, dtype=f), (P, 1)),
        "iota16": np.tile(np.arange(TOP, dtype=f), (P, 1)).astype(bf16),
    }


def blocks(w, width):
    n, d, c = w.shape
    return np.ascontiguousarray(w.reshape(n, d // P, P, c // width, width).transpose(0, 3, 2, 1, 4))


def rows_of(w, width):
    n, d, c = w.shape
    return np.ascontiguousarray(w.reshape(n, d // P, P, c).transpose(0, 2, 1, 3))


def lay_out(x_prompt, x_sample, c, cache_mla_ckv, cache_mla_krope, state_mlstm_C, state_mlstm_n, state_mlstm_m,
            c_ctx, norm1_g, ada_w, ada_b, w_in, mlstm_gate_b, cm_norm_g, cm_ws, cm_b, mla_q_norm_g, mla_w_uq,
            mla_kv_norm_g, mla_w_ukv, w_out, norm2_g, peer_w_q, peer_subkeys, peer_u, peer_v, final_g):
    f = np.float32
    L = DEPTH
    mq, mk, mv, mo = (w_in[..., i * 256:(i + 1) * 256] for i in range(4))
    g = w_in[..., 1024:1040]
    cu, cv, cq, ckv = (w_in[..., 1040 + i * 256:1040 + (i + 1) * 256] for i in range(4))
    kr = w_in[..., 2064:2096]
    w_small = np.zeros((L, D, SMALL), f)
    w_small[..., 0:4], w_small[..., 32:36] = g[..., 0:4], g[..., 8:12]
    w_small[..., 36:40], w_small[..., 68:72] = g[..., 4:8], g[..., 12:16]
    w_small[..., 72:104], w_small[..., 104:136] = kr, kr[..., ROPE_SWAP]
    gate_b = np.zeros((L, ROWS, 2), f)
    gate_b[:, 0:4, 0], gate_b[:, 32:36, 0] = mlstm_gate_b[:, 0:4], mlstm_gate_b[:, 8:12]
    gate_b[:, 0:4, 1], gate_b[:, 32:36, 1] = mlstm_gate_b[:, 4:8], mlstm_gate_b[:, 12:16]
    m0 = np.zeros((L, ROWS, 1), f)
    m0[:, 0:4, 0], m0[:, 32:36, 0] = state_mlstm_m[0, :, 0], state_mlstm_m[0, :, 1]
    cn0 = np.concatenate([state_mlstm_C[0], state_mlstm_n[0][..., None]], axis=-1)
    cn0 = cn0.reshape(L, 2, 2, 2, HD, HD + 1).transpose(0, 3, 4, 1, 2, 5).reshape(L, P, 2, 2, HD + 1)
    uq = mla_w_uq.reshape(L, 256, AH, QK)
    ukv = mla_w_ukv.reshape(L, 256, AH, 2 * HD)

    def halves(w):
        return np.ascontiguousarray(w.reshape(L, 2, P, -1).transpose(0, 2, 1, 3))

    return {
        "x": np.concatenate([x_prompt[0], x_sample[0]]),
        "cT": np.stack([c_ctx, c[0]]).reshape(2, KD, P).transpose(2, 1, 0),
        "normT": np.stack([norm1_g, norm2_g], axis=1).reshape(L, 2, KD, P).transpose(0, 3, 1, 2),
        "ada_w": blocks(ada_w, 512), "ada_b": ada_b.reshape(L, 12, 512),
        "w_in": blocks(np.concatenate([mk, mv, mo, cu, cv, cq, ckv, mq], axis=-1), 512),
        "w_small": rows_of(w_small, SMALL),
        "gate_b": gate_b, "m0": m0, "cn0": cn0,
        "wsT": cm_ws.transpose(0, 3, 1, 2), "cmb": cm_b.transpose(0, 2, 1),
        "normg": np.stack([cm_norm_g, mla_q_norm_g, mla_kv_norm_g], axis=1),
        "cacheT": cache_mla_ckv[0].transpose(0, 2, 1).reshape(L, 2, P, P).transpose(0, 2, 1, 3),
        "kr_cacheT": cache_mla_krope[0].transpose(0, 2, 1),
        "wuq": halves(mla_w_uq), "wqs": halves(uq[..., HD:][..., ROPE_SWAP]),
        "wuk": halves(ukv[..., :HD]), "wuv": halves(ukv[..., HD:]),
        "w_out": blocks(w_out, 512), "wq": blocks(peer_w_q, 512),
        "skT": peer_subkeys.transpose(0, 3, 1, 2),
        "u": peer_u.reshape(L, NKEYS, NKEYS, KD, P).transpose(0, 1, 4, 3, 2),
        "v": peer_v.reshape(L, NKEYS, NKEYS, D),
        "final_g": final_g,
        **constants(),
    }


OUTPUTS = {"y": (T, D), "ckv": (DEPTH, P, 256), "kr": (DEPTH, P, ROPE), "cn": (DEPTH, P, 2, 2, HD + 1),
           "m": (DEPTH, ROWS, 1)}


def kernel(**inputs):
    import concourse.bacc as bacc
    from concourse.bass_utils import run_bass_kernel_spmd

    nc = bacc.Bacc("TRN2", target_bir_lowering=False, num_devices=1)
    arrays = {f"in_{k}": np.ascontiguousarray(v) for k, v in lay_out(**{k: np.asarray(v) for k, v in inputs.items()}).items()}
    a = {k[3:]: nc.dram_tensor(k, v.shape, mybir.dt.from_np(v.dtype), kind="ExternalInput").ap() for k, v in arrays.items()}
    o = {k: nc.dram_tensor(f"out_{k}", v, F32, kind="ExternalOutput").ap() for k, v in OUTPUTS.items()}
    build_program(nc, a, o)
    r = run_bass_kernel_spmd(nc, [arrays], core_ids=[0]).results[0]
    cn = r["out_cn"].reshape(DEPTH, 2, HD, 2, 2, HD + 1).transpose(0, 3, 4, 1, 2, 5).reshape(DEPTH, 2, H, HD, HD + 1)
    m = r["out_m"][:, :, 0]
    m = np.stack([m[:, 0:4], m[:, 32:36]], axis=1)
    y = r["out_y"]
    return (y[None, :P], y[None, P:], r["out_ckv"][None], r["out_kr"][None],
            np.ascontiguousarray(cn[..., :HD])[None], np.ascontiguousarray(cn[..., HD])[None], m[None])
```

```python
import math
from contextlib import ExitStack

import numpy as np

import concourse.bass as bass
from concourse import mybir

F32 = mybir.dt.float32
F32R = mybir.dt.float32r
BF16 = mybir.dt.bfloat16
U32 = mybir.dt.uint32
ALU = mybir.AluOpType
ACT = mybir.ActivationFunctionType
AX = mybir.AxisListType

P = 128
D = 1024
KD = D // P
DEPTH = 2

NT = 5
T = NT * P
NS = 4
EPS = 1e-6
H = 4
HD = 64
AH = 8
ROPE = 32
QK = HD + ROPE
KT = NT + 1
SCALE = float(QK) ** -0.5
RH = 8
TOP = 16
SLOTS = RH * TOP
NKEYS = 128
MASKED = -1e30
ROWS = 36
GB = 64
NB = T // GB
NG = 4
GROUPS = NKEYS // NG
HALF = T // 2
MK, MV, MO, CU, CV, CQ, CKV = range(7)
SMALL = 2 * ROWS + 2 * ROPE
R_A, R_WK, R_WIN, R_EM = range(4)


def col(ap, n):
    return ap.unsqueeze(len(ap.shape)).to_broadcast(list(ap.shape) + [n])


class Kernel:
    def __init__(self, nc, a, o):
        self.nc, self.a, self.o = nc, a, o
        self.sems = []

    def sem(self, name):
        s = self.nc.alloc_semaphore(name)
        self.sems.append(s)
        return s


def chain_of(eng, sem):
    count = [0]

    def link(ins):
        count[0] += 1
        ins.then_inc(sem, 1)
        eng.wait_ge(sem, count[0])

    return link


def build_program(nc, a, o, upto=99):
    K = Kernel(nc, a, o)
    ctx = ExitStack()
    dbg = o.get("dbg")

    def sb(name, shape, dt=F32, stack=ctx):
        return stack.enter_context(nc.sbuf_tensor(name, shape, dt))

    x = sb("x", [P, NT, D])
    gate2 = sb("gate2", [P, 2, D])
    modT = sb("modT", [P, 4, KD, 2])
    ident = sb("ident", [P, P])
    ones_row = sb("ones_row", [1, P])
    sel2 = sb("sel2", [2, 2, P])
    cT = sb("cT", [P, KD, 2])
    rstd = sb("rstd", [P, 16])
    ss = sb("ss", [P, 16])
    eps_col = sb("eps_col", [P, 1])
    one_col = sb("one_col", [P, 1])
    ps = ctx.enter_context(nc.psum_tensor("ps", [P, 8, 512], F32))

    gates_dram = nc.dram_tensor("gates_dram", [NB, P, NKEYS * GB], F32, kind="Internal").ap()

    def normalise(act, dve, pe, which, start):
        psum_ready, hT_taken_act, hT_taken_dve = start["tp"], start["ta"], start["td"]
        sh, sc = 2 * which, 2 * which + 1
        hT, xn = start["hT"], start["x_n"]
        if act is not None:
            for t in range(NT):
                act.activation(xn[:, 1, :], x[:, t, :], ACT.Square,
                               accum_out=ss[:, t:t + 1]).then_inc(start["sq"], 1)
                act.wait_ge(start["sq"], t + 1)
            act.activation(rstd[:, 0:NT], ss[:, 0:NT], ACT.Sqrt, bias=eps_col[:, 0:1], scale=1.0 / D).then_inc(start["rt"], 1)
            if "mod" in start:
                act.wait_ge(start["mod"], 4)
            for t in range(NT):
                c = 0 if t == 0 else 1
                act.wait_ge(psum_ready, t + 1)
                for k in range(4):
                    ins = act.activation(hT[:, k, t * P:(t + 1) * P], ps[:, 4 + 2 * (t % 2), k * P:(k + 1) * P],
                                         ACT.Identity, bias=modT[:, sh, k, c:c + 1], scale=modT[:, sc, k, c:c + 1])
                ins.then_inc(hT_taken_act, 1)
        if dve is not None:
            link = start["link"]
            dve.wait_ge(start["rt"], 1)
            link(dve.reciprocal(rstd[:, 0:NT], rstd[:, 0:NT]))

            def scaled(t):
                if t >= 2:
                    dve.wait_ge(psum_ready, t - 1)
                dve.tensor_scalar(xn[:, t % 2, :], x[:, t, :], rstd[:, t:t + 1], None,
                                  ALU.mult).then_inc(start["xn"], 1)

            scaled(0)
            for t in range(NT):
                c = 0 if t == 0 else 1
                if t + 1 < NT:
                    scaled(t + 1)
                dve.wait_ge(psum_ready, t + 1)
                for k in range(4):
                    ins = dve.tensor_scalar(hT[:, 4 + k, t * P:(t + 1) * P],
                                            ps[:, 5 + 2 * (t % 2), k * P:(k + 1) * P],
                                            modT[:, sc, 4 + k, c:c + 1], modT[:, sh, 4 + k, c:c + 1],
                                            ALU.mult, ALU.add)
                ins.then_inc(hT_taken_dve, 1)
        if pe is not None:
            for t in range(NT):
                pe.wait_ge(start["xn"], t + 1)
                if t >= 2:
                    pe.wait_ge(hT_taken_act, t - 1)
                    pe.wait_ge(hT_taken_dve, t - 1)
                for k in range(KD):
                    ins = pe.transpose(ps[:, 4 + 2 * (t % 2) + k // 4, (k % 4) * P:(k % 4 + 1) * P],
                                       xn[:, t % 2, k * P:(k + 1) * P], ident[:, :])
                ins.then_inc(psum_ready, 1)

    load = K.nc.alloc_semaphore("first_loads")
    pre = K.nc.alloc_semaphore("first_constants")
    silu = K.nc.alloc_semaphore("silu_ready")
    with nc.Block() as block:
        @block.sync
        def _(sp):
            sp.dma_start(x[:, :, :], a["x"].rearrange("(t p) d -> p t d", p=P)).then_inc(load, 16)
            sp.dma_start(ident[:, :], a["ident"]).then_inc(load, 16)
            sp.dma_start(sel2[:, :, :], a["sel2"]).then_inc(load, 16)
            sp.dma_start(cT[:, :, :], a["cT"]).then_inc(load, 16)
            sp.wait_ge(load, 64)

        @block.vector
        def _(dve):
            dve.memset(ones_row[:, :], 1.0).then_inc(pre, 1)
            dve.memset(eps_col[:, :], EPS).then_inc(pre, 1)
            dve.memset(one_col[:, :], 1.0).then_inc(pre, 1)
            dve.wait_ge(pre, 3)

        @block.scalar
        def _(act):
            act.wait_ge(load, 64)
            act.activation(cT[:, :, :], cT[:, :, :], ACT.Silu).then_inc(silu, 1)
            act.wait_ge(silu, 1)

    mix_in = ctx.enter_context(ExitStack())

    def layer(l):
        project(l)
        if upto >= 2:
            mixers(l)
        if upto >= 4:
            retrieve(l)
        if upto >= 5:
            gate_matrices(l)
        if upto >= 6:
            experts(l)

    s1 = ExitStack()
    hT = sb("hT", [P, KD, T], stack=s1)
    xn = sb("xn", [P, 2, D], stack=s1)
    gate1 = sb("gate1", [P, 2, D], stack=s1)
    mixed = sb("mixed", [P, NT, D], stack=s1)
    cqT = sb("cqT", [P, 2, T], stack=s1)
    ckvT = sb("ckvT", [P, 2, KT * P], stack=s1)
    krT = sb("krT", [QK, KT * P], stack=s1)
    cos_sin = sb("cos_sin", [QK, 2, NS * P], stack=s1)
    s2 = ExitStack()
    proj = sb("proj", [P, NT, 7, 256], stack=s2)
    small = sb("small", [P, NT, SMALL], stack=s2)
    mqT = sb("mqT", [P, 2, T], stack=s2)
    s3 = ExitStack()
    wring = sb("wring", [P, 3, KD, 512], stack=s3)
    wsmall = sb("wsmall", [P, KD, SMALL], stack=s3)
    ada_rows = sb("ada_rows", [1, 2, 512], stack=s3)
    mod_row = sb("mod_row", [2, 2, 512], stack=s3)
    normT = sb("normT", [P, 2, KD], stack=s3)
    s3.close()
    s4 = ExitStack()
    mkT = sb("mkT", [P, 2, T], stack=s4)
    v1 = sb("v1", [P, NT, H, HD + 1], stack=s4)
    bwd = xn[:, :, :].rearrange("p a b -> p (a b)")[:, 0:NT * 256].rearrange("p (t e) -> p t e", t=NT)
    rowq = sb("rowq", [ROWS, 4, T], stack=s4)
    r_i, r_e, r_f = rowq[:, R_A, :], rowq[:, R_WK, :], rowq[:, R_WIN, :]
    r_b = sb("r_b", [ROWS, T], stack=s4)
    r_u = sb("r_u", [ROWS, T], stack=s4)
    r_prev = sb("r_prev", [ROWS, NT], stack=s4)
    r_end = sb("r_end", [ROWS, NT], stack=s4)
    r_dec = sb("r_dec", [ROWS, NT], stack=s4)
    r_m = sb("r_m", [ROWS, 1], stack=s4)
    gate_b = sb("gate_b", [ROWS, 2], stack=s4)
    m0 = sb("m0", [ROWS, 1], stack=s4)
    sel8 = sb("sel8", [ROWS, 8, P], stack=s4)
    maskb = sb("maskb", [P, 2, P], stack=s4)
    cols = sb("cols", [P, 4 * NT, ROWS], stack=s4)
    dec = sb("dec", [P, 8, NT], stack=s4)
    cn = sb("cn", [P, 2, 6, 2, HD + 1], stack=s4)
    wT = sb("wT", [P, 2, 512], stack=s4)
    swT = sb("swT", [P, 2, 512], stack=s4)
    kw = sb("kw", [P, 2, 256], stack=s4)
    nd = sb("nd", [P, H, HD + 1], stack=s4)
    dd = sb("dd", [P, 2, H], stack=s4)
    wsT = sb("wsT", [P, H, P], stack=s4)
    cmb = sb("cmb", [P, H], stack=s4)
    normg = sb("normg", [P, 3, 256], stack=s4)
    s4.close()
    s2.close()
    s5 = ExitStack()
    qT = sb("qT", [QK, AH, T], stack=s5)
    kT = sb("kT", [QK, AH, KT * P], stack=s5)
    val = sb("val", [P, KT, 512], stack=s5)
    prob = sb("prob", [P, 2, T], stack=s5)
    probT = sb("probT", [P, 2, T], stack=s5)
    wuq = sb("wuq", [P, 2, AH * QK], stack=s5)
    wqs = sb("wqs", [P, 2, AH * ROPE], stack=s5)
    wuk = sb("wuk", [P, 2, 512], stack=s5)
    wuv = sb("wuv", [P, 2, 512], stack=s5)
    rot = sb("rot", [QK, 2, 512], stack=s5)
    amax = sb("amax", [P, 2, 4], stack=s5)
    wout = sb("wout", [P, KD, 512], stack=s5)
    s5.close()
    s1.close()

    w_slot = [K.sem(f"w_slot{i}") for i in range(3)]
    w_free = K.sem("w_free")
    a_load = K.sem("a_load")
    ada_slot = [K.sem(f"ada_slot{i}") for i in range(2)]
    mod_psum = K.sem("mod_psum")
    mod_copied = K.sem("mod_copied")
    mod_spread = K.sem("mod_spread")
    mod_taken = K.sem("mod_taken")
    mod_final = K.sem("mod_final")
    n1 = dict(tp=K.sem("n1_psum"), ta=K.sem("n1_act"), td=K.sem("n1_dve"), sq=K.sem("n1_sq"), rt=K.sem("n1_root"),
              xn=K.sem("n1_xn"), mod=mod_final, hT=hT, x_n=xn)
    proj_psum = K.sem("proj_psum")
    proj_taken = K.sem("proj_taken")
    a_chain = K.sem("a_chain")

    def project(l):
        with nc.Block() as block:
            @block.sync
            def _(sp):
                sp.dma_start(normT[:, :, :], a["normT"][l]).then_inc(a_load, 16)
                sp.dma_start(wsmall[:, :, :], a["w_small"][l]).then_inc(a_load, 16)
                for j in range(16):
                    if 3 <= j < 15:
                        sp.wait_ge(w_free, j - 2)
                    if j == 15:
                        sp.wait_ge(proj_psum, NT)
                    src = a["ada_w"][l, j] if j < 12 else a["w_in"][l, j - 12]
                    sp.dma_start(wring[:, j % 3, :, :], src).then_inc(w_slot[j % 3], 16)
                    if j < 12:
                        if j >= 2:
                            sp.wait_ge(mod_psum, j - 1)
                        sp.dma_start(ada_rows[:, j % 2, :], a["ada_b"][l, j:j + 1, :]).then_inc(ada_slot[j % 2], 16)

            @block.tensor
            def _(pe):
                def mod(j):
                    pe.wait_ge(w_slot[j % 3], 16 * (j // 3 + 1))
                    pe.wait_ge(ada_slot[j % 2], 16 * (j // 2 + 1))
                    if j >= 2:
                        pe.wait_ge(mod_copied, j - 1)
                    for k in range(KD):
                        ins = pe.matmul(ps[0:2, j % 2, :], cT[:, k, :], wring[:, j % 3, k, :], start=(k == 0), stop=False)
                    ins.then_inc(w_free, 1)
                    pe.matmul(ps[0:2, j % 2, :], ones_row[:, 0:2], ada_rows[:, j % 2, :], start=False,
                              stop=True).then_inc(mod_psum, 1)

                def spread(j):
                    pe.wait_ge(mod_copied, j + 1)
                    if j >= 1:
                        pe.wait_ge(mod_taken, j)
                    if (j // 2) % 3 == 2:
                        for v in range(2):
                            ins = pe.matmul(ps[:, 3 + v, :], sel2[:, v, :], mod_row[:, j % 2, :], start=True, stop=True)
                    else:
                        for i in range(4):
                            ins = pe.transpose(ps[:, 2, 2 * i:2 * i + 2], mod_row[:, j % 2, i * P:(i + 1) * P], ident[0:2, 0:2])
                    ins.then_inc(mod_spread, 1)

                mod(0)
                for j in range(12):
                    if j + 1 < 12:
                        mod(j + 1)
                    spread(j)
                pe.wait_ge(mod_taken, 12)
                normalise(None, None, pe, 0, n1)
                pe.wait_ge(n1["ta"], NT)
                pe.wait_ge(n1["td"], NT)
                n = 0

                def bank_free():
                    if n >= 4:
                        pe.wait_ge(proj_taken, n - 3)

                for c in range(4):
                    pe.wait_ge(w_slot[(12 + c) % 3], 16 * ((12 + c) // 3 + 1))
                    for t in range(NT):
                        bank_free()
                        wide = 512 if c < 3 else 256
                        for k in range(KD):
                            ins = pe.matmul(ps[:, n % 4, 0:wide], hT[:, k, t * P:(t + 1) * P],
                                            wring[:, (12 + c) % 3, k, 0:wide], start=(k == 0), stop=(k == KD - 1))
                        ins.then_inc(proj_psum, 1)
                        n += 1
                for b in range(2):
                    for lo, wide in ((0, 512), (512, 128)):
                        bank_free()
                        for k in range(KD):
                            ins = pe.matmul(ps[:, n % 4, 0:wide], wring[:, 15 % 3, k, 256 + b * P:256 + (b + 1) * P],
                                            hT[:, k, lo:lo + wide], start=(k == 0), stop=(k == KD - 1))
                        ins.then_inc(proj_psum, 1)
                        n += 1
                pe.wait_ge(a_load, 32)
                for t in range(NT):
                    bank_free()
                    for k in range(KD):
                        ins = pe.matmul(ps[:, n % 4, 0:SMALL], hT[:, k, t * P:(t + 1) * P], wsmall[:, k, :],
                                        start=(k == 0), stop=(k == KD - 1))
                    ins.then_inc(proj_psum, 1)
                    n += 1

            @block.scalar
            def _(act):
                for j in range(12):
                    act.wait_ge(mod_psum, j + 1)
                    if j >= 2:
                        act.wait_ge(mod_spread, j - 1)
                    act.activation(mod_row[:, j % 2, :], ps[0:2, j % 2, :], ACT.Copy).then_inc(mod_copied, 1)
                normalise(act, None, None, 0, n1)
                n = 0
                for c in range(4):
                    for t in range(NT):
                        act.wait_ge(proj_psum, n + 1)
                        wide = 2 if c < 3 else 1
                        act.activation(proj[:, t, 2 * c:2 * c + wide, :],
                                       ps[:, n % 4, 0:wide * 256].rearrange("p (a b) -> p a b", a=wide),
                                       ACT.Copy).then_inc(proj_taken, 1)
                        n += 1
                for b in range(2):
                    for lo, wide in ((0, 512), (512, 128)):
                        act.wait_ge(proj_psum, n + 1)
                        act.activation(mqT[:, b, lo:lo + wide], ps[:, n % 4, 0:wide], ACT.Copy).then_inc(proj_taken, 1)
                        n += 1
                for t in range(NT):
                    act.wait_ge(proj_psum, n + 1)
                    act.activation(small[:, t, :], ps[:, n % 4, 0:SMALL], ACT.Copy).then_inc(proj_taken, 1)
                    n += 1
                act.wait_ge(proj_taken, n)

            @block.vector
            def _(dve):
                link = chain_of(dve, a_chain)
                for j in range(12):
                    dve.wait_ge(mod_spread, j + 1)
                    kind, half = j // 2, j % 2
                    if kind % 3 == 2:
                        for v in range(2):
                            ins = dve.tensor_copy((gate1, gate2)[kind // 3][:, v, half * 512:(half + 1) * 512], ps[:, 3 + v, :])
                    else:
                        which = kind if kind < 2 else kind - 1
                        ins = dve.tensor_copy(modT[:, which, half * 4:(half + 1) * 4, :],
                                              ps[:, 2, 0:8].rearrange("p (a b) -> p a b", b=2))
                    ins.then_inc(mod_taken, 1)
                dve.wait_ge(mod_taken, 12)
                dve.wait_ge(a_load, 32)
                for w in range(2):
                    for v in range(2):
                        dve.scalar_tensor_tensor(modT[:, 2 * w + 1, :, v], modT[:, 2 * w + 1, :, v], 1.0,
                                                 normT[:, w, :], ALU.add, ALU.mult).then_inc(mod_final, 1)
                dve.wait_ge(mod_final, 4)
                normalise(None, dve, None, 0, dict(n1, link=link))

    b_load = K.sem("b_load")
    b_out = K.sem("b_out")
    b_chain = K.sem("b_chain")
    sig_done = K.sem("sig_done")
    sq15 = K.sem("sq15")
    root15 = K.sem("root15")
    normed = K.sem("normed")
    kq_psum = K.sem("kq_psum")
    kq_taken = K.sem("kq_taken")
    row_psum = K.sem("row_psum")
    row_taken = K.sem("row_taken")
    lat_psum = K.sem("lat_psum")
    lat_taken = K.sem("lat_taken")
    sgu_psum = K.sem("sgu_psum")
    sgu_taken = K.sem("sgu_taken")
    nf_ready = K.sem("nf_ready")
    log_ready = K.sem("log_ready")
    rows_in = K.sem("rows_in")
    rows_exp = K.sem("rows_exp")
    cols_psum = K.sem("cols_psum")
    cols_taken = K.sem("cols_taken")
    w_psum = K.sem("w_psum")
    w_exp = K.sem("w_exp")
    st_psum = K.sem("st_psum")
    sw_ready = K.sem("sw_ready")
    kw_ready = K.sem("kw_ready")
    nd_psum = K.sem("nd_psum")
    nd_taken = K.sem("nd_taken")
    c_psum = K.sem("c_psum")
    c_ready = K.sem("c_ready")
    v1_ready = K.sem("v1_ready")
    done_b = K.sem("done_b")

    def mixers(l):
        with nc.Block() as block:
            @block.sync
            def _(sp):
                loads = [(gate_b[:, :], a["gate_b"][l]), (m0[:, :], a["m0"][l]), (sel8[:, :, :], a["sel8"]),
                         (maskb[:, :, :], a["maskb"]), (wsT[:, :, :], a["wsT"][l]), (cmb[:, :], a["cmb"][l]),
                         (normg[:, :, :], a["normg"][l].partition_broadcast(P)), (cn[:, :, 1, :, :], a["cn0"][l]),
                         (ckvT[:, :, P:2 * P], a["cacheT"][l]), (krT[HD:QK, P:2 * P], a["kr_cacheT"][l]),
                         (cos_sin[HD:QK, :, :], a["cos_sin"])]
                for dst, src in loads:
                    sp.dma_start(dst, src).then_inc(b_load, 16)
                sp.wait_ge(b_load, 16 * 11)
                sp.wait_ge(normed, NT)
                sp.dma_start(o["ckv"][l], proj[:, 0, CKV, :]).then_inc(b_out, 16)
                sp.dma_start(o["kr"][l], small[:, 0, 2 * ROWS:2 * ROWS + ROPE]).then_inc(b_out, 16)
                sp.wait_ge(c_ready, 2 * 1)
                sp.dma_start(o["cn"][l], cn[:, :, 5, :, :]).then_inc(b_out, 16)
                sp.dma_start(o["m"][l], r_m[:, :]).then_inc(b_out, 16)
                sp.wait_ge(b_out, 64)

            @block.tensor
            def _(pe):
                pe.wait_ge(b_load, 16 * 11)
                for t in range(NT):
                    b = 2 * (t % 2)
                    if t >= 2:
                        pe.wait_ge(kq_taken, t - 1)
                        pe.wait_ge(row_taken, t - 1)
                    pe.transpose(ps[:, b, 0:P], proj[:, t, MK, 0:P], ident[:, :])
                    pe.transpose(ps[:, b, P:2 * P], proj[:, t, MK, P:2 * P], ident[:, :]).then_inc(kq_psum, 1)
                    pe.transpose(ps[0:ROWS, b + 1, 0:P], small[:, t, 0:ROWS], ident[:, :])
                    pe.transpose(ps[0:ROWS, b + 1, P:2 * P], small[:, t, ROWS:2 * ROWS], ident[:, :])
                    pe.transpose(ps[0:QK, b + 1, 2 * P:3 * P], small[:, t, 8:8 + QK], ident[:, :])
                    pe.transpose(ps[0:QK, b + 1, 3 * P:4 * P], small[:, t, 8 + ROPE:8 + ROPE + QK],
                                 ident[:, :]).then_inc(row_psum, 1)
                for t in range(NT):
                    pe.wait_ge(normed, t + 1)
                    if t >= 2:
                        pe.wait_ge(lat_taken, t - 1)
                    for i, (c, h) in enumerate(((CQ, 0), (CQ, 1), (CKV, 0), (CKV, 1))):
                        ins = pe.transpose(ps[:, 4 + t % 2, i * P:(i + 1) * P], proj[:, t, c, h * P:(h + 1) * P], ident[:, :])
                    ins.then_inc(lat_psum, 1)
                for t in range(NT):
                    if t >= 2:
                        pe.wait_ge(sgu_taken, t - 1)
                    for g in range(H):
                        ins = pe.matmul(ps[:, 6 + t % 2, g * HD:(g + 1) * HD], wsT[:, g, :],
                                        proj[:, t, CV, g * HD:(g + 1) * HD], start=True, stop=True)
                    ins.then_inc(sgu_psum, 1)
                pe.wait_ge(kq_taken, NT)
                pe.wait_ge(row_taken, NT)
                pe.wait_ge(rows_exp, 2)
                for q in range(4):
                    for t in range(NT):
                        at = ((q % 2) * NT + t) * ROWS
                        pe.transpose(ps[:, q // 2, at:at + ROWS], rowq[:, q, t * P:(t + 1) * P], ident[0:ROWS, 0:ROWS])
                for r in range(8):
                    ins = pe.matmul(ps[:, 2, r * NT:(r + 1) * NT], sel8[:, r, :], r_dec[:, :], start=True, stop=True)
                ins.then_inc(cols_psum, 1)
                pe.wait_ge(cols_taken, 1)
                pe.wait_ge(v1_ready, 2)
                pe.wait_ge(lat_taken, NT)
                pe.wait_ge(sgu_taken, NT)

                def tile(n):
                    s, d = n // 2, n % 2
                    return s if d == 0 else (NT - s) % NT

                def weights_and_scores(n):
                    t, d = tile(n), n % 2
                    span = slice(t * P, (t + 1) * P)
                    if n >= 2:
                        pe.wait_ge(w_exp, n - 1)
                    for m in range(H):
                        h = (m % 2) * 2 + m // 2
                        at_m = ps[:, d, m * P:(m + 1) * P]
                        pe.matmul(at_m, ident[:, :], maskb[:, d, :], start=True, stop=False)
                        ins = pe.matmul(at_m, sel8[:, d * H + h, :], r_u[:, span], start=False, stop=True)
                    ins.then_inc(w_psum, 1)
                    if n >= 1:
                        pe.wait_ge(sw_ready, n)
                    for m in range(H):
                        hp, hh = m // 2, m % 2
                        part = slice(hp * HD, (hp + 1) * HD)
                        ins = pe.matmul(ps[:, 2 + hp, hh * P:(hh + 1) * P], mkT[part, hh, span], mqT[part, hh, span],
                                        start=True, stop=True)
                    ins.then_inc(st_psum, 1)

                weights_and_scores(0)
                for n in range(2 * NT):
                    s, d, t = n // 2, n % 2, tile(n)
                    span = slice(t * P, (t + 1) * P)
                    if n + 1 < 2 * NT:
                        weights_and_scores(n + 1)
                    pe.wait_ge(sw_ready, n + 1)
                    if n >= 1:
                        pe.wait_ge(nd_taken, n)
                    if s >= 2:
                        pe.wait_ge(c_ready, n - 1)
                    for m in range(H):
                        hp, hh = m // 2, m % 2
                        h = hh * 2 + hp
                        part = slice(hp * HD, (hp + 1) * HD)
                        pe.matmul(ps[:, 4, h * (HD + 1):(h + 1) * (HD + 1)], swT[:, d, m * P:(m + 1) * P],
                                  v1[:, t, h, :], start=True, stop=True)
                    for m in range(H):
                        hp, hh = m // 2, m % 2
                        part = slice(hp * HD, (hp + 1) * HD)
                        ins = pe.matmul(ps[:, 5 + hp, hh * (HD + 1):(hh + 1) * (HD + 1)], mqT[part, hh, span],
                                        cn[part, d, s, hh, :], start=True, stop=True)
                    ins.then_inc(nd_psum, 1)
                    if s < NT - 1:
                        pe.wait_ge(kw_ready, n + 1)
                        if n >= 1:
                            pe.wait_ge(c_ready, n)
                        for m in range(H):
                            hp, hh = m // 2, m % 2
                            h = hh * 2 + hp
                            ins = pe.matmul(ps[hp * HD:(hp + 1) * HD, 7, hh * (HD + 1):(hh + 1) * (HD + 1)],
                                            kw[:, d, h * HD:(h + 1) * HD], v1[:, t, h, :], start=True, stop=True)
                        ins.then_inc(c_psum, 1)

            @block.scalar
            def _(act):
                act.activation(proj[:, :, MO, :], proj[:, :, MO, :], ACT.Sigmoid).then_inc(sig_done, 1)
                for t in range(NT):
                    ins = act.activation(v1[:, t, :, 0:HD], proj[:, t, MV, :].rearrange("p (h e) -> p h e", h=H), ACT.Copy)
                ins.then_inc(v1_ready, 1)
                for t in range(NT):
                    for i, c in enumerate((CV, CQ, CKV)):
                        act.activation(nd[:, :, 0:HD], proj[:, t, c, :].rearrange("p (h e) -> p h e", h=H), ACT.Square,
                                       accum_out=ss[:, 3 * t + i:3 * t + i + 1]).then_inc(sq15, 1)
                        act.wait_ge(sq15, 3 * t + i + 1)
                act.activation(rstd[:, 0:15], ss[:, 0:15], ACT.Sqrt, bias=eps_col[:, 0:1], scale=1.0 / 256).then_inc(root15, 1)
                for t in range(NT):
                    act.wait_ge(kq_psum, t + 1)
                    act.activation(mkT[:, :, t * P:(t + 1) * P], ps[:, 2 * (t % 2), 0:2 * P].rearrange("p (a b) -> p a b", a=2),
                                   ACT.Copy).then_inc(kq_taken, 1)
                act.wait_ge(nf_ready, 1)
                act.activation(r_e[:, :], r_e[:, :], ACT.Exp).then_inc(log_ready, 1)
                act.wait_ge(log_ready, 1)
                act.activation(r_e[:, :], r_e[:, :], ACT.Ln, bias=1.0).then_inc(log_ready, 1)
                act.wait_ge(b_load, 16 * 11)
                for t in range(NT):
                    act.wait_ge(lat_psum, t + 1)
                    kt = 0 if t == 0 else t + 1
                    act.activation(cqT[:, :, t * P:(t + 1) * P], ps[:, 4 + t % 2, 0:2 * P].rearrange("p (a b) -> p a b", a=2), ACT.Copy)
                    act.activation(ckvT[:, :, kt * P:(kt + 1) * P],
                                   ps[:, 4 + t % 2, 2 * P:4 * P].rearrange("p (a b) -> p a b", a=2),
                                   ACT.Copy).then_inc(lat_taken, 1)
                act.wait_ge(rows_in, 1)
                act.activation(rowq[:, 1:4, :], rowq[:, 1:4, :], ACT.Exp).then_inc(rows_exp, 1)
                act.activation(r_dec[:, :], r_dec[:, :], ACT.Exp).then_inc(rows_exp, 1)
                act.wait_ge(cols_taken, 1)
                for n in range(2 * NT):
                    s, d = n // 2, n % 2
                    t = s if d == 0 else (NT - s) % NT
                    act.wait_ge(w_psum, n + 1)
                    if n >= 2:
                        act.wait_ge(sw_ready, n - 1)
                    for m in range(H):
                        h = (m % 2) * 2 + m // 2
                        ins = act.activation(wT[:, d, m * P:(m + 1) * P], ps[:, d, m * P:(m + 1) * P], ACT.Exp,
                                             bias=cols[:, R_A * NT + t, 32 * d + h:32 * d + h + 1])
                    ins.then_inc(w_exp, 1)

            @block.vector
            def _(dve):
                link = chain_of(dve, b_chain)
                dve.memset(v1[:, :, :, HD:HD + 1], 1.0).then_inc(v1_ready, 1)
                dve.memset(cn[:, :, 0, :, :], 0.0)
                dve.memset(r_b[:, :], 0.0)
                dve.memset(r_u[:, :], 0.0)
                dve.memset(r_prev[:, :], 0.0)
                dve.memset(r_end[:, :], 0.0)
                link(dve.memset(r_m[:, :], 0.0))
                dve.wait_ge(b_load, 16 * 11)
                for t in range(NT):
                    b = 2 * (t % 2) + 1
                    span = slice(t * P, (t + 1) * P)
                    dve.wait_ge(row_psum, t + 1)
                    dve.tensor_scalar(r_i[:, span], ps[0:ROWS, b, 0:P], gate_b[:, 0:1], None, ALU.add)
                    link(dve.tensor_scalar(r_f[:, span], ps[0:ROWS, b, P:2 * P], gate_b[:, 1:2], None, ALU.add))
                    if t == 0:
                        link(dve.tensor_copy(krT[HD:QK, 0:P], ps[HD:QK, b, 2 * P:3 * P]))
                    else:
                        pos = slice((t - 1) * P, t * P)
                        key = slice((t + 1) * P, (t + 2) * P)
                        link(dve.tensor_tensor(krT[HD:QK, key], ps[HD:QK, b, 2 * P:3 * P], cos_sin[HD:QK, 0, pos], ALU.mult))
                        link(dve.tensor_tensor(xn[HD:QK, 1, 0:P], ps[HD:QK, b, 3 * P:4 * P], cos_sin[HD:QK, 1, pos], ALU.mult))
                        link(dve.tensor_tensor(krT[HD:QK, key], krT[HD:QK, key], xn[HD:QK, 1, 0:P], ALU.add))
                    dve.sem_inc(row_taken, 1)
                dve.scalar_tensor_tensor(r_e[:, :], r_f[:, :], -1.0, r_f[:, :], ALU.mult, ALU.min).then_inc(nf_ready, 1)
                dve.wait_ge(root15, 1)
                link(dve.reciprocal(rstd[:, 0:15], rstd[:, 0:15]))
                for t in range(NT):
                    for i, c in enumerate((CV, CQ, CKV)):
                        ins = dve.scalar_tensor_tensor(proj[:, t, c, :], proj[:, t, c, :], rstd[:, 3 * t + i:3 * t + i + 1],
                                                       normg[:, i, :], ALU.mult, ALU.mult)
                    ins.then_inc(normed, 1)
                dve.wait_ge(log_ready, 2)
                link(dve.scalar_tensor_tensor(r_f[:, :], r_f[:, :], 0.0, r_e[:, :], ALU.min, ALU.subtract))
                fwd, bwd_rows = slice(0, H), slice(32, 32 + H)
                for lo, hi in ((0, P), (P, T)):
                    dve.tensor_tensor_scan(r_b[fwd, lo:hi], one_col[fwd, :].to_broadcast([H, hi - lo]), r_f[fwd, lo:hi], 0.0, ALU.mult, ALU.add)
                    rv = slice(hi - 1, lo - 1 if lo else None, -1)
                    link(dve.tensor_tensor_scan(r_b[bwd_rows, rv], one_col[bwd_rows, :].to_broadcast([H, hi - lo]), r_f[bwd_rows, rv], 0.0,
                                                ALU.mult, ALU.add))
                link(dve.tensor_tensor(rowq[:, R_A, :], r_i[:, :], r_b[:, :], ALU.subtract))
                for lo, hi in ((0, P), (P, T)):
                    rv = slice(hi - 1, lo - 1 if lo else None, -1)
                    dve.tensor_tensor_scan(r_u[fwd, lo:hi], rowq[fwd, R_A, lo:hi], rowq[fwd, R_A, lo:hi],
                                           m0[fwd, 0:1] if lo else 0.0, ALU.max, ALU.max)
                    link(dve.tensor_tensor_scan(r_u[bwd_rows, rv], rowq[bwd_rows, R_A, rv], rowq[bwd_rows, R_A, rv],
                                                m0[bwd_rows, 0:1] if lo else 0.0, ALU.max, ALU.max))
                dve.tensor_copy(r_prev[fwd, 1:2], m0[fwd, :])
                dve.tensor_copy(r_prev[fwd, 2:NT], r_u[fwd, 2 * P - 1:T - P:P])
                dve.tensor_copy(r_end[fwd, :], r_u[fwd, P - 1:T:P])
                dve.tensor_copy(r_prev[bwd_rows, NT - 1:NT], m0[bwd_rows, :])
                dve.tensor_copy(r_prev[bwd_rows, 1:NT - 1], r_u[bwd_rows, 2 * P:T:P])
                dve.tensor_copy(r_end[bwd_rows, :], r_u[bwd_rows, 0:T:P])
                dve.tensor_tensor(r_m[fwd, :], r_b[fwd, P - 1:P], r_u[fwd, P - 1:P], ALU.add)
                link(dve.tensor_tensor(r_m[bwd_rows, :], r_b[bwd_rows, 0:1], r_u[bwd_rows, 0:1], ALU.add))

                def tiles(ap):
                    return ap.rearrange("p (t s) -> p t s", t=NT)

                dve.tensor_tensor(tiles(rowq[:, R_WK, :]), tiles(rowq[:, R_A, :]), col(r_end[:, :], P), ALU.subtract)
                dve.tensor_tensor(tiles(rowq[:, R_WIN, :]), col(r_prev[:, :], P), tiles(r_u[:, :]), ALU.subtract)
                dve.scalar_tensor_tensor(rowq[:, R_EM, :], r_b[:, :], -1.0, r_u[:, :], ALU.mult, ALU.subtract)
                link(dve.tensor_tensor(r_dec[:, :], r_prev[:, :], r_end[:, :], ALU.subtract))
                link(dve.tensor_scalar(r_u[:, :], r_u[:, :], -1.0, None, ALU.mult))
                dve.sem_inc(rows_in, 1)
                for t in range(NT):
                    dve.wait_ge(sgu_psum, t + 1)
                    for g in range(H):
                        span = slice(g * HD, (g + 1) * HD)
                        ins = dve.scalar_tensor_tensor(mixed[:, t, 256 + g * HD:256 + (g + 1) * HD], ps[:, 6 + t % 2, span],
                                                       cmb[:, g:g + 1], proj[:, t, CU, span], ALU.add, ALU.mult)
                    ins.then_inc(sgu_taken, 1)
                dve.wait_ge(cols_psum, 1)
                link(dve.tensor_copy(cols[:, 0:2 * NT, :], ps[:, 0, 0:2 * NT * ROWS].rearrange("p (a b) -> p a b", b=ROWS)))
                link(dve.tensor_copy(cols[:, 2 * NT:, :], ps[:, 1, 0:2 * NT * ROWS].rearrange("p (a b) -> p a b", b=ROWS)))
                link(dve.tensor_copy(dec[:, :, :], ps[:, 2, 0:8 * NT].rearrange("p (a b) -> p a b", b=NT)))
                dve.sem_inc(cols_taken, 1)
                for n in range(2 * NT):
                    s, d = n // 2, n % 2
                    t = s if d == 0 else (NT - s) % NT
                    dve.wait_ge(w_exp, n + 1)
                    dve.wait_ge(st_psum, n + 1)
                    if n >= 2:
                        dve.wait_ge(nd_psum, n - 1)
                    pair = lambda ap: ap.rearrange("p (a b) -> p a b", a=2)
                    dve.scalar_tensor_tensor(pair(swT[:, d, :]), ps[:, 2:4, 0:2 * P], HD ** -0.5, pair(wT[:, d, :]),
                                             ALU.mult, ALU.mult).then_inc(sw_ready, 1)
                    heads = lambda ap: ap.rearrange("p (h e) -> p h e", h=H)
                    if s < NT - 1:
                        if n >= 2:
                            dve.wait_ge(c_psum, n - 1)
                        dve.scalar_tensor_tensor(heads(kw[:, d, :]), heads(proj[:, t, MK, :]), HD ** -0.5,
                                                 col(cols[:, R_WK * NT + t, 32 * d:32 * d + H], HD), ALU.mult,
                                                 ALU.mult).then_inc(kw_ready, 1)
                    dve.wait_ge(nd_psum, n + 1)
                    win = cols[:, R_WIN * NT + t, 32 * d:32 * d + H].rearrange("p (b a) -> p a b", a=2)
                    link(dve.tensor_tensor(nd[:, :, :].rearrange("p (b a) e -> p a b e", a=2),
                                           ps[:, 5:7, 0:2 * (HD + 1)].rearrange("p a (b e) -> p a b e", b=2),
                                           col(win, HD + 1), ALU.mult))
                    link(dve.tensor_tensor(nd[:, :, :], ps[:, 4, 0:H * (HD + 1)].rearrange("p (h e) -> p h e", h=H),
                                           nd[:, :, :], ALU.add))
                    dve.sem_inc(nd_taken, 1)
                    link(dve.scalar_tensor_tensor(dd[:, 0, :], nd[:, :, HD], -1.0, nd[:, :, HD], ALU.mult, ALU.max))
                    link(dve.tensor_tensor(dd[:, 1, :], dd[:, 0, :], cols[:, R_EM * NT + t, 32 * d:32 * d + H], ALU.max))
                    link(dve.reciprocal(dd[:, 0, :], dd[:, 1, :]))
                    out = mixed[:, t, 0:256] if d == 0 else bwd[:, t, :]
                    link(dve.tensor_tensor(heads(out), nd[:, :, 0:HD], col(dd[:, 0, :], HD), ALU.mult))
                    if s < NT - 1:
                        dve.wait_ge(c_psum, n + 1)
                        to = 5 if s == 0 else s + 1
                        for m in range(H):
                            hp, hh = m // 2, m % 2
                            h = hh * 2 + hp
                            part = slice(hp * HD, (hp + 1) * HD)
                            ins = dve.scalar_tensor_tensor(cn[part, d, to, hh, :], cn[part, d, s, hh, :],
                                                           dec[part, d * H + h, t:t + 1],
                                                           ps[part, 7, hh * (HD + 1):(hh + 1) * (HD + 1)], ALU.mult, ALU.add)
                        ins.then_inc(c_ready, 1)
                link(dve.tensor_tensor(mixed[:, :, 0:256], mixed[:, :, 0:256], bwd[:, :, :], ALU.add))
                dve.wait_ge(sig_done, 1)
                link(dve.tensor_tensor(mixed[:, :, 0:256], mixed[:, :, 0:256], proj[:, :, MO, :], ALU.mult))

        if upto >= 3:
            attention(l)

    c_load = K.sem("c_load")
    wout_slot = K.sem("wout_slot")
    q_psum = K.sem("q_psum")
    q_act = K.sem("q_act")
    q_dve = K.sem("q_dve")
    k_psum = K.sem("k_psum")
    k_act = K.sem("k_act")
    kr_ready = K.sem("kr_ready")
    v_psum = K.sem("v_psum")
    v_dve = K.sem("v_dve")
    s_psum = K.sem("s_psum")
    max_ready = K.sem("max_ready")
    p_ready = K.sem("p_ready")
    pt_psum = K.sem("pt_psum")
    pt_taken = K.sem("pt_taken")
    o_psum = K.sem("o_psum")
    o_taken = K.sem("o_taken")
    mt_psum = K.sem("mt_psum")
    mt_taken = K.sem("mt_taken")
    y_psum = K.sem("y_psum")
    y_taken = K.sem("y_taken")
    c_chain = K.sem("c_chain")

    def attention(l):
        units = [(h, t) for h in range(AH) for t in range(NT)]

        def keys(t):
            return (0, P, [0]) if t == 0 else (P, KT * P, list(range(1, KT)))

        with nc.Block() as block:
            @block.sync
            def _(sp):
                sp.dma_start(wuq[:, :, :], a["wuq"][l]).then_inc(c_load, 16)
                sp.dma_start(wqs[:, :, :], a["wqs"][l]).then_inc(c_load, 16)
                sp.dma_start(wuk[:, :, :], a["wuk"][l]).then_inc(c_load, 16)
                sp.dma_start(wuv[:, :, :], a["wuv"][l]).then_inc(c_load, 16)
                sp.dma_start(wout[:, :, :], a["w_out"][l, 0]).then_inc(wout_slot, 16)
                sp.wait_ge(y_psum, NT)
                sp.dma_start(wout[:, :, :], a["w_out"][l, 1]).then_inc(wout_slot, 16)

            @block.tensor
            def _(pe):
                pe.wait_ge(c_load, 64)
                for h in range(AH):
                    b = 3 * (h % 2)
                    if h >= 2:
                        pe.wait_ge(q_act, h - 1)
                        pe.wait_ge(q_dve, h - 1)
                    for k in range(2):
                        pe.matmul(ps[0:QK, b, :], wuq[:, k, h * QK:(h + 1) * QK], cqT[:, k, P:T], start=(k == 0), stop=(k == 1))
                    for k in range(2):
                        pe.matmul(ps[0:QK, b + 1, 0:P], wuq[:, k, h * QK:(h + 1) * QK], cqT[:, k, 0:P], start=(k == 0), stop=(k == 1))
                    for k in range(2):
                        ins = pe.matmul(ps[HD:QK, b + 2, :], wqs[:, k, h * ROPE:(h + 1) * ROPE], cqT[:, k, P:T],
                                        start=(k == 0), stop=(k == 1))
                    ins.then_inc(q_psum, 1)
                pe.wait_ge(q_act, AH)
                pe.wait_ge(q_dve, AH)
                for h in range(AH):
                    b = 2 * (h % 2)
                    if h >= 2:
                        pe.wait_ge(k_act, h - 1)
                    for k in range(2):
                        pe.matmul(ps[0:HD, b, :], wuk[:, k, h * HD:(h + 1) * HD], ckvT[:, k, 0:512], start=(k == 0), stop=(k == 1))
                    for k in range(2):
                        ins = pe.matmul(ps[0:HD, b + 1, 0:256], wuk[:, k, h * HD:(h + 1) * HD], ckvT[:, k, 512:768],
                                        start=(k == 0), stop=(k == 1))
                    ins.then_inc(k_psum, 1)
                for t in range(KT):
                    if t >= 2:
                        pe.wait_ge(v_dve, t - 1)
                    for k in range(2):
                        ins = pe.matmul(ps[:, 4 + t % 2, :], ckvT[:, k, t * P:(t + 1) * P], wuv[:, k, :], start=(k == 0), stop=(k == 1))
                    ins.then_inc(v_psum, 1)
                pe.wait_ge(k_act, AH)
                pe.wait_ge(v_dve, KT)
                pe.wait_ge(kr_ready, 1)

                def scores(n):
                    h, t = units[n]
                    lo, hi, _ = keys(t)
                    b = 2 * (n % 2)
                    if n >= 2:
                        pe.wait_ge(p_ready, n - 1)
                    q = qT[:, h, t * P:(t + 1) * P]
                    mid = min(hi, lo + 512)
                    ins = pe.matmul(ps[:, b, 0:mid - lo], q, kT[:, h, lo:mid], start=True, stop=True)
                    if hi > mid:
                        ins = pe.matmul(ps[:, b + 1, 0:hi - mid], q, kT[:, h, mid:hi], start=True, stop=True)
                    ins.then_inc(s_psum, 1)

                def turn(n):
                    h, t = units[n]
                    pe.wait_ge(p_ready, n + 1)
                    if n >= 1:
                        pe.wait_ge(pt_taken, n)
                    for i in range(len(keys(t)[2])):
                        ins = pe.transpose(ps[:, 4 + i // 4, (i % 4) * P:(i % 4 + 1) * P], prob[:, n % 2, i * P:(i + 1) * P], ident[:, :])
                    ins.then_inc(pt_psum, 1)

                def attend(n):
                    h, t = units[n]
                    pe.wait_ge(pt_taken, n + 1)
                    if n >= 2:
                        pe.wait_ge(o_taken, n - 1)
                    tiles = keys(t)[2]
                    for i, kt in enumerate(tiles):
                        ins = pe.matmul(ps[:, 6 + n % 2, 0:HD], probT[:, n % 2, i * P:(i + 1) * P], val[:, kt, h * HD:(h + 1) * HD],
                                        start=(i == 0), stop=(i == len(tiles) - 1))
                    ins.then_inc(o_psum, 1)

                scores(0)
                for n in range(len(units)):
                    if n + 1 < len(units):
                        scores(n + 1)
                    turn(n)
                    if n >= 1:
                        attend(n - 1)
                attend(len(units) - 1)
                pe.wait_ge(o_taken, len(units))
                for t in range(NT):
                    if t >= 2:
                        pe.wait_ge(mt_taken, t - 1)
                    for k in range(KD):
                        ins = pe.transpose(ps[:, 2 * (t % 2) + k // 4, (k % 4) * P:(k % 4 + 1) * P], mixed[:, t, k * P:(k + 1) * P], ident[:, :])
                    ins.then_inc(mt_psum, 1)
                pe.wait_ge(mt_taken, NT)
                for half in range(2):
                    pe.wait_ge(wout_slot, 16 * (half + 1))
                    for t in range(NT):
                        n = half * NT + t
                        if n >= 2:
                            pe.wait_ge(y_taken, n - 1)
                        for k in range(KD):
                            ins = pe.matmul(ps[:, 4 + n % 2, :], hT[:, k, t * P:(t + 1) * P], wout[:, k, :],
                                            start=(k == 0), stop=(k == KD - 1))
                        ins.then_inc(y_psum, 1)

            @block.scalar
            def _(act):
                for h in range(AH):
                    b = 3 * (h % 2)
                    act.wait_ge(q_psum, h + 1)
                    act.activation(qT[0:HD, h, P:T], ps[0:HD, b, :], ACT.Copy)
                    act.activation(qT[:, h, 0:P], ps[0:QK, b + 1, 0:P], ACT.Copy).then_inc(q_act, 1)
                for h in range(AH):
                    b = 2 * (h % 2)
                    act.wait_ge(k_psum, h + 1)
                    act.activation(kT[0:HD, h, 0:512], ps[0:HD, b, :], ACT.Copy)
                    act.activation(kT[0:HD, h, 512:768], ps[0:HD, b + 1, 0:256], ACT.Copy).then_inc(k_act, 1)
                for n, (h, t) in enumerate(units):
                    lo, hi, _ = keys(t)
                    act.wait_ge(max_ready, n + 1)
                    if n >= 2:
                        act.wait_ge(pt_psum, n - 1)
                        act.wait_ge(o_taken, n - 1)
                    act.activation(prob[:, n % 2, 0:hi - lo],
                                   ps[:, 2 * (n % 2):2 * (n % 2) + 2, :].rearrange("p a b -> p (a b)")[:, 0:hi - lo], ACT.Exp,
                                   bias=amax[:, n % 2, 1:2], scale=SCALE, accum_out=amax[:, n % 2, 2:3]).then_inc(p_ready, 1)
                for t in range(NT):
                    act.wait_ge(mt_psum, t + 1)
                    b = 2 * (t % 2)
                    act.activation(hT[:, :, t * P:(t + 1) * P], ps[:, b:b + 2, :].rearrange("p a (c d) -> p (a c) d", d=P),
                                   ACT.Copy).then_inc(mt_taken, 1)

            @block.vector
            def _(dve):
                link = chain_of(dve, c_chain)
                for h in range(AH):
                    b = 3 * (h % 2)
                    dve.wait_ge(q_psum, h + 1)
                    link(dve.tensor_tensor(rot[HD:QK, 0, :], ps[HD:QK, b, :], cos_sin[HD:QK, 0, :], ALU.mult))
                    link(dve.tensor_tensor(rot[HD:QK, 1, :], ps[HD:QK, b + 2, :], cos_sin[HD:QK, 1, :], ALU.mult))
                    dve.tensor_tensor(qT[HD:QK, h, P:T], rot[HD:QK, 0, :], rot[HD:QK, 1, :], ALU.add).then_inc(q_dve, 1)
                    dve.wait_ge(q_dve, h + 1)
                dve.tensor_copy(kT[HD:QK, :, :], krT[HD:QK, :].unsqueeze(1).to_broadcast([ROPE, AH, KT * P])).then_inc(kr_ready, 1)
                for t in range(KT):
                    dve.wait_ge(v_psum, t + 1)
                    dve.tensor_copy(val[:, t, :], ps[:, 4 + t % 2, :]).then_inc(v_dve, 1)

                def maxima(n):
                    h, t = units[n]
                    lo, hi, _ = keys(t)
                    dve.wait_ge(s_psum, n + 1)
                    if n >= 2:
                        dve.wait_ge(p_ready, n - 1)
                    link(dve.tensor_reduce(amax[:, n % 2, 0:1],
                                           ps[:, 2 * (n % 2):2 * (n % 2) + 2, :].rearrange("p a b -> p (a b)")[:, 0:hi - lo], AX.X, ALU.max))
                    dve.tensor_scalar(amax[:, n % 2, 1:2], amax[:, n % 2, 0:1], -SCALE, None, ALU.mult).then_inc(max_ready, 1)

                def turned(n):
                    dve.wait_ge(pt_psum, n + 1)
                    if n >= 2:
                        dve.wait_ge(o_psum, n - 1)
                    tiles = len(keys(units[n][1])[2])
                    dve.tensor_copy(probT[:, n % 2, 0:tiles * P],
                                    ps[:, 4:6, :].rearrange("p a b -> p (a b)")[:, 0:tiles * P]).then_inc(pt_taken, 1)

                def finish(n):
                    h, t = units[n]
                    dve.wait_ge(p_ready, n + 1)
                    link(dve.reciprocal(amax[:, n % 2, 3:4], amax[:, n % 2, 2:3]))
                    dve.wait_ge(o_psum, n + 1)
                    dve.tensor_scalar(mixed[:, t, 512 + h * HD:512 + (h + 1) * HD], ps[:, 6 + n % 2, 0:HD],
                                      amax[:, n % 2, 3:4], None, ALU.mult).then_inc(o_taken, 1)
                    dve.wait_ge(o_taken, n + 1)

                maxima(0)
                for n in range(len(units)):
                    if n >= 1:
                        finish(n - 1)
                    if n + 1 < len(units):
                        maxima(n + 1)
                    turned(n)
                finish(len(units) - 1)
                for half in range(2):
                    for t in range(NT):
                        n, v = half * NT + t, (0 if t == 0 else 1)
                        span = slice(half * 512, (half + 1) * 512)
                        dve.wait_ge(y_psum, n + 1)
                        link(dve.tensor_tensor(xn[:, n % 2, 0:512], ps[:, 4 + n % 2, :], gate1[:, v, span], ALU.mult))
                        dve.sem_inc(y_taken, 1)
                        dve.tensor_tensor(x[:, t, span], x[:, t, span], xn[:, n % 2, 0:512], ALU.add)

    s6 = ExitStack()
    h_hi = sb("h_hi", [P, KD, T], F32R, stack=s6)
    h_lo = sb("h_lo", [P, KD, T], F32R, stack=s6)
    s65 = ExitStack()
    slots = sb("slots", [P, 3, T], stack=s65)
    s7 = ExitStack()
    h2T = sb("h2T", [P, KD, T], stack=s7)
    xn2 = sb("xn2", [P, 2, D], stack=s7)
    wq = sb("wq", [P, 2, KD, 512], stack=s7)
    skT = sb("skT", [P, 2, NKEYS], stack=s7)
    pqT = sb("pqT", [P, 2, T], stack=s7)
    topv = sb("topv", [P, NT, RH, 2, TOP], stack=s7)
    topi = sb("topi", [P, NT, RH, 2, TOP], U32, stack=s7)
    topf = sb("topf", [P, NT, RH, 2, TOP], BF16, stack=s7)
    rest1 = sb("rest1", [P, NT, NKEYS], stack=s7)
    rest = sb("rest", [P, NT, 256], stack=s7)
    cand = sb("cand", [P, 2, NT, 256], stack=s7)
    best = sb("best", [P, NT, RH, TOP], stack=s7)
    pos = sb("pos", [P, NT, SLOTS], U32, stack=s7)
    pos12 = sb("pos12", [P, 2, NT, SLOTS], U32, stack=s7)
    posf = sb("posf", [P, 2, NT, SLOTS], BF16, stack=s7)
    gsum = sb("gsum", [P, 2, NT, RH], stack=s7)
    iota16 = sb("iota16", [P, TOP], BF16, stack=s7)
    hot = sb("hot", [P, 3, SLOTS, TOP], BF16, stack=s7)
    keysel = sb("keysel", [P, NT, 2, SLOTS], stack=s7)
    s7.close()
    s8 = ExitStack()
    iota = sb("iota", [P, NKEYS], stack=s8)
    stage = sb("stage", [P, 3, 2 * GB], stack=s8)
    hot1 = sb("hot1", [P, 2, 4, NKEYS], stack=s8)
    hot2 = sb("hot2", [P, 2, 4, NKEYS], stack=s8)
    gmat = sb("gmat", [P, 2, NKEYS, GB], stack=s8)
    s8.close()
    s65.close()
    s9 = ExitStack()
    y = sb("y", [P, NT, D], stack=s9)
    u_raw = sb("u_raw", [P, 2, KD, P], stack=s9)
    u_hi = sb("u_hi", [P, 2, KD, P], F32R, stack=s9)
    u_lo = sb("u_lo", [P, 2, KD, P], F32R, stack=s9)
    v_raw = sb("v_raw", [P, 2, D], stack=s9)
    v_hi = sb("v_hi", [P, NG, D], F32R, stack=s9)
    v_lo = sb("v_lo", [P, NG, D], F32R, stack=s9)
    gt = sb("gt", [P, 2, NB, 2, GB], stack=s9)
    a_hi = sb("a_hi", [P, 2, NG, T], F32R, stack=s9)
    a_lo = sb("a_lo", [P, 2, NG, T], F32R, stack=s9)
    s9.close()
    s6.close()

    d_load = K.sem("d_load")
    wq_slot = [K.sem(f"wq_slot{i}") for i in range(2)]
    n2 = dict(tp=K.sem("n2_psum"), ta=K.sem("n2_act"), td=K.sem("n2_dve"), sq=K.sem("n2_sq"), rt=K.sem("n2_root"),
              xn=K.sem("n2_xn"), hT=h2T, x_n=xn2)
    hi_ready = K.sem("hi_ready")
    pq_psum = K.sem("pq_psum")
    pq_taken = K.sem("pq_taken")
    sc_psum = K.sem("sc_psum")
    sc_taken = K.sem("sc_taken")
    d_chain = K.sem("d_chain")
    gate_in = K.sem("gate_in")
    gate_exp = K.sem("gate_exp")
    gate_done = K.sem("gate_done")
    top_step = K.sem("top_step")
    cand_ready = K.sem("cand_ready")
    cand_used = K.sem("cand_used")
    hot_ready = K.sem("hot_ready")
    hot_times = K.sem("hot_times")
    picked = K.sem("picked")
    slot_psum = K.sem("slot_psum")
    slot_taken = K.sem("slot_taken")

    def retrieve(l):
        with nc.Block() as block:
            @block.sync
            def _(sp):
                sp.dma_start(skT[:, :, :], a["skT"][l]).then_inc(d_load, 16)
                sp.dma_start(iota16[:, :], a["iota16"]).then_inc(d_load, 16)
                for c in range(4):
                    if c >= 2:
                        sp.wait_ge(pq_psum, 8 * (c - 1))
                    sp.dma_start(wq[:, c % 2, :, :], a["wq"][l, c]).then_inc(wq_slot[c % 2], 16)

            @block.tensor
            def _(pe):
                normalise(None, None, pe, 1, n2)
                pe.wait_ge(n2["ta"], NT)
                pe.wait_ge(n2["td"], NT)
                pe.wait_ge(d_load, 32)

                def query(j):
                    c = j // 4
                    pe.wait_ge(wq_slot[c % 2], 16 * (c // 2 + 1))
                    for half in range(2):
                        n = 2 * j + half
                        if n >= 2:
                            pe.wait_ge(pq_taken, n - 1)
                        for k in range(KD):
                            ins = pe.matmul(ps[:, half, 0:HALF], wq[:, c % 2, k, (j % 4) * P:(j % 4 + 1) * P],
                                            h2T[:, k, half * HALF:(half + 1) * HALF], start=(k == 0), stop=(k == KD - 1))
                        ins.then_inc(pq_psum, 1)

                query(0)
                for j in range(2 * RH):
                    if j + 1 < 2 * RH:
                        query(j + 1)
                    pe.wait_ge(pq_taken, 2 * (j + 1))
                    if j >= 2:
                        pe.wait_ge(sc_taken, j - 1)
                    for t in range(NT):
                        b = 2 + 2 * (j % 2) + t // 4
                        ins = pe.matmul(ps[:, b, (t % 4) * P:(t % 4 + 1) * P], pqT[:, j % 2, t * P:(t + 1) * P],
                                        skT[:, j % 2, :], start=True, stop=True)
                    ins.then_inc(sc_psum, 1)
                for t in range(NT):
                    pe.wait_ge(picked, 2 * t + 2)
                    pe.wait_ge(gate_done, 1)
                    if t >= 2:
                        pe.wait_ge(slot_taken, t - 1)
                    b = 6 + t % 2
                    pe.transpose(ps[:, b, 0:P], keysel[:, t, 0, :], ident[:, :])
                    pe.transpose(ps[:, b, P:2 * P], keysel[:, t, 1, :], ident[:, :])
                    pe.transpose(ps[:, b, 2 * P:3 * P], best[:, t, :, :].rearrange("p h s -> p (h s)"), ident[:, :]).then_inc(slot_psum, 1)

            @block.scalar
            def _(act):
                normalise(act, None, None, 1, n2)
                for t in range(NT):
                    act.wait_ge(n2["td"], t + 1)
                    act.wait_ge(n2["ta"], t + 1)
                    act.activation(h_hi[:, :, t * P:(t + 1) * P], h2T[:, :, t * P:(t + 1) * P], ACT.Copy).then_inc(hi_ready, 1)
                for n in range(4 * RH):
                    j, half = n // 2, n % 2
                    act.wait_ge(pq_psum, n + 1)
                    if j >= 2:
                        act.wait_ge(sc_psum, j - 1)
                    act.activation(pqT[:, j % 2, half * HALF:(half + 1) * HALF], ps[:, half, 0:HALF], ACT.Copy).then_inc(pq_taken, 1)
                act.wait_ge(gate_in, 1)
                act.activation(best[:, :, :, :], best[:, :, :, :], ACT.Exp).then_inc(gate_exp, 1)
                for t in range(NT):
                    act.wait_ge(slot_psum, t + 1)
                    act.activation(slots[:, :, t * P:(t + 1) * P], ps[:, 6 + t % 2, 0:3 * P].rearrange("p (a b) -> p a b", a=3),
                                   ACT.Copy).then_inc(slot_taken, 1)

            @block.vector
            def _(dve):
                link = chain_of(dve, d_chain)
                normalise(None, dve, None, 1, dict(n2, link=link))
                for t in range(NT):
                    dve.wait_ge(hi_ready, t + 1)
                    span = slice(t * P, (t + 1) * P)
                    dve.tensor_tensor(h_lo[:, :, span], h2T[:, :, span], h_hi[:, :, span], ALU.subtract)

                step = [0]

                def counted(ins):
                    step[0] += 1
                    ins.then_inc(top_step, 1)
                    return step[0]

                left_read = {}

                def top16(values, v, i, left, name):
                    first = [counted(dve.max(v(t)[:, 0:8], values(t))) for t in range(NT)]
                    cut = []
                    for t in range(NT):
                        dve.wait_ge(top_step, max(first[t], left_read.get((name, t), 1)))
                        counted(dve.max_index(i(t)[:, 0:8], v(t)[:, 0:8], values(t)))
                        cut.append(counted(dve.match_replace(left(t), v(t)[:, 0:8], values(t), -3.0e38)))
                    second = []
                    for t in range(NT):
                        dve.wait_ge(top_step, cut[t])
                        second.append(counted(dve.max(v(t)[:, 8:16], left(t))))
                    for t in range(NT):
                        dve.wait_ge(top_step, second[t])
                        left_read[name, t] = counted(dve.max_index(i(t)[:, 8:16], v(t)[:, 8:16], left(t)))

                def pairs(h):
                    dve.wait_ge(cand_ready, h + 1)
                    top16(lambda t: cand[:, h % 2, t, :], lambda t: best[:, t, h, :],
                          lambda t: pos[:, t, h * TOP:(h + 1) * TOP], lambda t: rest[:, t, :], "rest")
                    dve.wait_ge(top_step, step[0])
                    dve.sem_inc(cand_used, 1)

                for j in range(2 * RH):
                    h, half = j // 2, j % 2
                    b = 2 + 2 * (j % 2)
                    dve.wait_ge(sc_psum, j + 1)
                    top16(lambda t: ps[:, b + t // 4, (t % 4) * P:(t % 4 + 1) * P], lambda t: topv[:, t, h, half, :],
                          lambda t: topi[:, t, h, half, :], lambda t: rest1[:, t, :], "rest1")
                    dve.wait_ge(top_step, step[0])
                    dve.sem_inc(sc_taken, 1)
                    if half == 1 and h >= 1:
                        pairs(h - 1)
                link(dve.tensor_copy(topf[:, :, :, :, :].rearrange("p t h a s -> p (t h a s)"),
                                     topi[:, :, :, :, :].rearrange("p t h a s -> p (t h a s)")))
                pairs(RH - 1)
                link(dve.tensor_copy(gsum[:, 0, :, :].rearrange("p t h -> p (t h)"),
                                     best[:, :, :, 0:1].rearrange("p t h s -> p (t h s)")))
                link(dve.tensor_tensor(best[:, :, :, :].rearrange("p t h s -> p (t h) s"),
                                       best[:, :, :, :].rearrange("p t h s -> p (t h) s"),
                                       col(gsum[:, 0, :, :].rearrange("p t h -> p (t h)"), TOP), ALU.subtract))
                dve.sem_inc(gate_in, 1)
                dve.tensor_scalar(pos12[:, 0, :, :], pos[:, :, :], 4, None, ALU.logical_shift_right)
                link(dve.tensor_scalar(pos12[:, 1, :, :], pos[:, :, :], TOP - 1, None, ALU.bitwise_and))
                link(dve.tensor_copy(posf[:, :, :, :], pos12[:, :, :, :]))

                def one_hot(u):
                    t, half = u // 2, u % 2
                    if u >= 3:
                        dve.wait_ge(picked, u - 2)
                    dve.tensor_tensor(hot[:, u % 3, :, :], col(posf[:, half, t, :], TOP),
                                      iota16[:, :].unsqueeze(1).to_broadcast([P, SLOTS, TOP]), ALU.is_equal).then_inc(hot_ready, 1)

                one_hot(0)
                one_hot(1)
                for u in range(2 * NT):
                    if u + 2 < 2 * NT:
                        one_hot(u + 2)
                    if u == 2:
                        dve.wait_ge(gate_exp, 1)
                        link(dve.tensor_reduce(gsum[:, 0, :, :].rearrange("p t h -> p (t h)"),
                                               best[:, :, :, :].rearrange("p t h s -> p (t h) s"), AX.X, ALU.add))
                        link(dve.reciprocal(gsum[:, 1, :, :], gsum[:, 0, :, :]))
                        link(dve.tensor_tensor(best[:, :, :, :].rearrange("p t h s -> p (t h) s"),
                                               best[:, :, :, :].rearrange("p t h s -> p (t h) s"),
                                               col(gsum[:, 1, :, :].rearrange("p t h -> p (t h)"), TOP), ALU.mult))
                        dve.sem_inc(gate_done, 1)
                    dve.wait_ge(hot_times, u + 1)
                    dve.tensor_reduce(keysel[:, u // 2, u % 2, :], hot[:, u % 3, :, :], AX.X, ALU.add).then_inc(picked, 1)

            @block.gpsimd
            def _(pool):
                for h in range(RH):
                    pool.wait_ge(sc_taken, 2 * h + 2)
                    if h >= 2:
                        pool.wait_ge(cand_used, h - 1)
                    for t in range(NT):
                        ins = pool.tensor_tensor(cand[:, h % 2, t, :].rearrange("p (i j) -> p i j", i=TOP),
                                                 col(topv[:, t, h, 0, :], TOP),
                                                 topv[:, t, h, 1, :].unsqueeze(1).to_broadcast([P, TOP, TOP]), ALU.add)
                    ins.then_inc(cand_ready, 1)
                for u in range(2 * NT):
                    t, half = u // 2, u % 2
                    pool.wait_ge(hot_ready, u + 1)
                    at = hot[:, u % 3, :, :].rearrange("p (h s) j -> p h s j", h=RH)
                    pool.tensor_tensor(at, at, topf[:, t, :, half, :].unsqueeze(2).to_broadcast([P, RH, TOP, TOP]),
                                       ALU.mult).then_inc(hot_times, 1)

    e_load = K.sem("e_load")
    staged = K.sem("staged")
    hots_ready = K.sem("hots_ready")
    hots_pool = K.sem("hots_pool")
    pool_quads = K.sem("pool_quads")
    hots_used = K.sem("hots_used")
    gm_taken = K.sem("gm_taken")
    gm_stored = [K.sem(f"gm_stored{i}") for i in range(2)]

    def gate_matrices(l):
        quads = GB // 4
        turns = NB // 2
        with nc.Block() as block:
            @block.sync
            def _(sp):
                sp.dma_start(iota[:, :], a["iota"]).then_inc(e_load, 16)
                with sp.Fori(0, turns) as i:
                    for b in range(2):
                        sp.wait_ge(gm_taken, i * (2 * quads) + (b + 1) * quads + 8)
                        sp.dma_start(gates_dram[i * 2 + b], gmat[:, b, :, :].rearrange("p a b -> p (a b)")).then_inc(gm_stored[b], 16)
                for b in range(2):
                    sp.wait_ge(gm_stored[b], 16 * turns + 16)

            @block.vector
            def _(dve):
                dve.wait_ge(e_load, 16)
                dve.sem_inc(staged, 1)
                with dve.Fori(0, turns) as i:
                    dve.tensor_copy(stage[:, :, :], slots[:, :, bass.ds(i * (2 * GB), 2 * GB)]).then_inc(staged, 1)
                    dve.wait_ge(staged, i + 2)
                    for q in range(2 * quads):
                        s = q % 2
                        dve.wait_ge(hots_used, i * (2 * quads) + q + 1)
                        for r in range(4):
                            n = q * 4 + r
                            if r < 2:
                                dve.tensor_scalar(hot2[:, s, r, :], iota[:, :], stage[:, 1, n:n + 1], None, ALU.is_equal)
                            ins = dve.tensor_scalar(hot1[:, s, r, :], iota[:, :], stage[:, 0, n:n + 1], stage[:, 2, n:n + 1],
                                                    ALU.is_equal, ALU.mult)
                        ins.then_inc(hots_ready, 1)
                    dve.wait_ge(hots_ready, i * (2 * quads) + 2 * quads)
                    dve.wait_ge(hots_pool, i * (2 * quads) + 2 * quads)

            @block.gpsimd
            def _(pool):
                pool.wait_ge(e_load, 16)
                with pool.Fori(0, turns) as i:
                    pool.wait_ge(staged, i + 2)
                    for q in range(2 * quads):
                        pool.wait_ge(hots_used, i * (2 * quads) + q + 1)
                        pool.sem_inc(pool_quads, 1)
                        for r in range(2, 4):
                            n = q * 4 + r
                            ins = pool.tensor_scalar(hot2[:, q % 2, r, :], iota[:, :], stage[:, 1, n:n + 1], None, ALU.is_equal)
                        ins.then_inc(hots_pool, 1)

            @block.tensor
            def _(pe):
                pe.sem_inc(hots_used, 2)
                with pe.Fori(0, turns) as i:
                    for q in range(2 * quads):
                        s = q % 2
                        pe.wait_ge(hots_ready, i * (2 * quads) + q + 1)
                        pe.wait_ge(hots_pool, i * (2 * quads) + q + 1)
                        pe.wait_ge(gm_taken, i * (2 * quads) + q + 1)
                        for r in range(4):
                            ins = pe.matmul(ps[:, q % 8, r * P:(r + 1) * P], hot2[:, s, r, :], hot1[:, s, r, :], start=True, stop=True)
                        ins.then_inc(hots_used, 1)

            @block.scalar
            def _(act):
                act.sem_inc(gm_taken, 8)
                act.sem_inc(gm_stored[0], 16)
                act.sem_inc(gm_stored[1], 16)
                with act.Fori(0, turns) as i:
                    for b in range(2):
                        act.wait_ge(gm_stored[b], i * 16 + 16)
                        for q in range(quads):
                            n = b * quads + q
                            act.wait_ge(hots_used, i * (2 * quads) + n + 3)
                            act.activation(gmat[:, b, :, q * 4:(q + 1) * 4], ps[:, n % 8, :].rearrange("p (t k) -> p k t", t=4),
                                           ACT.Copy).then_inc(gm_taken, 1)

    u_in = [K.sem(f"u_in{i}") for i in range(2)]
    v_in = [K.sem(f"v_in{i}") for i in range(2)]
    g_in = [K.sem(f"g_in{i}") for i in range(2)]
    u_high = K.sem("u_high")
    u_split = K.sem("u_split")
    v_high = K.sem("v_high")
    v_split = K.sem("v_split")
    hid_psum = K.sem("hid_psum")
    hid_act = K.sem("hid_act")
    gated = K.sem("gated")
    a_high = K.sem("a_high")
    a_ready = K.sem("a_ready")
    out_psum = K.sem("out_psum")
    y_added = K.sem("y_added")
    f_chain = K.sem("f_chain")
    UNITS = 2 * NT
    PASSES = ((0, 0), (0, 1), (1, 0))

    def experts(l):
        with nc.Block() as block:
            @block.sync
            def _(sp):
                def load_u(g, j):
                    sp.wait_ge(u_split, g * NG + j + 1)
                    sp.dma_start(u_raw[:, j % 2, :, :], a["u"][l, g * NG + j]).then_inc(u_in[j % 2], 16)

                def load_v(g, j):
                    sp.wait_ge(v_split, g * NG + j + 1)
                    sp.dma_start(v_raw[:, j % 2, :], a["v"][l, g * NG + j]).then_inc(v_in[j % 2], 16)

                def load_g(g, q):
                    sp.wait_ge(gated, g * NG + 2 * q + 2)
                    sp.dma_start(gt[:, q, :, :, :].rearrange("p b k t -> p b (k t)"),
                                 gates_dram[:, :, bass.ds((g * NG + 2 * q) * GB, 2 * GB)].rearrange("b p n -> p b n")
                                 ).then_inc(g_in[q], 16)

                for j in range(NG):
                    load_u(0, j)
                    if j % 2 == 0:
                        load_g(0, j // 2)
                with sp.Fori(1, GROUPS) as g:
                    for j in range(NG):
                        load_u(g, j)
                        if j % 2 == 0:
                            load_g(g, j // 2)
                        load_v(g - 1, j)
                for j in range(NG):
                    load_v(GROUPS - 1, j)

            @block.tensor
            def _(pe):
                pe.sem_inc(hid_psum, 2)
                pe.sem_inc(out_psum, 2 * UNITS)

                def hidden(g):
                    for j in range(NG):
                        pe.wait_ge(u_split, g * NG + j + 3)
                        if not (isinstance(g, int) and g == 0 and j < 2):
                            pe.wait_ge(a_ready, g * NG + j - 1)
                        for half in range(2):
                            for k in range(KD):
                                for n, (wl, hl) in enumerate(PASSES):
                                    ins = pe.matmul(ps[:, 2 * (j % 2) + half, 0:HALF], (u_hi, u_lo)[wl][:, j % 2, k, :],
                                                    (h_hi, h_lo)[hl][:, k, half * HALF:(half + 1) * HALF],
                                                    start=(k == 0 and n == 0), stop=(k == KD - 1 and n == 2))
                        ins.then_inc(hid_psum, 1)

                def outputs(g, p):
                    pe.wait_ge(v_split, g * NG + NG + 2)
                    pe.wait_ge(a_ready, g * NG + NG)
                    for c in range(UNITS):
                        t, half = c // 2, c % 2
                        pe.wait_ge(y_added, g * UNITS + c + 1)
                        for j in range(NG):
                            for n, (al, vl) in enumerate(PASSES):
                                ins = pe.matmul(ps[:, 4 + (2 * p + c) % 4, :], (a_hi, a_lo)[al][:, p, j, t * P:(t + 1) * P],
                                                (v_hi, v_lo)[vl][:, j, half * 512:(half + 1) * 512],
                                                start=(j == 0 and n == 0), stop=(j == NG - 1 and n == 2))
                        ins.then_inc(out_psum, 1)

                hidden(0)
                with pe.Fori(0, GROUPS // 2 - 1) as i:
                    hidden(i * 2 + 1)
                    outputs(i * 2, 0)
                    hidden(i * 2 + 2)
                    outputs(i * 2 + 1, 1)
                hidden(GROUPS - 1)
                outputs(GROUPS - 2, 0)
                outputs(GROUPS - 1, 1)

            @block.scalar
            def _(act):
                def high_u(g, j):
                    act.wait_ge(u_in[j % 2], g * (NG // 2 * 16) + j // 2 * 16 + 16)
                    act.wait_ge(hid_psum, g * NG + j + 1)
                    act.activation(u_hi[:, j % 2, :, :], u_raw[:, j % 2, :, :], ACT.Copy).then_inc(u_high, 1)

                def high_v(g, j):
                    act.wait_ge(v_in[j % 2], g * (NG // 2 * 16) + j // 2 * 16 + 16)
                    act.wait_ge(out_psum, g * UNITS + 2 * UNITS)
                    act.activation(v_hi[:, j, :], v_raw[:, j % 2, :], ACT.Copy).then_inc(v_high, 1)

                def group(g, p, first=False, last=False):
                    for j in range(NG):
                        b = 2 * (j % 2)
                        if not first:
                            high_v(g - 1, j)
                        act.wait_ge(hid_psum, g * NG + j + 3)
                        act.activation(ps[:, b:b + 2, 0:HALF], ps[:, b:b + 2, 0:HALF], ACT.Gelu_apprx_tanh).then_inc(hid_act, 1)
                        if j + 2 < NG:
                            high_u(g, j + 2)
                        elif not last:
                            high_u(g + 1, j + 2 - NG)
                        act.wait_ge(gated, g * NG + j + 5)
                        act.wait_ge(out_psum, g * UNITS + UNITS)
                        act.activation(a_hi[:, p, j, :].rearrange("p (a b) -> p a b", a=2), ps[:, b:b + 2, 0:HALF],
                                       ACT.Copy).then_inc(a_high, 1)

                high_u(0, 0)
                high_u(0, 1)
                group(0, 0, first=True)
                with act.Fori(0, GROUPS // 2 - 1) as i:
                    group(i * 2 + 1, 1)
                    group(i * 2 + 2, 0)
                group(GROUPS - 1, 1, last=True)
                for j in range(NG):
                    high_v(GROUPS - 1, j)

            @block.gpsimd
            def _(pool):
                pool.sem_inc(u_split, 2)
                with pool.Fori(0, GROUPS) as g:
                    for j in range(NG):
                        pool.wait_ge(u_high, g * NG + j + 1)
                        pool.tensor_tensor(u_lo[:, j % 2, :, :], u_raw[:, j % 2, :, :], u_hi[:, j % 2, :, :],
                                           ALU.subtract).then_inc(u_split, 1)

            @block.vector
            def _(dve):
                link = chain_of(dve, f_chain)
                link(dve.memset(y[:, :, :], 0.0))
                dve.sem_inc(y_added, 4)
                dve.sem_inc(gated, 4)
                dve.sem_inc(v_split, 2)

                def low_v(g, j):
                    dve.wait_ge(v_high, g * NG + j + 1)
                    dve.tensor_tensor(v_lo[:, j, :], v_raw[:, j % 2, :], v_hi[:, j, :], ALU.subtract).then_inc(v_split, 1)

                def gate(g, p, first=False):
                    for j in range(NG):
                        if not first:
                            low_v(g - 1, j)
                        b, q = 2 * (j % 2), j // 2
                        dve.wait_ge(g_in[q], g * 16 + 16)
                        dve.wait_ge(hid_act, g * NG + j + 1)
                        for half in range(2):
                            at = ps[:, b + half, 0:HALF].rearrange("p (b t) -> p b t", t=GB)
                            ins = dve.tensor_tensor(at, at, gt[:, q, half * (NB // 2):(half + 1) * (NB // 2), j % 2, :], ALU.mult)
                        ins.then_inc(gated, 1)
                        dve.wait_ge(a_high, g * NG + j + 1)
                        dve.tensor_tensor(a_lo[:, p, j, :].rearrange("p (a b) -> p a b", a=2), ps[:, b:b + 2, 0:HALF],
                                          a_hi[:, p, j, :].rearrange("p (a b) -> p a b", a=2), ALU.subtract).then_inc(a_ready, 1)

                def add(g, p):
                    for c in range(UNITS):
                        t, half = c // 2, c % 2
                        dve.wait_ge(out_psum, g * UNITS + c + 1 + 2 * UNITS)
                        span = slice(half * 512, (half + 1) * 512)
                        dve.tensor_tensor(y[:, t, span], ps[:, 4 + (2 * p + c) % 4, :], y[:, t, span], ALU.add).then_inc(y_added, 1)
                    dve.wait_ge(y_added, g * UNITS + UNITS + 4)

                gate(0, 0, first=True)
                with dve.Fori(0, GROUPS // 2 - 1) as i:
                    gate(i * 2 + 1, 1)
                    add(i * 2, 0)
                    gate(i * 2 + 2, 0)
                    add(i * 2 + 1, 1)
                gate(GROUPS - 1, 1)
                add(GROUPS - 2, 0)
                for j in range(NG):
                    low_v(GROUPS - 1, j)
                add(GROUPS - 1, 1)
                for t in range(NT):
                    v = 0 if t == 0 else 1
                    ins = dve.tensor_tensor(y[:, t, :], y[:, t, :], gate2[:, v, :], ALU.mult)
                link(ins)
                for t in range(NT):
                    dve.tensor_tensor(x[:, t, :], x[:, t, :], y[:, t, :], ALU.add)

    with nc.Fori(0, DEPTH) as l:
        layer(l)
        for s in K.sems:
            nc.gpsimd.sem_clear(s)
        nc.all_engine_barrier()

    fg = sb("fg", [P, D])
    squares = sb("squares", [P, D])
    f_load = K.nc.alloc_semaphore("f_load")
    f_sq = K.nc.alloc_semaphore("f_sq")
    f_norm = K.nc.alloc_semaphore("f_norm")
    f_out = K.nc.alloc_semaphore("f_out")
    with nc.Block() as block:
        @block.sync
        def _(sp):
            sp.dma_start(fg[:, :], a["final_g"].partition_broadcast(P)).then_inc(f_load, 16)
            for t in range(NT):
                sp.wait_ge(f_norm, t + 2)
                sp.dma_start(o["y"][t * P:(t + 1) * P, :], x[:, t, :]).then_inc(f_out, 16)
            sp.wait_ge(f_out, 16 * NT)

        @block.scalar
        def _(act):
            for t in range(NT):
                act.activation(squares[:, :], x[:, t, :], ACT.Square, accum_out=ss[:, t:t + 1]).then_inc(f_sq, 1)
                act.wait_ge(f_sq, t + 1)
            act.activation(rstd[:, 0:NT], ss[:, 0:NT], ACT.Sqrt, bias=eps_col[:, 0:1], scale=1.0 / D).then_inc(f_sq, 1)

        @block.vector
        def _(dve):
            dve.wait_ge(f_sq, NT + 1)
            dve.wait_ge(f_load, 16)
            dve.reciprocal(rstd[:, 0:NT], rstd[:, 0:NT]).then_inc(f_norm, 1)
            dve.wait_ge(f_norm, 1)
            for t in range(NT):
                dve.scalar_tensor_tensor(x[:, t, :], x[:, t, :], rstd[:, t:t + 1], fg[:, :], ALU.mult,
                                         ALU.mult).then_inc(f_norm, 1)


ROPE_SWAP = np.r_[8:16, 0:8, 24:32, 16:24]


def constants():
    f = np.float32
    eye = np.eye(P, dtype=f)
    s, t = np.arange(P)[:, None], np.arange(P)[None, :]
    maskb = np.stack([np.where(s <= t, 0.0, MASKED), np.where(s >= t, 0.0, MASKED)], axis=1).astype(f)
    sel2 = np.zeros((2, 2, P), f)
    sel2[0, 0], sel2[1, 1] = 1.0, 1.0
    sel8 = np.zeros((ROWS, 8, P), f)
    for d in range(2):
        for h in range(H):
            sel8[32 * d + h, d * H + h] = 1.0
    grid_w, axis = 64, ROPE // 2
    freqs = (f(10000.0) ** (-np.arange(0, axis, 2, dtype=f) / f(axis))).astype(f)
    position = np.arange(NS * P)
    row, column = (position // grid_w).astype(f), (position % grid_w).astype(f)
    ang = np.concatenate([row[None] * freqs[:, None]] * 2 + [column[None] * freqs[:, None]] * 2).astype(f)
    sign = np.where(np.arange(ROPE) % axis < axis // 2, -1.0, 1.0).astype(f)[:, None]
    cos_sin = np.stack([np.cos(ang), np.sin(ang) * sign], axis=1).astype(f)
    bf16 = mybir.dt.np(BF16)
    return {
        "ident": eye, "maskb": maskb, "sel2": sel2, "sel8": sel8, "cos_sin": cos_sin,
        "iota": np.tile(np.arange(NKEYS, dtype=f), (P, 1)),
        "iota16": np.tile(np.arange(TOP, dtype=f), (P, 1)).astype(bf16),
    }


def blocks(w, width):
    n, d, c = w.shape
    return np.ascontiguousarray(w.reshape(n, d // P, P, c // width, width).transpose(0, 3, 2, 1, 4))


def rows_of(w, width):
    n, d, c = w.shape
    return np.ascontiguousarray(w.reshape(n, d // P, P, c).transpose(0, 2, 1, 3))


def lay_out(x_prompt, x_sample, c, cache_mla_ckv, cache_mla_krope, state_mlstm_C, state_mlstm_n, state_mlstm_m,
            c_ctx, norm1_g, ada_w, ada_b, w_in, mlstm_gate_b, cm_norm_g, cm_ws, cm_b, mla_q_norm_g, mla_w_uq,
            mla_kv_norm_g, mla_w_ukv, w_out, norm2_g, peer_w_q, peer_subkeys, peer_u, peer_v, final_g):
    f = np.float32
    L = DEPTH
    mq, mk, mv, mo = (w_in[..., i * 256:(i + 1) * 256] for i in range(4))
    g = w_in[..., 1024:1040]
    cu, cv, cq, ckv = (w_in[..., 1040 + i * 256:1040 + (i + 1) * 256] for i in range(4))
    kr = w_in[..., 2064:2096]
    w_small = np.zeros((L, D, SMALL), f)
    w_small[..., 0:4], w_small[..., 32:36] = g[..., 0:4], g[..., 8:12]
    w_small[..., 36:40], w_small[..., 68:72] = g[..., 4:8], g[..., 12:16]
    w_small[..., 72:104], w_small[..., 104:136] = kr, kr[..., ROPE_SWAP]
    gate_b = np.zeros((L, ROWS, 2), f)
    gate_b[:, 0:4, 0], gate_b[:, 32:36, 0] = mlstm_gate_b[:, 0:4], mlstm_gate_b[:, 8:12]
    gate_b[:, 0:4, 1], gate_b[:, 32:36, 1] = mlstm_gate_b[:, 4:8], mlstm_gate_b[:, 12:16]
    m0 = np.zeros((L, ROWS, 1), f)
    m0[:, 0:4, 0], m0[:, 32:36, 0] = state_mlstm_m[0, :, 0], state_mlstm_m[0, :, 1]
    cn0 = np.concatenate([state_mlstm_C[0], state_mlstm_n[0][..., None]], axis=-1)
    cn0 = cn0.reshape(L, 2, 2, 2, HD, HD + 1).transpose(0, 3, 4, 1, 2, 5).reshape(L, P, 2, 2, HD + 1)
    uq = mla_w_uq.reshape(L, 256, AH, QK)
    ukv = mla_w_ukv.reshape(L, 256, AH, 2 * HD)

    def halves(w):
        return np.ascontiguousarray(w.reshape(L, 2, P, -1).transpose(0, 2, 1, 3))

    return {
        "x": np.concatenate([x_prompt[0], x_sample[0]]),
        "cT": np.stack([c_ctx, c[0]]).reshape(2, KD, P).transpose(2, 1, 0),
        "normT": np.stack([norm1_g, norm2_g], axis=1).reshape(L, 2, KD, P).transpose(0, 3, 1, 2),
        "ada_w": blocks(ada_w, 512), "ada_b": ada_b.reshape(L, 12, 512),
        "w_in": blocks(np.concatenate([mk, mv, mo, cu, cv, cq, ckv, mq], axis=-1), 512),
        "w_small": rows_of(w_small, SMALL),
        "gate_b": gate_b, "m0": m0, "cn0": cn0,
        "wsT": cm_ws.transpose(0, 3, 1, 2), "cmb": cm_b.transpose(0, 2, 1),
        "normg": np.stack([cm_norm_g, mla_q_norm_g, mla_kv_norm_g], axis=1),
        "cacheT": cache_mla_ckv[0].transpose(0, 2, 1).reshape(L, 2, P, P).transpose(0, 2, 1, 3),
        "kr_cacheT": cache_mla_krope[0].transpose(0, 2, 1),
        "wuq": halves(mla_w_uq), "wqs": halves(uq[..., HD:][..., ROPE_SWAP]),
        "wuk": halves(ukv[..., :HD]), "wuv": halves(ukv[..., HD:]),
        "w_out": blocks(w_out, 512), "wq": blocks(peer_w_q, 512),
        "skT": peer_subkeys.transpose(0, 3, 1, 2),
        "u": peer_u.reshape(L, NKEYS, NKEYS, KD, P).transpose(0, 1, 4, 3, 2),
        "v": peer_v.reshape(L, NKEYS, NKEYS, D),
        "final_g": final_g,
        **constants(),
    }


OUTPUTS = {"y": (T, D), "ckv": (DEPTH, P, 256), "kr": (DEPTH, P, ROPE), "cn": (DEPTH, P, 2, 2, HD + 1),
           "m": (DEPTH, ROWS, 1)}


def kernel(**inputs):
    import concourse.bacc as bacc
    from concourse.bass_utils import run_bass_kernel_spmd

    nc = bacc.Bacc("TRN2", target_bir_lowering=False, num_devices=1)
    arrays = {f"in_{k}": np.ascontiguousarray(v) for k, v in lay_out(**{k: np.asarray(v) for k, v in inputs.items()}).items()}
    a = {k[3:]: nc.dram_tensor(k, v.shape, mybir.dt.from_np(v.dtype), kind="ExternalInput").ap() for k, v in arrays.items()}
    o = {k: nc.dram_tensor(f"out_{k}", v, F32, kind="ExternalOutput").ap() for k, v in OUTPUTS.items()}
    build_program(nc, a, o)
    r = run_bass_kernel_spmd(nc, [arrays], core_ids=[0]).results[0]
    cn = r["out_cn"].reshape(DEPTH, 2, HD, 2, 2, HD + 1).transpose(0, 3, 4, 1, 2, 5).reshape(DEPTH, 2, H, HD, HD + 1)
    m = r["out_m"][:, :, 0]
    m = np.stack([m[:, 0:4], m[:, 32:36]], axis=1)
    y = r["out_y"]
    return (y[None, :P], y[None, P:], r["out_ckv"][None], r["out_kr"][None],
            np.ascontiguousarray(cn[..., :HD])[None], np.ascontiguousarray(cn[..., HD])[None], m[None])
```

```python
import math
from contextlib import ExitStack

import numpy as np

import concourse.bass as bass
from concourse import mybir

F32 = mybir.dt.float32
F32R = mybir.dt.float32r
BF16 = mybir.dt.bfloat16
U32 = mybir.dt.uint32
ALU = mybir.AluOpType
ACT = mybir.ActivationFunctionType
AX = mybir.AxisListType

P = 128
D = 1024
KD = D // P
DEPTH = 2
NT = 5
T = NT * P
NS = 4
EPS = 1e-6
H = 4
HD = 64
AH = 8
ROPE = 32
QK = HD + ROPE
KT = NT + 1
SCALE = float(QK) ** -0.5
RH = 8
TOP = 16
SLOTS = RH * TOP
NKEYS = 128
STAIRS = ((0, 1, 16, 0), (1, 3, 8, 16), (4, 4, 4, 40), (8, 8, 1, 56))
NCAND = 64
MASKED = -1e30
ROWS = 36
GB = 64
NB = T // GB
HOTS = 4
NG = 4
GROUPS = NKEYS // NG
HALF = T // 2
PASSES = ((0, 0), (0, 1), (1, 0))
MK, MV, MO, CU, CV, CQ, CKV = range(7)
CMQ, CSMALL = 7, 8
R_A, R_WK, R_WIN, R_EM = range(4)


def col(ap, n):
    return ap.unsqueeze(len(ap.shape)).to_broadcast(list(ap.shape) + [n])


class Counts:

    def __init__(self, nc):
        self.nc = nc
        self.sems = []

    def sem(self, name):
        s = self.nc.alloc_semaphore(name)
        self.sems.append(s)
        return s


def chain_of(eng, sem):
    count = [0]

    def link(ins):
        count[0] += 1
        ins.then_inc(sem, 1)
        eng.wait_ge(sem, count[0])

    return link


def build_program(nc, a, o):
    K = Counts(nc)
    ctx = ExitStack()

    def sb(name, shape, dt=F32, stack=ctx):
        return stack.enter_context(nc.sbuf_tensor(name, shape, dt))

    x = sb("x", [P, NT, D])
    gate2 = sb("gate2", [P, 2, D])
    modT = sb("modT", [P, 4, KD, 2])
    ident = sb("ident", [P, P])
    mod_bias = sb("mod_bias", [P, 4, KD])
    cT = sb("cT", [P, KD, 2])
    rstd = sb("rstd", [P, 16])
    ss = sb("ss", [P, 16])
    eps_col = sb("eps_col", [P, 1])
    one_col = sb("one_col", [P, 1])
    ps = ctx.enter_context(nc.psum_tensor("ps", [P, 8, 512], F32))

    g_dram = nc.dram_tensor("g_dram", [2, 2, D], F32, kind="Internal").ap()
    gates_dram = nc.dram_tensor("gates_dram", [NB, P, NKEYS * GB], F32, kind="Internal").ap()

    def normalise(act, dve, pe, which, n, first=lambda: None):
        sh, sc = 2 * which, 2 * which + 1
        xn, places = n["x_n"], n["places"]

        def span(t):
            return slice(t * P, (t + 1) * P)

        if act is not None:
            def high(t):
                act.wait_ge(n["ta"], t + 1)
                act.wait_ge(n["td"], t + 1)
                act.activation(n["hi"][:, :, span(t)], n["whole"](t), ACT.Copy).then_inc(n["hs"], 1)

            act.activation(rstd[:, 0:NT], ss[:, 0:NT], ACT.Sqrt, bias=eps_col[:, 0:1], scale=1.0 / D).then_inc(n["rt"], 1)
            first()
            if "mod" in n:
                act.wait_ge(n["mod"], 4)
            for t in range(NT):
                c = 0 if t == 0 else 1
                act.wait_ge(n["tp"], t + 1)
                if t >= places:
                    act.wait_ge(n["ls"], t - places + 1)
                for k in range(4):
                    ins = act.activation(n["whole"](t)[:, k, :], ps[:, 4 + 2 * (t % 2), k * P:(k + 1) * P],
                                         ACT.Identity, bias=modT[:, sh, k, c:c + 1], scale=modT[:, sc, k, c:c + 1])
                ins.then_inc(n["ta"], 1)
                if t >= 1:
                    high(t - 1)
            high(NT - 1)
        if dve is not None:
            link = n["link"]
            dve.wait_ge(n["rt"], 1)
            link(dve.reciprocal(rstd[:, 0:NT], rstd[:, 0:NT]))

            def scaled(t):
                if t >= 2:
                    dve.wait_ge(n["tp"], t - 1)
                dve.tensor_scalar(xn[:, t % 2, :], x[:, t, :], rstd[:, t:t + 1], None,
                                  ALU.mult).then_inc(n["xn"], 1)

            def low(t):
                dve.wait_ge(n["hs"], t + 1)
                dve.tensor_tensor(n["lo"][:, :, span(t)], n["whole"](t), n["hi"][:, :, span(t)],
                                  ALU.subtract).then_inc(n["ls"], 1)

            scaled(0)
            for t in range(NT):
                c = 0 if t == 0 else 1
                if t + 1 < NT:
                    scaled(t + 1)
                dve.wait_ge(n["tp"], t + 1)
                if t >= places:
                    dve.wait_ge(n["ls"], t - places + 1)
                for k in range(4):
                    ins = dve.tensor_scalar(n["whole"](t)[:, 4 + k, :], ps[:, 5 + 2 * (t % 2), k * P:(k + 1) * P],
                                            modT[:, sc, 4 + k, c:c + 1], modT[:, sh, 4 + k, c:c + 1],
                                            ALU.mult, ALU.add)
                ins.then_inc(n["td"], 1)
                if t >= 1:
                    low(t - 1)
            low(NT - 1)
        if pe is not None:
            for t in range(NT):
                pe.wait_ge(n["xn"], t + 1)
                if t >= 2:
                    pe.wait_ge(n["ta"], t - 1)
                    pe.wait_ge(n["td"], t - 1)
                for k in range(KD):
                    ins = pe.transpose(ps[:, 4 + 2 * (t % 2) + k // 4, (k % 4) * P:(k % 4 + 1) * P],
                                       xn[:, t % 2, k * P:(k + 1) * P], ident[:, :])
                ins.then_inc(n["tp"], 1)

    def squares(act, sem, done, t, junk):
        act.activation(junk, x[:, t, :], ACT.Square, accum_out=ss[:, t:t + 1]).then_inc(sem, 1)
        act.wait_ge(sem, done + 1)

    CHUNKS = 12

    def is_gate(j):
        return (j // 2) % 3 == 2

    def turned_before(j):
        return sum(not is_gate(i) for i in range(j))

    def modulation_sems(prefix, new):
        return dict(slot=[new(f"{prefix}_slot{i}") for i in range(3)], bias=new(f"{prefix}_bias"),
                    psum=new(f"{prefix}_psum"), copied=new(f"{prefix}_copied"), spread=new(f"{prefix}_spread"),
                    taken=new(f"{prefix}_taken"), stored=[new(f"{prefix}_stored{i}") for i in range(2)])

    def modulation_loads(sp, m, ring, rows, ada, bias, slot_free):
        sp.dma_start(mod_bias[:, :, :], bias).then_inc(m["bias"], 16)
        for j in range(CHUNKS + 3):
            if j < CHUNKS:
                if j < 3:
                    slot_free(j)
                else:
                    sp.wait_ge(m["psum"], j - 2)
                sp.dma_start(ring[j % 3], ada[j]).then_inc(m["slot"][j % 3], 16)
            i = j - 3
            if i >= 0 and is_gate(i):
                sp.wait_ge(m["copied"], i + 1)
                sp.dma_start(g_dram[i // 6, :, (i % 2) * 512:(i % 2 + 1) * 512], rows[:, i % 2, :]).then_inc(m["stored"][i % 2], 16)
        for half in range(2):
            sp.wait_ge(m["stored"][half], 32)

    def modulation_products(pe, m, ring, rows):
        def product(j):
            pe.wait_ge(m["slot"][j % 3], 16 * (j // 3 + 1))
            if j >= 2:
                pe.wait_ge(m["copied"], j - 1)
            for k in range(KD):
                ins = pe.matmul(ps[0:2, j % 2, :], cT[:, k, :], ring[j % 3][:, k, :], start=(k == 0), stop=(k == KD - 1))
            ins.then_inc(m["psum"], 1)

        product(0)
        for j in range(CHUNKS):
            if j + 1 < CHUNKS:
                product(j + 1)
            if not is_gate(j):
                n = turned_before(j)
                pe.wait_ge(m["copied"], j + 1)
                if n >= 2:
                    pe.wait_ge(m["taken"], n - 1)
                for i in range(4):
                    ins = pe.transpose(ps[:, 6 + n % 2, 2 * i:2 * i + 2], rows[:, j % 2, i * P:(i + 1) * P], ident[0:2, 0:2])
                ins.then_inc(m["spread"], 1)
        pe.wait_ge(m["taken"], turned_before(CHUNKS))

    def modulation_copies(act, m, rows, after=None):
        def copy(j):
            act.wait_ge(m["psum"], j + 1)
            if j >= 2 and is_gate(j - 2):
                act.wait_ge(m["stored"][j % 2], 16 * ((j - 2) // 6 + 1))
            elif j >= 2:
                act.wait_ge(m["spread"], turned_before(j - 1))
            act.activation(rows[:, j % 2, :], ps[0:2, j % 2, :], ACT.Copy).then_inc(m["copied"], 1)

        act.wait_ge(m["bias"], 16)
        copy(0)
        for j in range(CHUNKS):
            if j + 1 < CHUNKS:
                copy(j + 1)
            if not is_gate(j):
                n, kind, half = turned_before(j), j // 2, j % 2
                which = kind if kind < 2 else kind - 1
                act.wait_ge(m["spread"], n + 1)
                for i in range(4):
                    k = half * 4 + i
                    ins = act.activation(modT[:, which, k, :], ps[:, 6 + n % 2, 2 * i:2 * i + 2], ACT.Identity,
                                         bias=mod_bias[:, which, k:k + 1], scale=1.0)
                ins.then_inc(m["taken"], 1)
            if after is not None:
                after(j)

    def clear_counts():
        for s in K.sems:
            nc.gpsimd.sem_clear(s)
        nc.all_engine_barrier()

    load = nc.alloc_semaphore("first_loads")
    pre = nc.alloc_semaphore("first_constants")
    silu = nc.alloc_semaphore("silu_ready")
    with nc.Block() as block:
        @block.sync
        def _(sp):
            sp.dma_start(x[:, :, :], a["x"].rearrange("(t p) d -> p t d", p=P)).then_inc(load, 16)
            sp.dma_start(ident[:, :], a["ident"]).then_inc(load, 16)
            sp.dma_start(cT[:, :, :], a["cT"]).then_inc(load, 16)
            sp.wait_ge(load, 48)

        @block.vector
        def _(dve):
            dve.memset(eps_col[:, :], EPS).then_inc(pre, 1)
            dve.memset(one_col[:, :], 1.0).then_inc(pre, 1)
            dve.wait_ge(pre, 2)

        @block.scalar
        def _(act):
            act.wait_ge(load, 48)
            act.activation(cT[:, :, :], cT[:, :, :], ACT.Silu).then_inc(silu, 1)
            act.wait_ge(silu, 1)

    def layer(l):
        project(l)
        mixers(l)
        attention(l)
        retrieve(l)
        gate_matrices(l)
        experts(l)

    s0 = ExitStack()
    n1_hi = sb("n1_hi", [P, KD, T], F32R, stack=s0)
    n1_lo = sb("n1_lo", [P, KD, T], F32R, stack=s0)
    s0.close()
    s1 = ExitStack()
    wuq = sb("wuq", [P, 2, AH * P], stack=s1)
    wuk = sb("wuk", [P, 2, 512], stack=s1)
    wuv = sb("wuv", [P, 2, 512], stack=s1)
    mixed = sb("mixed", [P, NT, D], stack=s1)
    cos_sin = sb("cos_sin", [P, 2, NS * P], stack=s1)
    xn = sb("xn", [P, 2, D], stack=s1)
    gate1 = sb("gate1", [P, 2, D], stack=s1)
    cqT = sb("cqT", [P, 2, T], stack=s1)
    ckvT = sb("ckvT", [P, 2, KT * P], stack=s1)
    krT = sb("krT", [QK, KT * P], stack=s1)
    s2 = ExitStack()
    proj = sb("proj", [P, NT, 7, 256], stack=s2)
    smallT = sb("smallT", [QK, 2, T], stack=s2)
    mqT = sb("mqT", [P, 2, T], stack=s2)
    s3 = ExitStack()
    w_raw = sb("w_raw", [P, 2, KD, 256], stack=s3)
    w_hi = sb("w_hi", [P, 2, KD, 256], F32R, stack=s3)
    w_lo = sb("w_lo", [P, 2, KD, 256], F32R, stack=s3)
    normT = sb("normT", [P, 2, KD], stack=s3)
    s3.close()
    s35 = ExitStack()
    wring = sb("wring", [P, 3, KD, 512], stack=s35)
    s35.close()
    s4 = ExitStack()
    mkT = sb("mkT", [P, 2, T], stack=s4)
    v1 = sb("v1", [P, NT, H, HD + 1], stack=s4)
    bwd = xn[:, :, :].rearrange("p a b -> p (a b)")[:, 0:NT * 256].rearrange("p (t e) -> p t e", t=NT)
    rowq = sb("rowq", [ROWS, 4, T], stack=s4)
    r_i, r_e, r_f = rowq[:, R_A, :], rowq[:, R_WK, :], rowq[:, R_WIN, :]
    r_b = sb("r_b", [ROWS, T], stack=s4)
    r_u = sb("r_u", [ROWS, T], stack=s4)
    r_prev = sb("r_prev", [ROWS, NT], stack=s4)
    r_end = sb("r_end", [ROWS, NT], stack=s4)
    r_dec = sb("r_dec", [ROWS, NT], stack=s4)
    r_m = sb("r_m", [ROWS, 1], stack=s4)
    gate_b = sb("gate_b", [ROWS, 2], stack=s4)
    m0 = sb("m0", [ROWS, 1], stack=s4)
    sel8 = sb("sel8", [ROWS, 8, P], stack=s4)
    maskb = sb("maskb", [P, 2, P], BF16, stack=s4)
    ident_b = sb("ident_b", [P, P], BF16, stack=s4)
    cols = sb("cols", [P, 4 * NT, ROWS], stack=s4)
    dec = sb("dec", [P, 8, NT], stack=s4)
    cn = sb("cn", [P, 2, 6, 2, HD + 1], stack=s4)
    wT = sb("wT", [P, 2, 512], stack=s4)
    swT = sb("swT", [P, 2, 512], stack=s4)
    kw = sb("kw", [P, 2, 256], stack=s4)
    nd = sb("nd", [P, H, HD + 1], stack=s4)
    dd = sb("dd", [P, 2, H], stack=s4)
    wsT = sb("wsT", [P, H, P], stack=s4)
    cmb = sb("cmb", [P, H], stack=s4)
    normg = sb("normg", [P, 3, 256], stack=s4)
    s4.close()
    s2.close()
    s45 = ExitStack()
    wout = sb("wout", [P, 2, KD, 256], stack=s45)
    s5 = ExitStack()
    qT = sb("qT", [QK, AH, T], stack=s5)
    kT = sb("kT", [QK, AH, KT * P], stack=s5)
    val = sb("val", [P, KT, 512], stack=s5)
    prob = sb("prob", [P, 2, T], stack=s5)
    probT = sb("probT", [P, 2, T], stack=s5)
    rot = [buffer[0:QK, :, 0:512] for buffer in (prob, probT)]
    amax = sb("amax", [P, 4, 4], stack=s5)
    s5.close()
    s55 = ExitStack()
    mix_hi = sb("mix_hi", [P, KD, T], F32R, stack=s55)
    mix_lo = sb("mix_lo", [P, KD, T], F32R, stack=s55)
    wout_hi = sb("wout_hi", [P, 2, KD, 256], F32R, stack=s55)
    wout_lo = sb("wout_lo", [P, 2, KD, 256], F32R, stack=s55)
    s55.close()
    s45.close()
    s1.close()

    mod_sems = modulation_sems("mod", K.sem)
    first_squares = nc.alloc_semaphore("first_squares")
    ring = [wring[:, i, :, :] for i in range(3)]
    with nc.Block() as block:
        @block.sync
        def _(sp):
            modulation_loads(sp, mod_sems, ring, xn[0:2, :, 0:512], a["ada_w"][DEPTH - 1], a["ada_bT"][DEPTH - 1],
                             lambda j: None)

        @block.tensor
        def _(pe):
            modulation_products(pe, mod_sems, ring, xn[0:2, :, 0:512])

        @block.scalar
        def _(act):
            for t in range(NT):
                squares(act, first_squares, t, t, gate2[:, 0, :])
            modulation_copies(act, mod_sems, xn[0:2, :, 0:512])

    clear_counts()

    sig_done = K.sem("sig_done")
    sq15 = K.sem("sq15")
    root15 = K.sem("root15")
    w_slot = [K.sem(f"w_slot{i}") for i in range(2)]
    w_high = K.sem("w_high")
    w_split = K.sem("w_split")
    a_load = K.sem("a_load")
    g_load = K.sem("g_load")
    mod_final = K.sem("mod_final")
    n1 = dict(tp=K.sem("n1_psum"), ta=K.sem("n1_act"), td=K.sem("n1_dve"), rt=K.sem("n1_root"),
              xn=K.sem("n1_xn"), mod=mod_final, x_n=xn, hs=K.sem("n1_hi_ready"), ls=K.sem("n1_lo_ready"), hi=n1_hi, lo=n1_lo,
              whole=lambda t: gate1[:, t % 2, :].rearrange("p (k s) -> p k s", k=KD), places=2)
    proj_psum = K.sem("proj_psum")
    proj_taken = K.sem("proj_taken")
    a_chain = K.sem("a_chain")

    def project(l):
        def done(c):
            return NT * (c + 1) if c < CMQ else NT * CMQ + 4 * (c - CMQ + 1)

        with nc.Block() as block:
            @block.sync
            def _(sp):
                sp.dma_start(normT[:, :, :], a["normT"][l]).then_inc(a_load, 16)
                for c in range(9):
                    if c >= 2:
                        sp.wait_ge(w_split, c - 1)
                    sp.dma_start(w_raw[:, c % 2, :, :], a["w_in"][l, c]).then_inc(w_slot[c % 2], 16)
                    if c == 3:
                        sp.wait_ge(n1["ls"], NT)
                        sp.dma_start(gate1[:, :, :], g_dram[0].partition_broadcast(P)).then_inc(g_load, 16)
                        sp.dma_start(gate2[:, :, :], g_dram[1].partition_broadcast(P)).then_inc(g_load, 16)
                        for g, to in enumerate((cqT, ckvT)):
                            sp.dma_start(to[:, :, 0:512], a["ada_g"][l, g].partition_broadcast(P)).then_inc(g_load, 16)

            @block.tensor
            def _(pe):
                normalise(None, None, pe, 0, n1)
                n = 0

                def product(rows, cols, m, left, right):
                    nonlocal n
                    if n >= 4:
                        pe.wait_ge(proj_taken, n - 3)
                    for k in range(KD):
                        for i, parts in enumerate(PASSES):
                            ins = pe.matmul(ps[0:rows, n % 4, 0:cols], left(k, parts), right(k, parts),
                                            start=(k == 0 and i == 0), stop=(k == KD - 1 and i == 2))
                    ins.then_inc(proj_psum, 1)
                    n += 1

                for c in range(9):
                    pe.wait_ge(w_split, c + 1)
                    if c < CMQ:
                        for t in range(NT):
                            if c == 0:
                                pe.wait_ge(n1["hs"], t + 1)
                                pe.wait_ge(n1["ls"], t + 1)
                            product(P, 256, c, lambda k, hw: (n1_hi, n1_lo)[hw[0]][:, k, t * P:(t + 1) * P],
                                    lambda k, hw: (w_hi, w_lo)[hw[1]][:, c % 2, k, :])
                    else:
                        wide = P if c == CMQ else QK
                        for b in range(2):
                            for half in range(2):
                                product(wide, HALF, c, lambda k, hw: (w_hi, w_lo)[hw[1]][:, c % 2, k, b * wide:(b + 1) * wide],
                                        lambda k, hw: (n1_hi, n1_lo)[hw[0]][:, k, half * HALF:(half + 1) * HALF])

            @block.scalar
            def _(act):
                def high_w(c):
                    act.wait_ge(w_slot[c % 2], 16 * (c // 2 + 1))
                    if c >= 2:
                        act.wait_ge(proj_psum, done(c - 2))
                        act.wait_ge(w_split, c - 1)
                    act.activation(w_hi[:, c % 2, :, :], w_raw[:, c % 2, :, :], ACT.Copy).then_inc(w_high, 1)

                def first():
                    high_w(0)
                    high_w(1)

                normalise(act, None, None, 0, n1, first)
                act.wait_ge(n1["tp"], NT)
                act.wait_ge(n1["xn"], NT)
                n = squared = 0
                for c in range(9):
                    for i in range(NT if c < CMQ else 4):
                        act.wait_ge(proj_psum, n + 1)
                        if c < CMQ:
                            act.activation(proj[:, i, c, :], ps[:, n % 4, 0:256], ACT.Copy).then_inc(proj_taken, 1)
                        else:
                            b, half = i // 2, i % 2
                            to, rows = (mqT, P) if c == CMQ else (smallT, QK)
                            act.activation(to[0:rows, b, half * HALF:(half + 1) * HALF], ps[0:rows, n % 4, 0:HALF],
                                           ACT.Copy).then_inc(proj_taken, 1)
                        n += 1
                        if c in (CV, CQ, CKV):
                            act.wait_ge(proj_taken, n)
                            at = 3 * i + (CV, CQ, CKV).index(c)
                            act.activation(xn[:, 0, 0:256], proj[:, i, c, :], ACT.Square, accum_out=ss[:, at:at + 1]).then_inc(sq15, 1)
                            squared += 1
                            act.wait_ge(sq15, squared)
                    if c + 2 < 9:
                        high_w(c + 2)
                    if c == CKV:
                        act.activation(rstd[:, 0:15], ss[:, 0:15], ACT.Sqrt, bias=eps_col[:, 0:1], scale=1.0 / 256).then_inc(root15, 1)
                        act.activation(proj[:, :, MO, :], proj[:, :, MO, :], ACT.Sigmoid).then_inc(sig_done, 1)

            @block.gpsimd
            def _(pool):
                for c in range(9):
                    pool.wait_ge(w_high, c + 1)
                    pool.tensor_tensor(w_lo[:, c % 2, :, :], w_raw[:, c % 2, :, :], w_hi[:, c % 2, :, :],
                                       ALU.subtract).then_inc(w_split, 1)

            @block.vector
            def _(dve):
                link = chain_of(dve, a_chain)
                dve.wait_ge(a_load, 16)
                for w in range(2):
                    for v in range(2):
                        dve.scalar_tensor_tensor(modT[:, 2 * w + 1, :, v], modT[:, 2 * w + 1, :, v], 1.0,
                                                 normT[:, w, :], ALU.add, ALU.mult).then_inc(mod_final, 1)
                dve.wait_ge(mod_final, 4)
                normalise(None, dve, None, 0, dict(n1, link=link))
                dve.wait_ge(g_load, 64)
                for gate, bias in ((gate1, cqT), (gate2, ckvT)):
                    both = gate[:, :, :].rearrange("p v (a b) -> p v a b", a=2)
                    dve.tensor_tensor(both, both, bias[:, :, 0:512].unsqueeze(1).to_broadcast([P, 2, 2, 512]), ALU.add)

    b_load = K.sem("b_load")
    rows_load = K.sem("rows_load")
    c_load = K.sem("c_load")
    b_out = K.sem("b_out")
    b_chain = K.sem("b_chain")
    normed = K.sem("normed")
    kq_psum = K.sem("kq_psum")
    kq_taken = K.sem("kq_taken")
    lat_psum = K.sem("lat_psum")
    lat_taken = K.sem("lat_taken")
    sgu_psum = K.sem("sgu_psum")
    sgu_taken = K.sem("sgu_taken")
    nf_ready = K.sem("nf_ready")
    log_ready = K.sem("log_ready")
    rows_in = K.sem("rows_in")
    rows_exp = K.sem("rows_exp")
    cols_psum = K.sem("cols_psum")
    cols_taken = K.sem("cols_taken")
    w_psum = K.sem("w_psum")
    w_exp = K.sem("w_exp")
    st_psum = K.sem("st_psum")
    sw_ready = K.sem("sw_ready")
    kw_ready = K.sem("kw_ready")
    nd_psum = K.sem("nd_psum")
    nd_taken = K.sem("nd_taken")
    c_psum = K.sem("c_psum")
    c_ready = K.sem("c_ready")
    v1_ready = K.sem("v1_ready")
    done_b = K.sem("done_b")

    def mixers(l):
        with nc.Block() as block:
            @block.sync
            def _(sp):
                sp.dma_start(cos_sin[HD:QK, :, :], a["cos_sin"]).then_inc(rows_load, 16)
                sp.dma_start(cos_sin[QK:P, 1, :], a["cos_sin"][:, 1, :]).then_inc(rows_load, 16)
                sp.dma_start(gate_b[:, :], a["gate_b"][l]).then_inc(rows_load, 16)
                loads = [(m0[:, :], a["m0"][l]), (sel8[:, :, :], a["sel8"]),
                         (maskb[:, :, :], a["maskb"]), (ident_b[:, :], a["ident_b"]), (wsT[:, :, :], a["wsT"][l]), (cmb[:, :], a["cmb"][l]),
                         (normg[:, :, :], a["normg"][l].partition_broadcast(P)), (cn[:, :, 1, :, :], a["cn0"][l]),
                         (ckvT[:, :, P:2 * P], a["cacheT"][l]), (krT[HD:QK, P:2 * P], a["kr_cacheT"][l])]
                for dst, src in loads:
                    sp.dma_start(dst, src).then_inc(b_load, 16)
                for dst, name in ((wuq, "wuq"), (wuk, "wuk"), (wuv, "wuv")):
                    sp.dma_start(dst[:, :, :], a[name][l]).then_inc(c_load, 16)
                sp.wait_ge(rows_load, 48)
                sp.wait_ge(b_load, 16 * 10)
                sp.wait_ge(normed, NT)
                sp.dma_start(o["ckv"][l], proj[:, 0, CKV, :]).then_inc(b_out, 16)
                sp.dma_start(o["kr"][l], smallT[HD:QK, 0, 0:P]).then_inc(b_out, 16)
                sp.wait_ge(c_ready, 2 * 1)
                sp.dma_start(o["cn"][l], cn[:, :, 5, :, :]).then_inc(b_out, 16)
                sp.dma_start(o["m"][l], r_m[:, :]).then_inc(b_out, 16)
                sp.wait_ge(b_out, 64)
                sp.wait_ge(c_load, 48)

            @block.tensor
            def _(pe):
                for t in range(NT):
                    b = 2 * (t % 2)
                    if t >= 2:
                        pe.wait_ge(kq_taken, t - 1)
                    pe.transpose(ps[:, b, 0:P], proj[:, t, MK, 0:P], ident[:, :])
                    pe.transpose(ps[:, b, P:2 * P], proj[:, t, MK, P:2 * P], ident[:, :]).then_inc(kq_psum, 1)
                for t in range(NT):
                    pe.wait_ge(normed, t + 1)
                    if t >= 2:
                        pe.wait_ge(lat_taken, t - 1)
                    for i, (c, h) in enumerate(((CQ, 0), (CQ, 1), (CKV, 0), (CKV, 1))):
                        ins = pe.transpose(ps[:, 4 + t % 2, i * P:(i + 1) * P], proj[:, t, c, h * P:(h + 1) * P], ident[:, :])
                    ins.then_inc(lat_psum, 1)
                pe.wait_ge(b_load, 16 * 10)
                for t in range(NT):
                    if t >= 2:
                        pe.wait_ge(sgu_taken, t - 1)
                    for g in range(H):
                        ins = pe.matmul(ps[:, 6 + t % 2, g * HD:(g + 1) * HD], wsT[:, g, :],
                                        proj[:, t, CV, g * HD:(g + 1) * HD], start=True, stop=True)
                    ins.then_inc(sgu_psum, 1)
                pe.wait_ge(kq_taken, NT)
                pe.wait_ge(rows_exp, 2)
                for q in range(4):
                    for t in range(NT):
                        at = ((q % 2) * NT + t) * ROWS
                        pe.transpose(ps[:, q // 2, at:at + ROWS], rowq[:, q, t * P:(t + 1) * P], ident[0:ROWS, 0:ROWS])
                for r in range(8):
                    ins = pe.matmul(ps[:, 2, r * NT:(r + 1) * NT], sel8[:, r, :], r_dec[:, :], start=True, stop=True)
                ins.then_inc(cols_psum, 1)
                pe.wait_ge(cols_taken, 1)
                pe.wait_ge(v1_ready, 2)
                pe.wait_ge(lat_taken, NT)
                pe.wait_ge(sgu_taken, NT)

                def tile(n):
                    s, d = n // 2, n % 2
                    return s if d == 0 else (NT - s) % NT

                def weights_and_scores(n):
                    t, d = tile(n), n % 2
                    span = slice(t * P, (t + 1) * P)
                    if n >= 2:
                        pe.wait_ge(w_exp, n - 1)
                    for m in range(H):
                        h = (m % 2) * 2 + m // 2
                        at_m = ps[:, d, m * P:(m + 1) * P]
                        pe.matmul(at_m, ident_b[:, :], maskb[:, d, :], start=True, stop=False)
                        ins = pe.matmul(at_m, sel8[:, d * H + h, :], r_u[:, span], start=False, stop=True)
                    ins.then_inc(w_psum, 1)
                    if n >= 1:
                        pe.wait_ge(sw_ready, n)
                    for m in range(H):
                        hp, hh = m // 2, m % 2
                        part = slice(hp * HD, (hp + 1) * HD)
                        ins = pe.matmul(ps[:, 2 + hp, hh * P:(hh + 1) * P], mkT[part, hh, span], mqT[part, hh, span],
                                        start=True, stop=True)
                    ins.then_inc(st_psum, 1)

                weights_and_scores(0)
                for n in range(2 * NT):
                    s, d, t = n // 2, n % 2, tile(n)
                    span = slice(t * P, (t + 1) * P)
                    if n + 1 < 2 * NT:
                        weights_and_scores(n + 1)
                    pe.wait_ge(sw_ready, n + 1)
                    if n >= 1:
                        pe.wait_ge(nd_taken, n)
                    if s >= 2:
                        pe.wait_ge(c_ready, n - 1)
                    for m in range(H):
                        hp, hh = m // 2, m % 2
                        h = hh * 2 + hp
                        part = slice(hp * HD, (hp + 1) * HD)
                        pe.matmul(ps[:, 4, h * (HD + 1):(h + 1) * (HD + 1)], swT[:, d, m * P:(m + 1) * P],
                                  v1[:, t, h, :], start=True, stop=True)
                    for m in range(H):
                        hp, hh = m // 2, m % 2
                        part = slice(hp * HD, (hp + 1) * HD)
                        ins = pe.matmul(ps[:, 5 + hp, hh * (HD + 1):(hh + 1) * (HD + 1)], mqT[part, hh, span],
                                        cn[part, d, s, hh, :], start=True, stop=True)
                    ins.then_inc(nd_psum, 1)
                    if s < NT - 1:
                        pe.wait_ge(kw_ready, n + 1)
                        if n >= 1:
                            pe.wait_ge(c_ready, n)
                        for m in range(H):
                            hp, hh = m // 2, m % 2
                            h = hh * 2 + hp
                            ins = pe.matmul(ps[hp * HD:(hp + 1) * HD, 7, hh * (HD + 1):(hh + 1) * (HD + 1)],
                                            kw[:, d, h * HD:(h + 1) * HD], v1[:, t, h, :], start=True, stop=True)
                        ins.then_inc(c_psum, 1)

            @block.scalar
            def _(act):
                for t in range(NT):
                    ins = act.activation(v1[:, t, :, 0:HD], proj[:, t, MV, :].rearrange("p (h e) -> p h e", h=H), ACT.Copy)
                ins.then_inc(v1_ready, 1)
                for t in range(NT):
                    act.wait_ge(kq_psum, t + 1)
                    act.activation(mkT[:, :, t * P:(t + 1) * P], ps[:, 2 * (t % 2), 0:2 * P].rearrange("p (a b) -> p a b", a=2),
                                   ACT.Copy).then_inc(kq_taken, 1)
                act.wait_ge(nf_ready, 1)
                act.activation(r_e[:, :], r_e[:, :], ACT.Exp).then_inc(log_ready, 1)
                act.wait_ge(log_ready, 1)
                act.activation(r_e[:, :], r_e[:, :], ACT.Ln, bias=1.0).then_inc(log_ready, 1)
                act.wait_ge(b_load, 16 * 10)
                for t in range(NT):
                    act.wait_ge(lat_psum, t + 1)
                    kt = 0 if t == 0 else t + 1
                    act.activation(cqT[:, :, t * P:(t + 1) * P], ps[:, 4 + t % 2, 0:2 * P].rearrange("p (a b) -> p a b", a=2), ACT.Copy)
                    act.activation(ckvT[:, :, kt * P:(kt + 1) * P],
                                   ps[:, 4 + t % 2, 2 * P:4 * P].rearrange("p (a b) -> p a b", a=2),
                                   ACT.Copy).then_inc(lat_taken, 1)
                act.wait_ge(rows_in, 1)
                act.activation(rowq[:, 1:4, :], rowq[:, 1:4, :], ACT.Exp).then_inc(rows_exp, 1)
                act.activation(r_dec[:, :], r_dec[:, :], ACT.Exp).then_inc(rows_exp, 1)
                act.wait_ge(cols_taken, 1)
                for n in range(2 * NT):
                    s, d = n // 2, n % 2
                    t = s if d == 0 else (NT - s) % NT
                    act.wait_ge(w_psum, n + 1)
                    if n >= 2:
                        act.wait_ge(sw_ready, n - 1)
                    for m in range(H):
                        h = (m % 2) * 2 + m // 2
                        ins = act.activation(wT[:, d, m * P:(m + 1) * P], ps[:, d, m * P:(m + 1) * P], ACT.Exp,
                                             bias=cols[:, R_A * NT + t, 32 * d + h:32 * d + h + 1])
                    ins.then_inc(w_exp, 1)

            @block.vector
            def _(dve):
                link = chain_of(dve, b_chain)
                dve.memset(v1[:, :, :, HD:HD + 1], 1.0).then_inc(v1_ready, 1)
                dve.memset(cn[:, :, 0, :, :], 0.0)
                dve.memset(r_b[:, :], 0.0)
                dve.memset(r_u[:, :], 0.0)
                dve.memset(r_prev[:, :], 0.0)
                dve.memset(r_end[:, :], 0.0)
                link(dve.memset(r_m[:, :], 0.0))
                dve.wait_ge(rows_load, 48)
                dve.tensor_scalar(r_i[:, :], smallT[0:ROWS, 0, :], gate_b[:, 0:1], None, ALU.add)
                link(dve.tensor_scalar(r_f[:, :], smallT[0:ROWS, 1, :], gate_b[:, 1:2], None, ALU.add))
                dve.scalar_tensor_tensor(r_e[:, :], r_f[:, :], -1.0, r_f[:, :], ALU.mult, ALU.min).then_inc(nf_ready, 1)
                turning = xn[HD:QK, 1, 0:NS * P]
                dve.tensor_copy(krT[HD:QK, 0:P], smallT[HD:QK, 0, 0:P])
                dve.tensor_tensor(krT[HD:QK, 2 * P:], smallT[HD:QK, 0, P:], cos_sin[HD:QK, 0, :], ALU.mult)
                link(dve.tensor_tensor(turning, smallT[HD:QK, 1, P:], cos_sin[HD:QK, 1, :], ALU.mult))
                link(dve.tensor_tensor(krT[HD:QK, 2 * P:], krT[HD:QK, 2 * P:], turning, ALU.add))
                dve.wait_ge(b_load, 16 * 10)
                dve.wait_ge(root15, 1)
                link(dve.reciprocal(rstd[:, 0:15], rstd[:, 0:15]))
                for t in range(NT):
                    for i, c in enumerate((CV, CQ, CKV)):
                        ins = dve.scalar_tensor_tensor(proj[:, t, c, :], proj[:, t, c, :], rstd[:, 3 * t + i:3 * t + i + 1],
                                                       normg[:, i, :], ALU.mult, ALU.mult)
                    ins.then_inc(normed, 1)
                dve.wait_ge(log_ready, 2)
                link(dve.scalar_tensor_tensor(r_f[:, :], r_f[:, :], 0.0, r_e[:, :], ALU.min, ALU.subtract))
                fwd, bwd_rows = slice(0, H), slice(32, 32 + H)
                for lo, hi in ((0, P), (P, T)):
                    dve.tensor_tensor_scan(r_b[fwd, lo:hi], one_col[fwd, :].to_broadcast([H, hi - lo]), r_f[fwd, lo:hi], 0.0, ALU.mult, ALU.add)
                    rv = slice(hi - 1, lo - 1 if lo else None, -1)
                    link(dve.tensor_tensor_scan(r_b[bwd_rows, rv], one_col[bwd_rows, :].to_broadcast([H, hi - lo]), r_f[bwd_rows, rv], 0.0,
                                                ALU.mult, ALU.add))
                link(dve.tensor_tensor(rowq[:, R_A, :], r_i[:, :], r_b[:, :], ALU.subtract))
                for lo, hi in ((0, P), (P, T)):
                    rv = slice(hi - 1, lo - 1 if lo else None, -1)
                    dve.tensor_tensor_scan(r_u[fwd, lo:hi], rowq[fwd, R_A, lo:hi], rowq[fwd, R_A, lo:hi],
                                           m0[fwd, 0:1] if lo else 0.0, ALU.max, ALU.max)
                    link(dve.tensor_tensor_scan(r_u[bwd_rows, rv], rowq[bwd_rows, R_A, rv], rowq[bwd_rows, R_A, rv],
                                                m0[bwd_rows, 0:1] if lo else 0.0, ALU.max, ALU.max))
                dve.tensor_copy(r_prev[fwd, 1:2], m0[fwd, :])
                dve.tensor_copy(r_prev[fwd, 2:NT], r_u[fwd, 2 * P - 1:T - P:P])
                dve.tensor_copy(r_end[fwd, :], r_u[fwd, P - 1:T:P])
                dve.tensor_copy(r_prev[bwd_rows, NT - 1:NT], m0[bwd_rows, :])
                dve.tensor_copy(r_prev[bwd_rows, 1:NT - 1], r_u[bwd_rows, 2 * P:T:P])
                dve.tensor_copy(r_end[bwd_rows, :], r_u[bwd_rows, 0:T:P])
                dve.tensor_tensor(r_m[fwd, :], r_b[fwd, P - 1:P], r_u[fwd, P - 1:P], ALU.add)
                link(dve.tensor_tensor(r_m[bwd_rows, :], r_b[bwd_rows, 0:1], r_u[bwd_rows, 0:1], ALU.add))

                def tiles(ap):
                    return ap.rearrange("p (t s) -> p t s", t=NT)

                dve.tensor_tensor(tiles(rowq[:, R_WK, :]), tiles(rowq[:, R_A, :]), col(r_end[:, :], P), ALU.subtract)
                dve.tensor_tensor(tiles(rowq[:, R_WIN, :]), col(r_prev[:, :], P), tiles(r_u[:, :]), ALU.subtract)
                dve.scalar_tensor_tensor(rowq[:, R_EM, :], r_b[:, :], -1.0, r_u[:, :], ALU.mult, ALU.subtract)
                link(dve.tensor_tensor(r_dec[:, :], r_prev[:, :], r_end[:, :], ALU.subtract))
                link(dve.tensor_scalar(r_u[:, :], r_u[:, :], -1.0, None, ALU.mult))
                dve.sem_inc(rows_in, 1)
                for t in range(NT):
                    dve.wait_ge(sgu_psum, t + 1)
                    for g in range(H):
                        span = slice(g * HD, (g + 1) * HD)
                        ins = dve.scalar_tensor_tensor(mixed[:, t, 256 + g * HD:256 + (g + 1) * HD], ps[:, 6 + t % 2, span],
                                                       cmb[:, g:g + 1], proj[:, t, CU, span], ALU.add, ALU.mult)
                    ins.then_inc(sgu_taken, 1)
                dve.wait_ge(cols_psum, 1)
                link(dve.tensor_copy(cols[:, 0:2 * NT, :], ps[:, 0, 0:2 * NT * ROWS].rearrange("p (a b) -> p a b", b=ROWS)))
                link(dve.tensor_copy(cols[:, 2 * NT:, :], ps[:, 1, 0:2 * NT * ROWS].rearrange("p (a b) -> p a b", b=ROWS)))
                link(dve.tensor_copy(dec[:, :, :], ps[:, 2, 0:8 * NT].rearrange("p (a b) -> p a b", b=NT)))
                dve.sem_inc(cols_taken, 1)
                def heads(ap):
                    return ap.rearrange("p (h e) -> p h e", h=H)

                def pair(ap):
                    return ap.rearrange("p (a b) -> p a b", a=2)

                def place(n):
                    s, d = n // 2, n % 2
                    return s, d, (s if d == 0 else (NT - s) % NT)

                def weighted(n):
                    s, d, t = place(n)
                    dve.wait_ge(w_exp, n + 1)
                    dve.wait_ge(st_psum, n + 1)
                    if n >= 2:
                        dve.wait_ge(nd_psum, n - 1)
                    dve.scalar_tensor_tensor(pair(swT[:, d, :]), ps[:, 2:4, 0:2 * P], HD ** -0.5, pair(wT[:, d, :]),
                                             ALU.mult, ALU.mult).then_inc(sw_ready, 1)
                    if s < NT - 1:
                        if n >= 2:
                            dve.wait_ge(c_psum, n - 1)
                        dve.scalar_tensor_tensor(heads(kw[:, d, :]), heads(proj[:, t, MK, :]), HD ** -0.5,
                                                 col(cols[:, R_WK * NT + t, 32 * d:32 * d + H], HD), ALU.mult,
                                                 ALU.mult).then_inc(kw_ready, 1)

                weighted(0)
                for n in range(2 * NT):
                    s, d, t = place(n)
                    if n + 1 < 2 * NT:
                        weighted(n + 1)
                    dve.wait_ge(nd_psum, n + 1)
                    win = cols[:, R_WIN * NT + t, 32 * d:32 * d + H].rearrange("p (b a) -> p a b", a=2)
                    link(dve.tensor_tensor(nd[:, :, :].rearrange("p (b a) e -> p a b e", a=2),
                                           ps[:, 5:7, 0:2 * (HD + 1)].rearrange("p a (b e) -> p a b e", b=2),
                                           col(win, HD + 1), ALU.mult))
                    link(dve.tensor_tensor(nd[:, :, :], ps[:, 4, 0:H * (HD + 1)].rearrange("p (h e) -> p h e", h=H),
                                           nd[:, :, :], ALU.add))
                    dve.sem_inc(nd_taken, 1)
                    link(dve.scalar_tensor_tensor(dd[:, 0, :], nd[:, :, HD], -1.0, nd[:, :, HD], ALU.mult, ALU.max))
                    link(dve.tensor_tensor(dd[:, 1, :], dd[:, 0, :], cols[:, R_EM * NT + t, 32 * d:32 * d + H], ALU.max))
                    link(dve.reciprocal(dd[:, 0, :], dd[:, 1, :]))
                    out = mixed[:, t, 0:256] if d == 0 else bwd[:, t, :]
                    link(dve.tensor_tensor(heads(out), nd[:, :, 0:HD], col(dd[:, 0, :], HD), ALU.mult))
                    if s < NT - 1:
                        dve.wait_ge(c_psum, n + 1)
                        to = 5 if s == 0 else s + 1
                        for m in range(H):
                            hp, hh = m // 2, m % 2
                            h = hh * 2 + hp
                            part = slice(hp * HD, (hp + 1) * HD)
                            ins = dve.scalar_tensor_tensor(cn[part, d, to, hh, :], cn[part, d, s, hh, :],
                                                           dec[part, d * H + h, t:t + 1],
                                                           ps[part, 7, hh * (HD + 1):(hh + 1) * (HD + 1)], ALU.mult, ALU.add)
                        ins.then_inc(c_ready, 1)
                link(dve.tensor_tensor(mixed[:, :, 0:256], mixed[:, :, 0:256], bwd[:, :, :], ALU.add))
                dve.wait_ge(sig_done, 1)
                link(dve.tensor_tensor(mixed[:, :, 0:256], mixed[:, :, 0:256], proj[:, :, MO, :], ALU.mult))

    wq_slot = [K.sem(f"wq_slot{i}") for i in range(2)]
    wout_slot = [K.sem(f"wout_slot{i}") for i in range(2)]
    wout_high = K.sem("wout_high")
    wout_split = K.sem("wout_split")
    q_psum = K.sem("q_psum")
    q_act = K.sem("q_act")
    q_dve = K.sem("q_dve")
    k_psum = K.sem("k_psum")
    k_act = K.sem("k_act")
    kr_ready = K.sem("kr_ready")
    v_psum = K.sem("v_psum")
    v_dve = K.sem("v_dve")
    s_psum = K.sem("s_psum")
    max_ready = K.sem("max_ready")
    p_ready = K.sem("p_ready")
    pt_psum = K.sem("pt_psum")
    pt_taken = K.sem("pt_taken")
    o_psum = K.sem("o_psum")
    o_taken = K.sem("o_taken")
    mt_psum = K.sem("mt_psum")
    mt_high = K.sem("mt_high")
    mt_low = K.sem("mt_low")
    y_psum = K.sem("y_psum")
    y_taken = K.sem("y_taken")
    x_mixed = [K.sem(f"x_mixed{c}") for c in range(4)]
    c_squares = K.sem("c_squares")
    c_chain = K.sem("c_chain")

    def attention(l):
        units = [(h, t) for h in range(AH) for t in range(NT)]

        def turned_mix(t):
            b = 2 * (t % 2)
            return ps[:, b:b + 2, :].rearrange("p a (c d) -> p (a c) d", d=P)

        def keys(t):
            return (0, P, [0]) if t == 0 else (P, KT * P, list(range(1, KT)))

        with nc.Block() as block:
            @block.sync
            def _(sp):
                sp.dma_start(wq[:, 1, :, :], a["wq"][l, 0]).then_inc(wq_slot[0], 16)
                for c in range(4):
                    if c >= 2:
                        sp.wait_ge(wout_split, c - 1)
                    sp.dma_start(wout[:, c % 2, :, :], a["w_out"][l, c]).then_inc(wout_slot[c % 2], 16)

            @block.tensor
            def _(pe):
                for h in range(AH):
                    b = 2 * (h % 2)
                    if h >= 2:
                        pe.wait_ge(q_act, h - 1)
                        pe.wait_ge(q_dve, h - 1)
                    for k in range(2):
                        pe.matmul(ps[:, b, :], wuq[:, k, h * P:(h + 1) * P], cqT[:, k, P:T], start=(k == 0), stop=(k == 1))
                    for k in range(2):
                        ins = pe.matmul(ps[0:QK, b + 1, 0:P], wuq[:, k, h * P:h * P + QK], cqT[:, k, 0:P],
                                        start=(k == 0), stop=(k == 1))
                    ins.then_inc(q_psum, 1)
                pe.wait_ge(q_act, AH)
                pe.wait_ge(q_dve, AH)
                for h in range(AH):
                    b = 2 * (h % 2)
                    if h >= 2:
                        pe.wait_ge(k_act, h - 1)
                    for k in range(2):
                        pe.matmul(ps[0:HD, b, :], wuk[:, k, h * HD:(h + 1) * HD], ckvT[:, k, 0:512], start=(k == 0), stop=(k == 1))
                    for k in range(2):
                        ins = pe.matmul(ps[0:HD, b + 1, 0:256], wuk[:, k, h * HD:(h + 1) * HD], ckvT[:, k, 512:768],
                                        start=(k == 0), stop=(k == 1))
                    ins.then_inc(k_psum, 1)
                for t in range(KT):
                    if t >= 2:
                        pe.wait_ge(v_dve, t - 1)
                    for k in range(2):
                        ins = pe.matmul(ps[:, 4 + t % 2, :], ckvT[:, k, t * P:(t + 1) * P], wuv[:, k, :], start=(k == 0), stop=(k == 1))
                    ins.then_inc(v_psum, 1)
                pe.wait_ge(k_act, AH)
                pe.wait_ge(v_dve, KT)
                pe.wait_ge(kr_ready, 1)

                def scores(n):
                    h, t = units[n]
                    lo, hi, _ = keys(t)
                    b = 2 * (n % 2)
                    if n >= 2:
                        pe.wait_ge(p_ready, n - 1)
                    q = qT[:, h, t * P:(t + 1) * P]
                    mid = min(hi, lo + 512)
                    ins = pe.matmul(ps[:, b, 0:mid - lo], q, kT[0:QK, h, lo:mid], start=True, stop=True)
                    if hi > mid:
                        ins = pe.matmul(ps[:, b + 1, 0:hi - mid], q, kT[0:QK, h, mid:hi], start=True, stop=True)
                    ins.then_inc(s_psum, 1)

                def turn(n):
                    h, t = units[n]
                    pe.wait_ge(p_ready, n + 1)
                    if n >= 1:
                        pe.wait_ge(pt_taken, n)
                    for i in range(len(keys(t)[2])):
                        ins = pe.transpose(ps[:, 4 + i // 4, (i % 4) * P:(i % 4 + 1) * P], prob[:, n % 2, i * P:(i + 1) * P], ident[:, :])
                    ins.then_inc(pt_psum, 1)

                def attend(n):
                    h, t = units[n]
                    pe.wait_ge(pt_taken, n + 1)
                    if n >= 2:
                        pe.wait_ge(o_taken, n - 1)
                    tiles = keys(t)[2]
                    for i, kt in enumerate(tiles):
                        ins = pe.matmul(ps[:, 6 + n % 2, 0:HD], probT[:, n % 2, i * P:(i + 1) * P], val[:, kt, h * HD:(h + 1) * HD],
                                        start=(i == 0), stop=(i == len(tiles) - 1))
                    ins.then_inc(o_psum, 1)

                scores(0)
                for n in range(len(units)):
                    if n + 1 < len(units):
                        scores(n + 1)
                    turn(n)
                    if n >= 1:
                        attend(n - 1)
                attend(len(units) - 1)
                pe.wait_ge(o_taken, len(units))
                for t in range(NT):
                    if t >= 2:
                        pe.wait_ge(mt_low, t - 1)
                    for k in range(KD):
                        ins = pe.transpose(ps[:, 2 * (t % 2) + k // 4, (k % 4) * P:(k % 4 + 1) * P], mixed[:, t, k * P:(k + 1) * P], ident[:, :])
                    ins.then_inc(mt_psum, 1)
                for c in range(4):
                    pe.wait_ge(wout_split, c + 1)
                    for t in range(NT):
                        n = c * NT + t
                        if c == 0:
                            pe.wait_ge(mt_low, t + 1)
                        if n >= 4:
                            pe.wait_ge(y_taken, n - 3)
                        for k in range(KD):
                            for i, (ml, wl) in enumerate(PASSES):
                                ins = pe.matmul(ps[:, 4 + n % 4, 0:256], (mix_hi, mix_lo)[ml][:, k, t * P:(t + 1) * P],
                                                (wout_hi, wout_lo)[wl][:, c % 2, k, :],
                                                start=(k == 0 and i == 0), stop=(k == KD - 1 and i == 2))
                        ins.then_inc(y_psum, 1)

            @block.scalar
            def _(act):
                for h in range(AH):
                    b = 2 * (h % 2)
                    act.wait_ge(q_psum, h + 1)
                    act.activation(qT[0:HD, h, P:T], ps[0:HD, b, :], ACT.Copy)
                    act.activation(qT[:, h, 0:P], ps[0:QK, b + 1, 0:P], ACT.Copy).then_inc(q_act, 1)
                for h in range(AH):
                    b = 2 * (h % 2)
                    act.wait_ge(k_psum, h + 1)
                    act.activation(kT[0:HD, h, 0:512], ps[0:HD, b, :], ACT.Copy)
                    act.activation(kT[0:HD, h, 512:768], ps[0:HD, b + 1, 0:256], ACT.Copy).then_inc(k_act, 1)
                for n, (h, t) in enumerate(units):
                    lo, hi, _ = keys(t)
                    act.wait_ge(max_ready, n + 1)
                    if n >= 2:
                        act.wait_ge(pt_psum, n - 1)
                    act.activation(prob[:, n % 2, 0:hi - lo],
                                   ps[:, 2 * (n % 2):2 * (n % 2) + 2, :].rearrange("p a b -> p (a b)")[:, 0:hi - lo], ACT.Exp,
                                   bias=amax[:, n % 4, 1:2], scale=SCALE, accum_out=amax[:, n % 4, 2:3]).then_inc(p_ready, 1)

                def high_wout(c):
                    act.wait_ge(wout_slot[c % 2], 16 * (c // 2 + 1))
                    if c >= 2:
                        act.wait_ge(y_psum, NT * (c - 1))
                    act.activation(wout_hi[:, c % 2, :, :], wout[:, c % 2, :, :], ACT.Copy).then_inc(wout_high, 1)

                act.wait_ge(o_taken, len(units))
                high_wout(0)
                for t in range(NT):
                    act.wait_ge(mt_psum, t + 1)
                    act.activation(mix_hi[:, :, t * P:(t + 1) * P], turned_mix(t), ACT.Copy).then_inc(mt_high, 1)
                high_wout(1)
                high_wout(2)
                high_wout(3)
                for t in range(NT):
                    for c in range(4):
                        act.wait_ge(x_mixed[c], t + 1)
                    squares(act, c_squares, t, t, mixed[:, 0, :])

            @block.gpsimd
            def _(pool):
                for c in range(4):
                    pool.wait_ge(wout_high, c + 1)
                    pool.tensor_tensor(wout_lo[:, c % 2, :, :], wout[:, c % 2, :, :], wout_hi[:, c % 2, :, :],
                                       ALU.subtract).then_inc(wout_split, 1)

            @block.vector
            def _(dve):
                link = chain_of(dve, c_chain)
                for h in range(AH):
                    b = 2 * (h % 2)
                    dve.wait_ge(q_psum, h + 1)
                    if h >= 2:
                        dve.wait_ge(q_dve, h - 1)
                    turn = rot[h % 2]
                    dve.tensor_tensor(turn[HD:QK, 0, :], ps[HD:QK, b, :], cos_sin[HD:QK, 0, :], ALU.mult)
                    link(dve.tensor_tensor(turn[HD:QK, 1, :], ps[QK:P, b, :], cos_sin[QK:P, 1, :], ALU.mult))
                    dve.tensor_tensor(qT[HD:QK, h, P:T], turn[HD:QK, 0, :], turn[HD:QK, 1, :], ALU.add).then_inc(q_dve, 1)
                dve.tensor_copy(kT[HD:QK, :, :], krT[HD:QK, :].unsqueeze(1).to_broadcast([ROPE, AH, KT * P])).then_inc(kr_ready, 1)
                for t in range(KT):
                    dve.wait_ge(v_psum, t + 1)
                    dve.tensor_copy(val[:, t, :], ps[:, 4 + t % 2, :]).then_inc(v_dve, 1)

                def maxima(n):
                    h, t = units[n]
                    lo, hi, _ = keys(t)
                    dve.wait_ge(s_psum, n + 1)
                    if n >= 4:
                        dve.wait_ge(o_taken, n - 3)
                    link(dve.tensor_reduce(amax[:, n % 4, 0:1],
                                           ps[:, 2 * (n % 2):2 * (n % 2) + 2, :].rearrange("p a b -> p (a b)")[:, 0:hi - lo], AX.X, ALU.max))
                    dve.tensor_scalar(amax[:, n % 4, 1:2], amax[:, n % 4, 0:1], -SCALE, None, ALU.mult).then_inc(max_ready, 1)

                def turned(n):
                    dve.wait_ge(pt_psum, n + 1)
                    if n >= 2:
                        dve.wait_ge(o_psum, n - 1)
                    tiles = len(keys(units[n][1])[2])
                    dve.tensor_copy(probT[:, n % 2, 0:tiles * P],
                                    ps[:, 4:6, :].rearrange("p a b -> p (a b)")[:, 0:tiles * P]).then_inc(pt_taken, 1)

                def finish(n):
                    h, t = units[n]
                    dve.wait_ge(p_ready, n + 1)
                    link(dve.reciprocal(amax[:, n % 4, 3:4], amax[:, n % 4, 2:3]))
                    dve.wait_ge(o_psum, n + 1)
                    dve.tensor_scalar(mixed[:, t, 512 + h * HD:512 + (h + 1) * HD], ps[:, 6 + n % 2, 0:HD],
                                      amax[:, n % 4, 3:4], None, ALU.mult).then_inc(o_taken, 1)
                    dve.wait_ge(o_taken, n + 1)

                maxima(0)
                for n in range(len(units)):
                    if n + 1 < len(units):
                        maxima(n + 1)
                    turned(n)
                    if n >= 1:
                        finish(n - 1)
                finish(len(units) - 1)
                for t in range(NT):
                    dve.wait_ge(mt_high, t + 1)
                    dve.tensor_tensor(mix_lo[:, :, t * P:(t + 1) * P], turned_mix(t), mix_hi[:, :, t * P:(t + 1) * P],
                                      ALU.subtract).then_inc(mt_low, 1)
                for c in range(4):
                    for t in range(NT):
                        n, v = c * NT + t, (0 if t == 0 else 1)
                        span = slice(c * 256, (c + 1) * 256)
                        dve.wait_ge(y_psum, n + 1)
                        link(dve.tensor_tensor(xn[:, n % 2, 0:256], ps[:, 4 + n % 4, 0:256], gate1[:, v, span], ALU.mult))
                        dve.sem_inc(y_taken, 1)
                        dve.tensor_tensor(x[:, t, span], x[:, t, span], xn[:, n % 2, 0:256], ALU.add).then_inc(x_mixed[c], 1)

    s6 = ExitStack()
    h_hi = sb("h_hi", [P, KD, T], F32R, stack=s6)
    h_lo = sb("h_lo", [P, KD, T], F32R, stack=s6)
    s65 = ExitStack()
    slots = sb("slots", [P, 3, T], stack=s65)
    s7 = ExitStack()
    h2T = sb("h2T", [P, KD, T], stack=s7)
    xn2 = sb("xn2", [P, 2, D], stack=s7)
    wq_hi = sb("wq_hi", [P, 2, KD, P], F32R, stack=s7)
    wq_lo = sb("wq_lo", [P, 2, KD, P], F32R, stack=s7)
    skT = sb("skT", [P, 2, NKEYS], stack=s7)
    pqT = sb("pqT", [P, 2, T], stack=s7)
    topv = sb("topv", [P, NT, RH, 2, TOP], stack=s7)
    topi = sb("topi", [P, NT, RH, 2, TOP], U32, stack=s7)
    topf = sb("topf", [P, NT, RH, 2, TOP], BF16, stack=s7)
    rest1 = sb("rest1", [P, NT, NKEYS], stack=s7)
    rest = sb("rest", [P, NT, NCAND], stack=s7)
    cand = sb("cand", [P, 2, NT, NCAND], stack=s7)
    best = sb("best", [P, NT, RH, TOP], stack=s7)
    pos = sb("pos", [P, NT, SLOTS], U32, stack=s7)
    pos12 = sb("pos12", [P, 2, NT, SLOTS], U32, stack=s7)
    posf = sb("posf", [P, 2, NT, SLOTS], BF16, stack=s7)
    posw = sb("posw", [P, 4, NT, SLOTS], BF16, stack=s7)
    gsum = sb("gsum", [P, 2, NT, RH], stack=s7)
    iota16 = sb("iota16", [P, TOP], BF16, stack=s7)
    hot = sb("hot", [P, 3, SLOTS, TOP], BF16, stack=s7)
    wq = sb("wq", [P, 2, KD, 512], stack=s7)
    keysel = pqT[:, :, :].rearrange("p a b -> p (a b)").rearrange("p (t h s) -> p t h s", t=NT, h=2)
    s7.close()
    s8 = ExitStack()
    gmat = sb("gmat", [P, 2, NKEYS, GB], stack=s8)
    iota = sb("iota", [P, NKEYS], stack=s8)
    stage = sb("stage", [P, 3, 2 * GB], stack=s8)
    hot1 = sb("hot1", [P, HOTS, 4, NKEYS], stack=s8)
    hot2 = sb("hot2", [P, HOTS, 4, NKEYS], stack=s8)
    s8.close()
    s65.close()
    s9 = ExitStack()
    a_hi = sb("a_hi", [P, 2, NG, T], F32R, stack=s9)
    a_lo = sb("a_lo", [P, 2, NG, T], F32R, stack=s9)
    y = sb("y", [P, NT, D], stack=s9)
    u_hi = sb("u_hi", [P, 2, KD, P], F32R, stack=s9)
    u_lo = sb("u_lo", [P, 2, KD, P], F32R, stack=s9)
    v_raw = sb("v_raw", [P, 2, D], stack=s9)
    v_hi = sb("v_hi", [P, NG, D], F32R, stack=s9)
    v_lo = sb("v_lo", [P, NG, D], F32R, stack=s9)
    gt = sb("gt", [P, 2, NB, 2, GB], stack=s9)
    u_raw = sb("u_raw", [P, 2, KD, P], stack=s9)
    s9.close()
    s6.close()

    d_load = K.sem("d_load")
    n2 = dict(tp=K.sem("n2_psum"), ta=K.sem("n2_act"), td=K.sem("n2_dve"), rt=K.sem("n2_root"),
              xn=K.sem("n2_xn"), x_n=xn2, hs=K.sem("hi_ready"), ls=K.sem("lo_ready"), hi=h_hi, lo=h_lo,
              whole=lambda t: h2T[:, :, t * P:(t + 1) * P], places=NT)
    hi_ready, lo_ready = n2["hs"], n2["ls"]
    pq_psum = K.sem("pq_psum")
    wq_high = K.sem("wq_high")
    wq_split = K.sem("wq_split")
    pq_taken = K.sem("pq_taken")
    sc_psum = K.sem("sc_psum")
    sc_taken = K.sem("sc_taken")
    d_chain = K.sem("d_chain")
    gate_in = K.sem("gate_in")
    gate_exp = K.sem("gate_exp")
    gate_done = K.sem("gate_done")
    top_step = K.sem("top_step")
    cand_ready = K.sem("cand_ready")
    cand_used = K.sem("cand_used")
    hot_ready = K.sem("hot_ready")
    hot_times = K.sem("hot_times")
    picked = K.sem("picked")
    slot_psum = K.sem("slot_psum")
    slot_taken = K.sem("slot_taken")

    def retrieve(l):
        ring2 = [wq[:, 1, :, :], wq[:, 0, :, :], h2T[:, :, 0:512]]
        rows2 = xn2[0:2, :, 0:512]

        with nc.Block() as block:
            @block.sync
            def _(sp):
                sp.dma_start(skT[:, :, :], a["skT"][l]).then_inc(d_load, 16)
                sp.dma_start(iota16[:, :], a["iota16"]).then_inc(d_load, 16)
                for c in range(1, 4):
                    if c >= 2:
                        sp.wait_ge(wq_split, 4 * (c - 1))
                    sp.dma_start(wq[:, 1 - c % 2, :, :], a["wq"][l, c]).then_inc(wq_slot[c % 2], 16)

                def slot_free(j):
                    if j < 2:
                        sp.wait_ge(wq_split, 12 + 4 * j)
                    else:
                        sp.wait_ge(hi_ready, NT)
                        sp.wait_ge(lo_ready, NT)

                modulation_loads(sp, mod_sems, ring2, rows2, a["ada_w"][l], a["ada_bT"][l], slot_free)

            @block.tensor
            def _(pe):
                normalise(None, None, pe, 1, n2)
                pe.wait_ge(d_load, 32)

                def query(j):
                    pe.wait_ge(wq_split, j + 1)
                    for half in range(2):
                        n = 2 * j + half
                        if j == 0:
                            pe.wait_ge(hi_ready, (NT + 1) // 2 + half * (NT // 2))
                            pe.wait_ge(lo_ready, (NT + 1) // 2 + half * (NT // 2))
                        if n >= 2:
                            pe.wait_ge(pq_taken, n - 1)
                        for k in range(KD):
                            for m, (wl, hl) in enumerate(PASSES):
                                ins = pe.matmul(ps[:, half, 0:HALF], (wq_hi, wq_lo)[wl][:, j % 2, k, :],
                                                (h_hi, h_lo)[hl][:, k, half * HALF:(half + 1) * HALF],
                                                start=(k == 0 and m == 0), stop=(k == KD - 1 and m == 2))
                        ins.then_inc(pq_psum, 1)

                query(0)
                for j in range(2 * RH):
                    if j + 1 < 2 * RH:
                        query(j + 1)
                    pe.wait_ge(pq_taken, 2 * (j + 1))
                    if j >= 2:
                        pe.wait_ge(sc_taken, j - 1)
                    for t in range(NT):
                        b = 2 + 2 * (j % 2) + t // 4
                        ins = pe.matmul(ps[:, b, (t % 4) * P:(t % 4 + 1) * P], pqT[:, j % 2, t * P:(t + 1) * P],
                                        skT[:, j % 2, :], start=True, stop=True)
                    ins.then_inc(sc_psum, 1)
                modulation_products(pe, mod_sems, ring2, rows2)
                for t in range(NT):
                    pe.wait_ge(picked, 2 * t + 2)
                    pe.wait_ge(gate_done, 1)
                    if t >= 2:
                        pe.wait_ge(slot_taken, t - 1)
                    b = 6 + t % 2
                    pe.transpose(ps[:, b, 0:P], keysel[:, t, 0, :], ident[:, :])
                    pe.transpose(ps[:, b, P:2 * P], keysel[:, t, 1, :], ident[:, :])
                    pe.transpose(ps[:, b, 2 * P:3 * P], best[:, t, :, :].rearrange("p h s -> p (h s)"), ident[:, :]).then_inc(slot_psum, 1)

            @block.scalar
            def _(act):
                def first():
                    for j in range(2):
                        act.wait_ge(wq_slot[0], 16)
                        act.activation(wq_hi[:, j, :, :], wq[:, 1, :, j * P:(j + 1) * P], ACT.Copy).then_inc(wq_high, 1)

                normalise(act, None, None, 1, n2, first)

                def high_wq(j):
                    act.wait_ge(wq_slot[j // 4 % 2], 16 * (j // 8 + 1))
                    if j >= 2:
                        act.wait_ge(pq_psum, 2 * (j - 1))
                        act.wait_ge(wq_split, j - 1)
                    act.activation(wq_hi[:, j % 2, :, :], wq[:, 1 - j // 4 % 2, :, (j % 4) * P:(j % 4 + 1) * P],
                                   ACT.Copy).then_inc(wq_high, 1)

                for n in range(4 * RH):
                    j, half = n // 2, n % 2
                    if half == 0 and 1 <= j < 2 * RH - 1:
                        high_wq(j + 1)
                    act.wait_ge(pq_psum, n + 1)
                    if j >= 2:
                        act.wait_ge(sc_psum, j - 1)
                    act.activation(pqT[:, j % 2, half * HALF:(half + 1) * HALF], ps[:, half, 0:HALF], ACT.Copy).then_inc(pq_taken, 1)

                def gate_exponentials(j):
                    if j == 7:
                        act.wait_ge(gate_in, 1)
                        act.activation(best[:, :, :, :], best[:, :, :, :], ACT.Exp).then_inc(gate_exp, 1)

                act.wait_ge(n2["tp"], NT)
                modulation_copies(act, mod_sems, rows2, gate_exponentials)
                for t in range(NT):
                    act.wait_ge(slot_psum, t + 1)
                    act.activation(slots[:, :, t * P:(t + 1) * P], ps[:, 6 + t % 2, 0:3 * P].rearrange("p (a b) -> p a b", a=3),
                                   ACT.Copy).then_inc(slot_taken, 1)

            @block.vector
            def _(dve):
                link = chain_of(dve, d_chain)
                normalise(None, dve, None, 1, dict(n2, link=link))
                step = [0]

                def counted(ins):
                    step[0] += 1
                    ins.then_inc(top_step, 1)
                    return step[0]

                left_read = {}

                def top16(values, v, i, left, name):
                    first = [counted(dve.max(v(t)[:, 0:8], values(t))) for t in range(NT)]
                    cut = []
                    for t in range(NT):
                        dve.wait_ge(top_step, max(first[t], left_read.get((name, t), 1)))
                        counted(dve.max_index(i(t)[:, 0:8], v(t)[:, 0:8], values(t)))
                        cut.append(counted(dve.match_replace(left(t), v(t)[:, 0:8], values(t), -3.0e38)))
                    second = []
                    for t in range(NT):
                        dve.wait_ge(top_step, cut[t])
                        second.append(counted(dve.max(v(t)[:, 8:16], left(t))))
                    for t in range(NT):
                        dve.wait_ge(top_step, second[t])
                        left_read[name, t] = counted(dve.max_index(i(t)[:, 8:16], v(t)[:, 8:16], left(t)))

                def pairs(h):
                    dve.wait_ge(cand_ready, h + 1)
                    top16(lambda t: cand[:, h % 2, t, :], lambda t: best[:, t, h, :],
                          lambda t: pos[:, t, h * TOP:(h + 1) * TOP], lambda t: rest[:, t, :], "rest")
                    dve.wait_ge(top_step, step[0])
                    dve.sem_inc(cand_used, 1)

                for j in range(2 * RH):
                    h, half = j // 2, j % 2
                    b = 2 + 2 * (j % 2)
                    dve.wait_ge(sc_psum, j + 1)
                    top16(lambda t: ps[:, b + t // 4, (t % 4) * P:(t % 4 + 1) * P], lambda t: topv[:, t, h, half, :],
                          lambda t: topi[:, t, h, half, :], lambda t: rest1[:, t, :], "rest1")
                    dve.wait_ge(top_step, step[0])
                    dve.sem_inc(sc_taken, 1)
                    if half == 1 and h >= 1:
                        pairs(h - 1)
                link(dve.tensor_copy(topf[:, :, :, :, :].rearrange("p t h a s -> p (t h a s)"),
                                     topi[:, :, :, :, :].rearrange("p t h a s -> p (t h a s)")))
                pairs(RH - 1)
                link(dve.tensor_copy(gsum[:, 0, :, :].rearrange("p t h -> p (t h)"),
                                     best[:, :, :, 0:1].rearrange("p t h s -> p (t h s)")))
                link(dve.tensor_tensor(best[:, :, :, :].rearrange("p t h s -> p (t h) s"),
                                       best[:, :, :, :].rearrange("p t h s -> p (t h) s"),
                                       col(gsum[:, 0, :, :].rearrange("p t h -> p (t h)"), TOP), ALU.subtract))
                dve.sem_inc(gate_in, 1)
                dve.tensor_scalar(pos12[:, 0, :, :], pos[:, :, :], 3, None, ALU.logical_shift_right)
                dve.tensor_scalar(pos12[:, 1, :, :], pos[:, :, :], 2, None, ALU.logical_shift_right)
                link(dve.tensor_copy(posw[:, 2, :, :], pos[:, :, :]))
                link(dve.tensor_copy(posw[:, 0:2, :, :], pos12[:, :, :, :]))
                eighth, fourth, whole, start = (posw[:, n, :, :] for n in range(4))
                i_at, j_at = posf[:, 0, :, :], posf[:, 1, :, :]
                link(dve.tensor_scalar(eighth, eighth, -1.0, 0.0, ALU.add, ALU.max))
                link(dve.scalar_tensor_tensor(fourth, fourth, -6.0, eighth, ALU.add, ALU.max))
                link(dve.scalar_tensor_tensor(i_at, whole, -48.0, fourth, ALU.add, ALU.max))
                dve.tensor_scalar(eighth, i_at, 8.0, 8.0, ALU.mult, ALU.add)
                link(dve.tensor_scalar(fourth, i_at, 4.0, 24.0, ALU.mult, ALU.add))
                link(dve.scalar_tensor_tensor(eighth, i_at, 16.0, eighth, ALU.mult, ALU.min))
                link(dve.scalar_tensor_tensor(fourth, i_at, 48.0, fourth, ALU.add, ALU.min))
                link(dve.tensor_tensor(start, eighth, fourth, ALU.min))
                link(dve.tensor_tensor(j_at, whole, start, ALU.subtract))

                def one_hot(u):
                    t, half = u // 2, u % 2
                    if u >= 3:
                        dve.wait_ge(picked, u - 2)
                    dve.tensor_tensor(hot[:, u % 3, :, :], col(posf[:, half, t, :], TOP),
                                      iota16[:, :].unsqueeze(1).to_broadcast([P, SLOTS, TOP]), ALU.is_equal).then_inc(hot_ready, 1)

                one_hot(0)
                one_hot(1)
                for u in range(2 * NT):
                    if u + 2 < 2 * NT:
                        one_hot(u + 2)
                    if u == 7:
                        dve.wait_ge(gate_exp, 1)
                        link(dve.tensor_reduce(gsum[:, 0, :, :].rearrange("p t h -> p (t h)"),
                                               best[:, :, :, :].rearrange("p t h s -> p (t h) s"), AX.X, ALU.add))
                        link(dve.reciprocal(gsum[:, 1, :, :], gsum[:, 0, :, :]))
                        link(dve.tensor_tensor(best[:, :, :, :].rearrange("p t h s -> p (t h) s"),
                                               best[:, :, :, :].rearrange("p t h s -> p (t h) s"),
                                               col(gsum[:, 1, :, :].rearrange("p t h -> p (t h)"), TOP), ALU.mult))
                        dve.sem_inc(gate_done, 1)
                    dve.wait_ge(hot_times, u + 1)
                    dve.tensor_reduce(keysel[:, u // 2, u % 2, :], hot[:, u % 3, :, :], AX.X, ALU.add).then_inc(picked, 1)

            @block.gpsimd
            def _(pool):
                def low_wq(j):
                    pool.wait_ge(wq_high, j + 1)
                    pool.tensor_tensor(wq_lo[:, j % 2, :, :], wq[:, 1 - j // 4 % 2, :, (j % 4) * P:(j % 4 + 1) * P],
                                       wq_hi[:, j % 2, :, :], ALU.subtract).then_inc(wq_split, 1)

                for j in range(3):
                    low_wq(j)
                for h in range(RH):
                    for j in range(2 * h + 3, min(2 * h + 5, 2 * RH)):
                        low_wq(j)
                    pool.wait_ge(sc_taken, 2 * h + 2)
                    if h >= 2:
                        pool.wait_ge(cand_used, h - 1)
                    for i, ni, nj, at in STAIRS:
                        ins = pool.tensor_tensor(cand[:, h % 2, :, at:at + ni * nj].rearrange("p t (i j) -> p t i j", j=nj),
                                                 col(topv[:, :, h, 0, i:i + ni], nj),
                                                 topv[:, :, h, 1, 0:nj].unsqueeze(2).to_broadcast([P, NT, ni, nj]), ALU.add)
                    ins.then_inc(cand_ready, 1)
                for u in range(2 * NT):
                    t, half = u // 2, u % 2
                    pool.wait_ge(hot_ready, u + 1)
                    at = hot[:, u % 3, :, :].rearrange("p (h s) j -> p h s j", h=RH)
                    pool.tensor_tensor(at, at, topf[:, t, :, half, :].unsqueeze(2).to_broadcast([P, RH, TOP, TOP]),
                                       ALU.mult).then_inc(hot_times, 1)

    e_load = K.sem("e_load")
    u_in = [K.sem(f"u_in{i}") for i in range(2)]
    staged = K.sem("staged")
    hots_ready = K.sem("hots_ready")
    hots_pool = K.sem("hots_pool")
    hots_act = K.sem("hots_act")
    far = K.sem("far")
    pool_quads = K.sem("pool_quads")
    hots_used = K.sem("hots_used")
    gm_taken = K.sem("gm_taken")
    gm_stored = [K.sem(f"gm_stored{i}") for i in range(2)]

    def gate_matrices(l):
        quads = GB // 4
        turns = NB // 2
        with nc.Block() as block:
            @block.sync
            def _(sp):
                sp.dma_start(iota[:, :], a["iota"]).then_inc(e_load, 16)
                for j in range(2):
                    sp.dma_start(u_raw[:, j, :, :], a["u"][l, j]).then_inc(u_in[j], 16)
                with sp.Fori(0, turns) as i:
                    for b in range(2):
                        sp.wait_ge(gm_taken, i * (2 * quads) + (b + 1) * quads + 8)
                        sp.dma_start(gates_dram[i * 2 + b], gmat[:, 1 - b, :, :].rearrange("p a b -> p (a b)")).then_inc(gm_stored[b], 16)
                sp.wait_ge(gm_stored[0], 16 * turns + 16)

            @block.vector
            def _(dve):
                dve.wait_ge(e_load, 16)
                dve.sem_inc(staged, 1)
                with dve.Fori(0, turns) as i:
                    dve.tensor_copy(stage[:, :, :], slots[:, :, bass.ds(i * (2 * GB), 2 * GB)]).then_inc(staged, 1)
                    dve.wait_ge(staged, i + 2)
                    for q in range(2 * quads):
                        s = q % HOTS
                        dve.wait_ge(hots_used, i * (2 * quads) + q + 1)
                        for r in range(4):
                            n = q * 4 + r
                            if r == 0:
                                dve.tensor_scalar(hot2[:, s, r, :], iota[:, :], stage[:, 1, n:n + 1], None, ALU.is_equal)
                            ins = dve.tensor_scalar(hot1[:, s, r, :], iota[:, :], stage[:, 0, n:n + 1], stage[:, 2, n:n + 1],
                                                    ALU.is_equal, ALU.mult)
                        ins.then_inc(hots_ready, 1)
                    dve.wait_ge(hots_ready, i * (2 * quads) + 2 * quads)
                    dve.wait_ge(hots_pool, i * (2 * quads) + 2 * quads)
                    dve.wait_ge(hots_act, i * (2 * quads) + 2 * quads)

            @block.gpsimd
            def _(pool):
                pool.wait_ge(e_load, 16)
                with pool.Fori(0, turns) as i:
                    pool.wait_ge(staged, i + 2)
                    for q in range(2 * quads):
                        pool.wait_ge(hots_used, i * (2 * quads) + q + 1)
                        pool.sem_inc(pool_quads, 1)
                        for r in range(1, 3):
                            n = q * 4 + r
                            ins = pool.tensor_scalar(hot2[:, q % HOTS, r, :], iota[:, :], stage[:, 1, n:n + 1], None, ALU.is_equal)
                        ins.then_inc(hots_pool, 1)

            @block.tensor
            def _(pe):
                pe.sem_inc(hots_used, HOTS)
                with pe.Fori(0, turns) as i:
                    for q in range(2 * quads):
                        s = q % HOTS
                        pe.wait_ge(hots_ready, i * (2 * quads) + q + 1)
                        pe.wait_ge(hots_pool, i * (2 * quads) + q + 1)
                        pe.wait_ge(hots_act, i * (2 * quads) + q + 1)
                        pe.wait_ge(gm_taken, i * (2 * quads) + q + 1)
                        for r in range(4):
                            ins = pe.matmul(ps[:, q % 8, r * P:(r + 1) * P], hot2[:, s, r, :], hot1[:, s, r, :], start=True, stop=True)
                        ins.then_inc(hots_used, 1)

            @block.scalar
            def _(act):
                act.sem_inc(gm_taken, 8)
                act.sem_inc(gm_stored[0], 16)
                act.sem_inc(gm_stored[1], 16)
                act.wait_ge(e_load, 16)
                with act.Fori(0, turns) as i:
                    def gather(n):
                        b, q = n // quads, n % quads
                        if q == 0:
                            act.wait_ge(gm_stored[b], i * 16 + 16)
                        act.wait_ge(hots_used, i * (2 * quads) + n + 1 + HOTS)
                        act.activation(gmat[:, 1 - b, :, q * 4:(q + 1) * 4], ps[:, n % 8, :].rearrange("p (t k) -> p k t", t=4),
                                       ACT.Copy).then_inc(gm_taken, 1)

                    act.wait_ge(staged, i + 2)
                    for q in range(2 * quads):
                        row = hot2[:, q % HOTS, 3, :]
                        act.wait_ge(hots_used, i * (2 * quads) + q + 1)
                        act.activation(row, iota[:, :], ACT.Square, bias=stage[:, 1, q * 4 + 3:q * 4 + 4], scale=-1.0).then_inc(far, 1)
                        if q >= 2:
                            gather(q - 2)
                        act.wait_ge(far, i * (2 * quads) + q + 1)
                        act.activation(row, row, ACT.Relu, bias=one_col[:, 0:1], scale=-1.0).then_inc(hots_act, 1)
                    gather(2 * quads - 2)
                    gather(2 * quads - 1)

    v_in = [K.sem(f"v_in{i}") for i in range(2)]
    g_in = [K.sem(f"g_in{i}") for i in range(2)]
    u_high = K.sem("u_high")
    u_split = K.sem("u_split")
    v_high = K.sem("v_high")
    v_split = K.sem("v_split")
    hid_psum = K.sem("hid_psum")
    hid_act = K.sem("hid_act")
    gated = K.sem("gated")
    a_high = K.sem("a_high")
    a_ready = K.sem("a_ready")
    out_psum = K.sem("out_psum")
    y_added = K.sem("y_added")
    f_chain = K.sem("f_chain")
    x_done = K.sem("x_done")
    f_squares = K.sem("f_squares")
    UNITS = 2 * NT

    def experts(l):
        with nc.Block() as block:
            @block.sync
            def _(sp):
                def load_u(g, j):
                    sp.wait_ge(u_split, g * NG + j + 1)
                    sp.dma_start(u_raw[:, j % 2, :, :], a["u"][l, g * NG + j]).then_inc(u_in[j % 2], 16)

                def load_v(g, j):
                    sp.wait_ge(v_split, g * NG + j + 1)
                    sp.dma_start(v_raw[:, j % 2, :], a["v"][l, g * NG + j]).then_inc(v_in[j % 2], 16)

                def load_g(g, q):
                    sp.wait_ge(gated, g * NG + 2 * q + 2)
                    sp.dma_start(gt[:, q, :, :, :].rearrange("p b k t -> p b (k t)"),
                                 gates_dram[:, :, bass.ds((g * NG + 2 * q) * GB, 2 * GB)].rearrange("b p n -> p b n")
                                 ).then_inc(g_in[q], 16)

                sp.wait_ge(gm_stored[1], 16 * (NB // 2) + 16)
                load_g(0, 0)
                load_u(0, 2)
                load_g(0, 1)
                load_u(0, 3)
                with sp.Fori(1, GROUPS) as g:
                    for j in range(NG):
                        load_u(g, j)
                        if j % 2 == 0:
                            load_g(g, j // 2)
                        load_v(g - 1, j)
                for j in range(NG):
                    load_v(GROUPS - 1, j)

            @block.tensor
            def _(pe):
                pe.sem_inc(hid_psum, 2)
                pe.sem_inc(out_psum, 2 * UNITS)

                def hidden(g):
                    for j in range(NG):
                        pe.wait_ge(u_split, g * NG + j + 3)
                        if not (isinstance(g, int) and g == 0 and j < 2):
                            pe.wait_ge(a_ready, g * NG + j - 1)
                        for half in range(2):
                            for k in range(KD):
                                for n, (wl, hl) in enumerate(PASSES):
                                    ins = pe.matmul(ps[:, 2 * (j % 2) + half, 0:HALF], (u_hi, u_lo)[wl][:, j % 2, k, :],
                                                    (h_hi, h_lo)[hl][:, k, half * HALF:(half + 1) * HALF],
                                                    start=(k == 0 and n == 0), stop=(k == KD - 1 and n == 2))
                        ins.then_inc(hid_psum, 1)

                def outputs(g, p):
                    pe.wait_ge(v_split, g * NG + NG + 2)
                    pe.wait_ge(a_ready, g * NG + NG)
                    for c in range(UNITS):
                        t, half = c // 2, c % 2
                        pe.wait_ge(y_added, g * UNITS + c + 1)
                        for j in range(NG):
                            for n, (al, vl) in enumerate(PASSES):
                                ins = pe.matmul(ps[:, 4 + (2 * p + c) % 4, :], (a_hi, a_lo)[al][:, p, j, t * P:(t + 1) * P],
                                                (v_hi, v_lo)[vl][:, j, half * 512:(half + 1) * 512],
                                                start=(j == 0 and n == 0), stop=(j == NG - 1 and n == 2))
                        ins.then_inc(out_psum, 1)

                hidden(0)
                with pe.Fori(0, GROUPS // 2 - 1) as i:
                    hidden(i * 2 + 1)
                    outputs(i * 2, 0)
                    hidden(i * 2 + 2)
                    outputs(i * 2 + 1, 1)
                hidden(GROUPS - 1)
                outputs(GROUPS - 2, 0)
                outputs(GROUPS - 1, 1)

            @block.scalar
            def _(act):
                def high_u(g, j):
                    act.wait_ge(u_in[j % 2], g * (NG // 2 * 16) + j // 2 * 16 + 16)
                    act.wait_ge(hid_psum, g * NG + j + 1)
                    act.activation(u_hi[:, j % 2, :, :], u_raw[:, j % 2, :, :], ACT.Copy).then_inc(u_high, 1)

                def high_v(g, j):
                    act.wait_ge(v_in[j % 2], g * (NG // 2 * 16) + j // 2 * 16 + 16)
                    act.wait_ge(out_psum, g * UNITS + 2 * UNITS)
                    act.activation(v_hi[:, j, :], v_raw[:, j % 2, :], ACT.Copy).then_inc(v_high, 1)

                def group(g, p, first=False, last=False):
                    for j in range(NG):
                        b = 2 * (j % 2)
                        if not first:
                            high_v(g - 1, j)
                        act.wait_ge(hid_psum, g * NG + j + 3)
                        act.activation(ps[:, b:b + 2, 0:HALF], ps[:, b:b + 2, 0:HALF], ACT.Gelu_apprx_tanh).then_inc(hid_act, 1)
                        if j + 2 < NG:
                            high_u(g, j + 2)
                        elif not last:
                            high_u(g + 1, j + 2 - NG)
                        act.wait_ge(gated, g * NG + j + 5)
                        act.wait_ge(out_psum, g * UNITS + UNITS)
                        act.activation(a_hi[:, p, j, :].rearrange("p (a b) -> p a b", a=2), ps[:, b:b + 2, 0:HALF],
                                       ACT.Copy).then_inc(a_high, 1)

                high_u(0, 0)
                high_u(0, 1)
                group(0, 0, first=True)
                with act.Fori(0, GROUPS // 2 - 1) as i:
                    group(i * 2 + 1, 1)
                    group(i * 2 + 2, 0)
                group(GROUPS - 1, 1, last=True)
                for j in range(NG):
                    high_v(GROUPS - 1, j)
                for t in range(NT):
                    act.wait_ge(x_done, t + 1)
                    squares(act, f_squares, t, t, y[:, t, :])

            @block.gpsimd
            def _(pool):
                pool.sem_inc(u_split, 2)
                with pool.Fori(0, GROUPS) as g:
                    for j in range(NG):
                        pool.wait_ge(u_high, g * NG + j + 1)
                        pool.tensor_tensor(u_lo[:, j % 2, :, :], u_raw[:, j % 2, :, :], u_hi[:, j % 2, :, :],
                                           ALU.subtract).then_inc(u_split, 1)

            @block.vector
            def _(dve):
                link = chain_of(dve, f_chain)
                link(dve.memset(y[:, :, :], 0.0))
                dve.sem_inc(y_added, 4)
                dve.sem_inc(gated, 4)
                dve.sem_inc(v_split, 2)

                def low_v(g, j):
                    dve.wait_ge(v_high, g * NG + j + 1)
                    dve.tensor_tensor(v_lo[:, j, :], v_raw[:, j % 2, :], v_hi[:, j, :], ALU.subtract).then_inc(v_split, 1)

                def gate(g, p, first=False):
                    for j in range(NG):
                        if not first:
                            low_v(g - 1, j)
                        b, q = 2 * (j % 2), j // 2
                        dve.wait_ge(g_in[q], g * 16 + 16)
                        dve.wait_ge(hid_act, g * NG + j + 1)
                        for half in range(2):
                            at = ps[:, b + half, 0:HALF].rearrange("p (b t) -> p b t", t=GB)
                            ins = dve.tensor_tensor(at, at, gt[:, q, half * (NB // 2):(half + 1) * (NB // 2), j % 2, :], ALU.mult)
                        ins.then_inc(gated, 1)
                        dve.wait_ge(a_high, g * NG + j + 1)
                        dve.tensor_tensor(a_lo[:, p, j, :].rearrange("p (a b) -> p a b", a=2), ps[:, b:b + 2, 0:HALF],
                                          a_hi[:, p, j, :].rearrange("p (a b) -> p a b", a=2), ALU.subtract).then_inc(a_ready, 1)

                def add(g, p, after=None):
                    for c in range(UNITS):
                        t, half = c // 2, c % 2
                        dve.wait_ge(out_psum, g * UNITS + c + 1 + 2 * UNITS)
                        span = slice(half * 512, (half + 1) * 512)
                        dve.tensor_tensor(y[:, t, span], ps[:, 4 + (2 * p + c) % 4, :], y[:, t, span], ALU.add).then_inc(y_added, 1)
                        if after is not None and half == 1:
                            after(t)
                    dve.wait_ge(y_added, g * UNITS + UNITS + 4)

                gate(0, 0, first=True)
                with dve.Fori(0, GROUPS // 2 - 1) as i:
                    gate(i * 2 + 1, 1)
                    add(i * 2, 0)
                    gate(i * 2 + 2, 0)
                    add(i * 2 + 1, 1)
                gate(GROUPS - 1, 1)
                add(GROUPS - 2, 0)
                for j in range(NG):
                    low_v(GROUPS - 1, j)

                def residual(t):
                    dve.wait_ge(y_added, (GROUPS - 1) * UNITS + 2 * t + 2 + 4)
                    link(dve.tensor_tensor(y[:, t, :], y[:, t, :], gate2[:, (0 if t == 0 else 1), :], ALU.mult))
                    dve.tensor_tensor(x[:, t, :], x[:, t, :], y[:, t, :], ALU.add).then_inc(x_done, 1)

                add(GROUPS - 1, 1, residual)

    with nc.Fori(0, DEPTH) as l:
        layer(l)
        clear_counts()

    fg = sb("fg", [P, D])
    f_load = nc.alloc_semaphore("f_load")
    f_sq = nc.alloc_semaphore("f_sq")
    f_norm = nc.alloc_semaphore("f_norm")
    f_out = nc.alloc_semaphore("f_out")
    with nc.Block() as block:
        @block.sync
        def _(sp):
            sp.dma_start(fg[:, :], a["final_g"].partition_broadcast(P)).then_inc(f_load, 16)
            for t in range(NT):
                sp.wait_ge(f_norm, t + 2)
                sp.dma_start(o["y"][t * P:(t + 1) * P, :], x[:, t, :]).then_inc(f_out, 16)
            sp.wait_ge(f_out, 16 * NT)

        @block.scalar
        def _(act):
            act.activation(rstd[:, 0:NT], ss[:, 0:NT], ACT.Sqrt, bias=eps_col[:, 0:1], scale=1.0 / D).then_inc(f_sq, 1)

        @block.vector
        def _(dve):
            dve.wait_ge(f_sq, 1)
            dve.wait_ge(f_load, 16)
            dve.reciprocal(rstd[:, 0:NT], rstd[:, 0:NT]).then_inc(f_norm, 1)
            dve.wait_ge(f_norm, 1)
            for t in range(NT):
                dve.scalar_tensor_tensor(x[:, t, :], x[:, t, :], rstd[:, t:t + 1], fg[:, :], ALU.mult,
                                         ALU.mult).then_inc(f_norm, 1)


ROPE_SWAP = np.r_[8:16, 0:8, 24:32, 16:24]


def constants():
    f = np.float32
    eye = np.eye(P, dtype=f)
    s, t = np.arange(P)[:, None], np.arange(P)[None, :]
    maskb = np.stack([np.where(s <= t, 0.0, MASKED), np.where(s >= t, 0.0, MASKED)], axis=1).astype(f)
    sel8 = np.zeros((ROWS, 8, P), f)
    for d in range(2):
        for h in range(H):
            sel8[32 * d + h, d * H + h] = 1.0
    grid_w, axis = 64, ROPE // 2
    freqs = (f(10000.0) ** (-np.arange(0, axis, 2, dtype=f) / f(axis))).astype(f)
    position = np.arange(NS * P)
    row, column = (position // grid_w).astype(f), (position % grid_w).astype(f)
    ang = np.concatenate([row[None] * freqs[:, None]] * 2 + [column[None] * freqs[:, None]] * 2).astype(f)
    sign = np.where(np.arange(ROPE) % axis < axis // 2, -1.0, 1.0).astype(f)[:, None]
    cos_sin = np.stack([np.cos(ang), np.sin(ang) * sign], axis=1).astype(f)
    bf16 = mybir.dt.np(BF16)
    return {
        "ident": eye, "ident_b": eye.astype(bf16), "maskb": maskb.astype(bf16), "sel8": sel8, "cos_sin": cos_sin,
        "iota": np.tile(np.arange(NKEYS, dtype=f), (P, 1)),
        "iota16": np.tile(np.arange(TOP, dtype=f), (P, 1)).astype(bf16),
    }


def blocks(w, width):
    n, d, c = w.shape
    return np.ascontiguousarray(w.reshape(n, d // P, P, c // width, width).transpose(0, 3, 2, 1, 4))


def lay_out(x_prompt, x_sample, c, cache_mla_ckv, cache_mla_krope, state_mlstm_C, state_mlstm_n, state_mlstm_m,
            c_ctx, norm1_g, ada_w, ada_b, w_in, mlstm_gate_b, cm_norm_g, cm_ws, cm_b, mla_q_norm_g, mla_w_uq,
            mla_kv_norm_g, mla_w_ukv, w_out, norm2_g, peer_w_q, peer_subkeys, peer_u, peer_v, final_g):
    f = np.float32
    L = DEPTH
    mq, mk, mv, mo = (w_in[..., i * 256:(i + 1) * 256] for i in range(4))
    g = w_in[..., 1024:1040]
    cu, cv, cq, ckv = (w_in[..., 1040 + i * 256:1040 + (i + 1) * 256] for i in range(4))
    kr = w_in[..., 2064:2096]
    w_small = np.zeros((L, D, 256), f)
    for at, gates, keys in ((0, (0, 8), kr), (QK, (4, 12), kr[..., ROPE_SWAP])):
        for d in range(2):
            w_small[..., at + 32 * d:at + 32 * d + H] = g[..., gates[d]:gates[d] + H]
        w_small[..., at + HD:at + QK] = keys
    gate_b = np.zeros((L, ROWS, 2), f)
    gate_b[:, 0:4, 0], gate_b[:, 32:36, 0] = mlstm_gate_b[:, 0:4], mlstm_gate_b[:, 8:12]
    gate_b[:, 0:4, 1], gate_b[:, 32:36, 1] = mlstm_gate_b[:, 4:8], mlstm_gate_b[:, 12:16]
    m0 = np.zeros((L, ROWS, 1), f)
    m0[:, 0:4, 0], m0[:, 32:36, 0] = state_mlstm_m[0, :, 0], state_mlstm_m[0, :, 1]
    cn0 = np.concatenate([state_mlstm_C[0], state_mlstm_n[0][..., None]], axis=-1)
    cn0 = cn0.reshape(L, 2, 2, 2, HD, HD + 1).transpose(0, 3, 4, 1, 2, 5).reshape(L, P, 2, 2, HD + 1)
    uq = mla_w_uq.reshape(L, 256, AH, QK)
    ukv = mla_w_ukv.reshape(L, 256, AH, 2 * HD)

    def halves(w):
        return np.ascontiguousarray(w.reshape(L, 2, P, -1).transpose(0, 2, 1, 3))

    return {
        "x": np.concatenate([x_prompt[0], x_sample[0]]),
        "cT": np.stack([c_ctx, c[0]]).reshape(2, KD, P).transpose(2, 1, 0),
        "normT": np.stack([norm1_g, norm2_g], axis=1).reshape(L, 2, KD, P).transpose(0, 3, 1, 2),
        "ada_w": np.roll(blocks(ada_w, 512), -1, axis=0),
        "ada_bT": np.roll(ada_b.reshape(L, 6, KD, P)[:, [0, 1, 3, 4]].transpose(0, 3, 1, 2), -1, axis=0),
        "ada_g": ada_b.reshape(L, 6, 2, 512)[:, [2, 5]],
        "w_in": blocks(np.concatenate([mk, mv, mo, cu, cv, cq, ckv, mq, w_small], axis=-1), 256),
        "gate_b": gate_b, "m0": m0, "cn0": cn0,
        "wsT": cm_ws.transpose(0, 3, 1, 2), "cmb": cm_b.transpose(0, 2, 1),
        "normg": np.stack([cm_norm_g, mla_q_norm_g, mla_kv_norm_g], axis=1),
        "cacheT": cache_mla_ckv[0].transpose(0, 2, 1).reshape(L, 2, P, P).transpose(0, 2, 1, 3),
        "kr_cacheT": cache_mla_krope[0].transpose(0, 2, 1),
        "wuq": halves(np.concatenate([uq, uq[..., HD:][..., ROPE_SWAP]], axis=-1)),
        "wuk": halves(ukv[..., :HD]), "wuv": halves(ukv[..., HD:]),
        "w_out": blocks(w_out, 256), "wq": blocks(peer_w_q, 512),
        "skT": peer_subkeys.transpose(0, 3, 1, 2),
        "u": peer_u.reshape(L, NKEYS, NKEYS, KD, P).transpose(0, 1, 4, 3, 2),
        "v": peer_v.reshape(L, NKEYS, NKEYS, D),
        "final_g": final_g,
        **constants(),
    }


OUTPUTS = {"y": (T, D), "ckv": (DEPTH, P, 256), "kr": (DEPTH, ROPE, P), "cn": (DEPTH, P, 2, 2, HD + 1),
           "m": (DEPTH, ROWS, 1)}


def kernel(**inputs):
    import concourse.bacc as bacc
    from concourse.bass_utils import run_bass_kernel_spmd

    nc = bacc.Bacc("TRN2", target_bir_lowering=False, num_devices=1)
    arrays = {f"in_{k}": np.ascontiguousarray(v) for k, v in lay_out(**{k: np.asarray(v) for k, v in inputs.items()}).items()}
    a = {k[3:]: nc.dram_tensor(k, v.shape, mybir.dt.from_np(v.dtype), kind="ExternalInput").ap() for k, v in arrays.items()}
    o = {k: nc.dram_tensor(f"out_{k}", v, F32, kind="ExternalOutput").ap() for k, v in OUTPUTS.items()}
    build_program(nc, a, o)
    r = run_bass_kernel_spmd(nc, [arrays], core_ids=[0]).results[0]
    cn = r["out_cn"].reshape(DEPTH, 2, HD, 2, 2, HD + 1).transpose(0, 3, 4, 1, 2, 5).reshape(DEPTH, 2, H, HD, HD + 1)
    m = r["out_m"][:, :, 0]
    m = np.stack([m[:, 0:4], m[:, 32:36]], axis=1)
    y = r["out_y"]
    return (y[None, :P], y[None, P:], r["out_ckv"][None], np.ascontiguousarray(r["out_kr"].transpose(0, 2, 1))[None],
            np.ascontiguousarray(cn[..., :HD])[None], np.ascontiguousarray(cn[..., HD])[None], m[None])
```
